# Optimizing a Trainium2 kernel written in Bass

```python
import jax, jax.numpy as jnp
from jax import lax
import numpy as np
import math

D_MODEL = 1024
BATCH = 1
SEQ = 256
DEPTH = 1

CHUNK = 64
D_CONV = D_MODEL
CONV_WIDTH = 31
D_SGU = D_MODEL
SGU_BLOCK = 128
SGU_GROUPS = 8
SGU_GROUP_DIM = D_SGU // SGU_GROUPS
D_IN = 2 * D_CONV + 2 * D_SGU + 2 * D_MODEL
SPLITS = (D_CONV, 2 * D_CONV, 2 * D_CONV + 2 * D_SGU, 2 * D_CONV + 2 * D_SGU + D_MODEL)
N_EXPERTS = 32
TOP_K = 4
D_EXPERT = D_MODEL
SWIGLU_LIMIT = 7.0
SWIGLU_ALPHA = 1.702
MOE_BLOCK = 128
LN_EPS = 1e-5
DEEPNORM_ALPHA = float((2 * DEPTH) ** 0.25)
DEEPNORM_BETA = float((8 * DEPTH) ** -0.25)


def _layer_norm(x, gain=None, bias=None):
    xf = x.astype(jnp.float32)
    mu = jnp.mean(xf, axis=-1, keepdims=True)
    var = jnp.mean(jnp.square(xf - mu), axis=-1, keepdims=True)
    y = (xf - mu) * lax.rsqrt(var + LN_EPS)
    if gain is not None:
        y = y * gain.astype(jnp.float32) + bias.astype(jnp.float32)
    return y.astype(x.dtype)

def _causal_depthwise_conv(x, w, b):
    y = lax.conv_general_dilated(
        x, w[:, None, :], window_strides=(1,), padding=[(CONV_WIDTH - 1, 0)],
        dimension_numbers=('NWC', 'WIO', 'NWC'), feature_group_count=x.shape[-1])
    return y + b

def _spatial_gating(u, v, ln_g, ln_b, w_s, b_s):
    B, S, _ = v.shape
    n_blk = S // SGU_BLOCK
    v = _layer_norm(v, ln_g, ln_b).reshape(B, n_blk, SGU_BLOCK, SGU_GROUPS, SGU_GROUP_DIM)
    chunk_id = jnp.arange(SGU_BLOCK) // CHUNK
    mask = chunk_id[:, None] >= chunk_id[None, :]
    w = jnp.where(mask[None], w_s, 0)
    mixed = jnp.einsum('gij,bnjgc->bnigc', w, v) + jnp.transpose(b_s)[None, None, :, :, None]
    return u * mixed.reshape(B, S, D_SGU)

def _token_mixer(h, w_in, b_in, conv_w, conv_b, ln_a_g, ln_a_b, w_a, b_a,
                 ln_v_g, ln_v_b, w_s, b_s, w_b, b_b, w_out, b_out):
    z = h @ w_in + b_in
    a_val, a_gate, sgu, g_a, g_b = jnp.split(z, SPLITS, axis=-1)
    ya = a_val * jax.nn.sigmoid(a_gate)
    ya = _causal_depthwise_conv(ya, conv_w, conv_b)
    ya = jax.nn.silu(_layer_norm(ya, ln_a_g, ln_a_b))
    ya = ya @ w_a + b_a
    u, v = jnp.split(jax.nn.gelu(sgu, approximate=False), 2, axis=-1)
    yb = _spatial_gating(u, v, ln_v_g, ln_v_b, w_s, b_s) @ w_b + b_b
    m = jax.nn.sigmoid(g_a) * ya + jax.nn.sigmoid(g_b) * yb
    return m @ w_out + b_out

def _moe(h, w_router, b_router, w_gu, b_gu, w_dn, b_dn):
    B, S, D = h.shape
    T = B * S
    xt = h.reshape(T, D)
    logits = (xt @ w_router + b_router).astype(jnp.float32)
    top_logits, top_idx = lax.top_k(logits, TOP_K)
    top_w = jax.nn.softmax(top_logits, axis=-1)
    flat_e = top_idx.reshape(-1)
    order = jnp.argsort(flat_e)
    sorted_e = flat_e[order]
    counts = jnp.bincount(flat_e, length=N_EXPERTS)
    padded = (counts + MOE_BLOCK - 1) // MOE_BLOCK * MOE_BLOCK
    start = jnp.cumsum(counts) - counts
    pad_end = jnp.cumsum(padded)
    pad_start = pad_end - padded
    dest = pad_start[sorted_e] + jnp.arange(T * TOP_K) - start[sorted_e]
    n_slots = T * TOP_K + N_EXPERTS * MOE_BLOCK
    n_blocks = n_slots // MOE_BLOCK
    slot_tok = jnp.full((n_slots,), T, jnp.int32).at[dest].set((order // TOP_K).astype(jnp.int32))
    slot_w = jnp.zeros((n_slots,), jnp.float32).at[dest].set(top_w.reshape(-1)[order])
    block_e = jnp.minimum(
        jnp.searchsorted(pad_end, jnp.arange(n_blocks) * MOE_BLOCK, side='right'), N_EXPERTS - 1)
    xt_pad = jnp.concatenate([xt, jnp.zeros((1, D), xt.dtype)], axis=0)

    def expert_block(args):
        tok, e = args
        xb = xt_pad[tok]
        gate, up = jnp.split(xb @ w_gu[e] + b_gu[e], 2, axis=-1)
        gate = jnp.minimum(gate, SWIGLU_LIMIT)
        up = jnp.clip(up, -SWIGLU_LIMIT, SWIGLU_LIMIT)
        act = (up + 1) * (gate * jax.nn.sigmoid(SWIGLU_ALPHA * gate))
        return act @ w_dn[e] + b_dn[e]

    yb = lax.map(expert_block, (slot_tok.reshape(n_blocks, MOE_BLOCK), block_e))
    y = jnp.zeros((T + 1, D), jnp.float32).at[slot_tok].add(
        yb.reshape(n_slots, D).astype(jnp.float32) * slot_w[:, None])
    return y[:T].reshape(B, S, D).astype(h.dtype)

def _normal(k, shape, scale):
    return jax.random.normal(k, shape, jnp.float32) * scale

def first_inputs(seed: int = 0) -> dict:
    key = jax.random.key(seed)
    ks = jax.random.split(key, 32)
    L, D = DEPTH, D_MODEL
    return {
        "x": _normal(ks[0], (BATCH, SEQ, D), 1.0),
        "c": _normal(ks[1], (BATCH, D), 1.0),
        "w_mod": _normal(ks[2], (L, D, 6 * D), 0.5 * D ** -0.5),
        "b_mod": _normal(ks[3], (L, 6 * D), 0.02),
        "w_in": _normal(ks[4], (L, D, D_IN), D ** -0.5),
        "b_in": _normal(ks[5], (L, D_IN), 0.02),
        "conv_w": _normal(ks[6], (L, CONV_WIDTH, D_CONV), CONV_WIDTH ** -0.5),
        "conv_b": _normal(ks[7], (L, D_CONV), 0.02),
        "ln_a_g": 1.0 + _normal(ks[8], (L, D_CONV), 0.05),
        "ln_a_b": _normal(ks[9], (L, D_CONV), 0.02),
        "w_a": _normal(ks[10], (L, D_CONV, D), D_CONV ** -0.5),
        "b_a": _normal(ks[11], (L, D), 0.02),
        "ln_v_g": 1.0 + _normal(ks[12], (L, D_SGU), 0.05),
        "ln_v_b": _normal(ks[13], (L, D_SGU), 0.02),
        "w_s": _normal(ks[14], (L, SGU_GROUPS, SGU_BLOCK, SGU_BLOCK), SGU_BLOCK ** -0.5),
        "b_s": 1.0 + _normal(ks[15], (L, SGU_GROUPS, SGU_BLOCK), 0.1),
        "w_b": _normal(ks[16], (L, D_SGU, D), D_SGU ** -0.5),
        "b_b": _normal(ks[17], (L, D), 0.02),
        "w_out": _normal(ks[18], (L, D, D), DEEPNORM_BETA * D ** -0.5),
        "b_out": _normal(ks[19], (L, D), 0.02),
        "post1_g": 1.0 + _normal(ks[20], (L, D), 0.05),
        "post1_b": _normal(ks[21], (L, D), 0.02),
        "w_router": _normal(ks[22], (L, D, N_EXPERTS), D ** -0.5),
        "b_router": _normal(ks[23], (L, N_EXPERTS), 0.01),
        "w_gu": _normal(ks[24], (L, N_EXPERTS, D, 2 * D_EXPERT), D ** -0.5),
        "b_gu": _normal(ks[25], (L, N_EXPERTS, 2 * D_EXPERT), 0.02),
        "w_dn": _normal(ks[26], (L, N_EXPERTS, D_EXPERT, D), DEEPNORM_BETA * D_EXPERT ** -0.5),
        "b_dn": _normal(ks[27], (L, N_EXPERTS, D), 0.02),
        "post2_g": 1.0 + _normal(ks[28], (L, D), 0.05),
        "post2_b": _normal(ks[29], (L, D), 0.02),
    }

def first_block(x, c, w_mod, b_mod, w_in, b_in, conv_w, conv_b, ln_a_g, ln_a_b, w_a, b_a,
              ln_v_g, ln_v_b, w_s, b_s, w_b, b_b, w_out, b_out, post1_g, post1_b,
              w_router, b_router, w_gu, b_gu, w_dn, b_dn, post2_g, post2_b):
    cond = jax.nn.silu(c)
    for l in range(DEPTH):
        mod = cond @ w_mod[l] + b_mod[l]
        sh1, sc1, g1, sh2, sc2, g2 = [m[:, None, :] for m in jnp.split(mod, 6, axis=-1)]
        h = _layer_norm(x) * (1 + sc1) + sh1
        y = _token_mixer(h, w_in[l], b_in[l], conv_w[l], conv_b[l], ln_a_g[l], ln_a_b[l],
                         w_a[l], b_a[l], ln_v_g[l], ln_v_b[l], w_s[l], b_s[l], w_b[l], b_b[l],
                         w_out[l], b_out[l])
        x = _layer_norm(DEEPNORM_ALPHA * x + g1 * y, post1_g[l], post1_b[l])
        h = _layer_norm(x) * (1 + sc2) + sh2
        y = _moe(h, w_router[l], b_router[l], w_gu[l], b_gu[l], w_dn[l], b_dn[l])
        x = _layer_norm(DEEPNORM_ALPHA * x + g2 * y, post2_g[l], post2_b[l])
    return x


DEPTH_2 = 2

N_MIXERS = 2
N_POOL_LAYERS = (DEPTH_2 + 1) // 2
N_GDN_LAYERS = DEPTH_2 // 2
PLE_DIM = 256
D_FF = 4 * D_MODEL
POOL_WINDOWS = (2, 4, 8, 16)
N_POOL_GROUPS = len(POOL_WINDOWS)
POOL_GROUP = D_MODEL // N_POOL_GROUPS
GDN_HEADS = 8
GDN_HEAD_DIM = 128
GDN_KEY_DIM = GDN_HEADS * GDN_HEAD_DIM
GDN_VAL_DIM = GDN_HEADS * GDN_HEAD_DIM
GDN_CONV_DIM = 2 * GDN_KEY_DIM + GDN_VAL_DIM
GDN_IN_DIM = GDN_CONV_DIM + GDN_VAL_DIM + 2 * GDN_HEADS
CONV_WIDTH_2 = 4
DEEPNORM_ALPHA_2 = (2.0 * DEPTH_2) ** 0.25
DEEPNORM_BETA_2 = (8.0 * DEPTH_2) ** -0.25
RMS_EPS = 1e-6
L2_EPS = 1e-6


def layer_norm(x, g, b):
    xf = x.astype(jnp.float32)
    mu = jnp.mean(xf, axis=-1, keepdims=True)
    var = jnp.mean(jnp.square(xf - mu), axis=-1, keepdims=True)
    return ((xf - mu) * lax.rsqrt(var + LN_EPS) * g + b).astype(x.dtype)

def pool_mixer(x, w_grp, b_grp, scale):
    B, S, _ = x.shape
    xg = x.astype(jnp.float32).reshape(B, S, N_POOL_GROUPS, POOL_GROUP)
    cs = jnp.cumsum(xg, axis=1)
    pos = jnp.arange(1, S + 1, dtype=jnp.float32)[None, :, None]
    outs = []
    for gi, w in enumerate(POOL_WINDOWS):
        c = cs[:, :, gi]
        c_prev = jnp.pad(c, ((0, 0), (w, 0), (0, 0)))[:, :S]
        mean = (c - c_prev) / jnp.minimum(pos, float(w))
        outs.append(mean - xg[:, :, gi])
    pooled = jnp.stack(outs, axis=2).astype(x.dtype)
    y = jnp.einsum('bsgc,gcd->bsgd', pooled, w_grp) + b_grp
    return y.reshape(B, S, D_MODEL) * scale

def causal_depthwise_conv(x, w):
    C = x.shape[-1]
    return lax.conv_general_dilated(
        x, w[:, None, :].astype(x.dtype), window_strides=(1,),
        padding=[(CONV_WIDTH_2 - 1, 0)], dimension_numbers=('NWC', 'WIO', 'NWC'),
        feature_group_count=C)

def l2_normalize(t):
    return t * lax.rsqrt(jnp.sum(jnp.square(t), axis=-1, keepdims=True) + L2_EPS)

def chunk_gated_delta_rule(q, k, v, g, beta):
    B, S, H, Dk = q.shape
    Dv = v.shape[-1]
    N = S // CHUNK

    def to_chunks(t):
        return t.reshape(B, N, CHUNK, H, -1).transpose(0, 3, 1, 2, 4)

    q, k, v = to_chunks(q), to_chunks(k), to_chunks(v)
    g = g.reshape(B, N, CHUNK, H).transpose(0, 3, 1, 2)
    beta = beta.reshape(B, N, CHUNK, H).transpose(0, 3, 1, 2)
    g = jnp.cumsum(g, axis=-1)

    idx = jnp.arange(CHUNK)
    causal = idx[:, None] >= idx[None, :]
    strict = idx[:, None] > idx[None, :]
    decay = jnp.exp(jnp.where(causal, g[..., :, None] - g[..., None, :], -jnp.inf))

    k_beta = k * beta[..., None]
    a = jnp.einsum('bhncd,bhnmd->bhncm', k_beta, k) * decay
    m = jnp.where(strict, a, 0.0) + jnp.eye(CHUNK, dtype=jnp.float32)
    rhs = jnp.concatenate([v * beta[..., None], k_beta * jnp.exp(g)[..., None]], axis=-1)
    sol = lax.linalg.triangular_solve(m, rhs, left_side=True, lower=True, unit_diagonal=True)
    u, w = sol[..., :Dv], sol[..., Dv:]

    qk = jnp.einsum('bhncd,bhnmd->bhncm', q, k) * decay
    q_dec = q * jnp.exp(g)[..., None]
    k_dec = k * jnp.exp(g[..., -1:] - g)[..., None]
    g_last = jnp.exp(g[..., -1])

    def step(state, xs):
        u_c, w_c, qk_c, qd_c, kd_c, gl_c = xs
        v_new = u_c - jnp.einsum('bhcd,bhde->bhce', w_c, state)
        o_c = (jnp.einsum('bhcd,bhde->bhce', qd_c, state)
               + jnp.einsum('bhcm,bhme->bhce', qk_c, v_new))
        state = state * gl_c[..., None, None] + jnp.einsum('bhcd,bhce->bhde', kd_c, v_new)
        return state, o_c

    xs = tuple(jnp.moveaxis(t, 2, 0) for t in (u, w, qk, q_dec, k_dec, g_last))
    s0 = jnp.zeros((B, H, Dk, Dv), jnp.float32)
    _, o = lax.scan(step, s0, xs)
    return o.transpose(1, 0, 3, 2, 4).reshape(B, S, H, Dv)

def gated_deltanet(x, w_in, conv_w, a_log, dt_bias, norm_w, w_out):
    B, S, _ = x.shape
    H, Dh = GDN_HEADS, GDN_HEAD_DIM
    proj = x @ w_in
    qkv, z, b_logit, a_logit = jnp.split(
        proj, [GDN_CONV_DIM, GDN_CONV_DIM + GDN_VAL_DIM, GDN_CONV_DIM + GDN_VAL_DIM + H], axis=-1)
    qkv = jax.nn.silu(causal_depthwise_conv(qkv, conv_w))
    q, k, v = jnp.split(qkv, [GDN_KEY_DIM, 2 * GDN_KEY_DIM], axis=-1)
    q = l2_normalize(q.reshape(B, S, H, Dh).astype(jnp.float32)) * (Dh ** -0.5)
    k = l2_normalize(k.reshape(B, S, H, Dh).astype(jnp.float32))
    v = v.reshape(B, S, H, Dh).astype(jnp.float32)
    beta = jax.nn.sigmoid(b_logit.astype(jnp.float32))
    g = -jnp.exp(a_log.astype(jnp.float32)) * jax.nn.softplus(
        a_logit.astype(jnp.float32) + dt_bias.astype(jnp.float32))
    o = chunk_gated_delta_rule(q, k, v, g, beta)
    zf = z.reshape(B, S, H, Dh).astype(jnp.float32)
    o = o * lax.rsqrt(jnp.mean(jnp.square(o), axis=-1, keepdims=True) + RMS_EPS) * norm_w * jax.nn.silu(zf)
    return o.reshape(B, S, GDN_VAL_DIM).astype(x.dtype) @ w_out

def squared_relu_mlp(x, w1, w2):
    return jnp.square(jax.nn.relu(x @ w1)) @ w2

def second_inputs(seed: int = 0) -> dict:
    key = jax.random.key(seed)
    ks = jax.random.split(key, 20)
    f32 = jnp.float32
    nrm = lambda k, s: jax.random.normal(k, s, f32)
    dt = jnp.exp(jax.random.uniform(ks[9], (N_GDN_LAYERS, GDN_HEADS), f32,
                                    math.log(1e-3), math.log(1e-1)))
    return {
        "x": nrm(ks[0], (BATCH, SEQ, D_MODEL)),
        "p": nrm(ks[1], (DEPTH_2, BATCH, SEQ, PLE_DIM)),
        "ln_gain": 1.0 + 0.02 * nrm(ks[2], (DEPTH_2, 2, D_MODEL)),
        "ln_bias": 0.02 * nrm(ks[3], (DEPTH_2, 2, D_MODEL)),
        "pool_w": nrm(ks[4], (N_POOL_LAYERS, N_POOL_GROUPS, POOL_GROUP, POOL_GROUP)) * (POOL_GROUP ** -0.5) * DEEPNORM_BETA_2,
        "pool_b": 0.02 * nrm(ks[5], (N_POOL_LAYERS, N_POOL_GROUPS, POOL_GROUP)),
        "pool_scale": 1.0 + 0.1 * nrm(ks[6], (N_POOL_LAYERS, D_MODEL)),
        "gdn_w_in": nrm(ks[7], (N_GDN_LAYERS, D_MODEL, GDN_IN_DIM)) * (D_MODEL ** -0.5),
        "gdn_conv": nrm(ks[8], (N_GDN_LAYERS, CONV_WIDTH_2, GDN_CONV_DIM)) * (CONV_WIDTH_2 ** -0.5),
        "gdn_a_log": jnp.log(jax.random.uniform(ks[10], (N_GDN_LAYERS, GDN_HEADS), f32, 1.0, 16.0)),
        "gdn_dt_bias": dt + jnp.log(-jnp.expm1(-dt)),
        "gdn_norm_w": 1.0 + 0.02 * nrm(ks[11], (N_GDN_LAYERS, GDN_HEAD_DIM)),
        "gdn_w_out": nrm(ks[12], (N_GDN_LAYERS, GDN_VAL_DIM, D_MODEL)) * (GDN_VAL_DIM ** -0.5) * DEEPNORM_BETA_2,
        "mlp_w1": nrm(ks[13], (DEPTH_2, D_MODEL, D_FF)) * (D_MODEL ** -0.5),
        "mlp_w2": nrm(ks[14], (DEPTH_2, D_FF, D_MODEL)) * (D_FF ** -0.5) * DEEPNORM_BETA_2,
        "ple_gate_w": nrm(ks[15], (DEPTH_2, D_MODEL, D_MODEL)) * (D_MODEL ** -0.5),
        "ple_gate_b": 0.02 * nrm(ks[16], (DEPTH_2, D_MODEL)),
        "ple_proj": nrm(ks[17], (DEPTH_2, PLE_DIM, D_MODEL)) * (PLE_DIM ** -0.5),
    }

def second_block(x, p, ln_gain, ln_bias, pool_w, pool_b, pool_scale, gdn_w_in, gdn_conv,
              gdn_a_log, gdn_dt_bias, gdn_norm_w, gdn_w_out, mlp_w1, mlp_w2,
              ple_gate_w, ple_gate_b, ple_proj):
    for i in range(DEPTH_2):
        j = i // N_MIXERS
        if i % N_MIXERS == 0:
            mix = pool_mixer(x, pool_w[j], pool_b[j], pool_scale[j])
        else:
            mix = gated_deltanet(x, gdn_w_in[j], gdn_conv[j], gdn_a_log[j], gdn_dt_bias[j],
                                 gdn_norm_w[j], gdn_w_out[j])
        x = layer_norm(DEEPNORM_ALPHA_2 * x + mix, ln_gain[i, 0], ln_bias[i, 0])
        ff = squared_relu_mlp(x, mlp_w1[i], mlp_w2[i])
        pe = jax.nn.sigmoid(x @ ple_gate_w[i] + ple_gate_b[i]) * (p[i] @ ple_proj[i])
        x = layer_norm(DEEPNORM_ALPHA_2 * x + ff + pe, ln_gain[i, 1], ln_bias[i, 1])
    return x


def setup_inputs(seed=0):
    out = dict(first_inputs(seed))
    for name, value in second_inputs(seed + 1).items():
        if name != "x":
            out[name + "_2"] = value
    return out


def reference(
    x, c, w_mod, b_mod, w_in, b_in, conv_w, conv_b, ln_a_g, ln_a_b, w_a, b_a, ln_v_g, ln_v_b,
    w_s, b_s, w_b, b_b, w_out, b_out, post1_g, post1_b, w_router, b_router, w_gu, b_gu, w_dn,
    b_dn, post2_g, post2_b, p_2, ln_gain_2, ln_bias_2, pool_w_2, pool_b_2, pool_scale_2,
    gdn_w_in_2, gdn_conv_2, gdn_a_log_2, gdn_dt_bias_2, gdn_norm_w_2, gdn_w_out_2, mlp_w1_2,
    mlp_w2_2, ple_gate_w_2, ple_gate_b_2, ple_proj_2,
):
    x = first_block(
        x, c, w_mod, b_mod, w_in, b_in, conv_w, conv_b, ln_a_g, ln_a_b, w_a, b_a, ln_v_g,
        ln_v_b, w_s, b_s, w_b, b_b, w_out, b_out, post1_g, post1_b, w_router, b_router, w_gu,
        b_gu, w_dn, b_dn, post2_g, post2_b,
    )
    return second_block(
        x, p_2, ln_gain_2, ln_bias_2, pool_w_2, pool_b_2, pool_scale_2, gdn_w_in_2, gdn_conv_2,
        gdn_a_log_2, gdn_dt_bias_2, gdn_norm_w_2, gdn_w_out_2, mlp_w1_2, mlp_w2_2, ple_gate_w_2,
        ple_gate_b_2, ple_proj_2,
    )


_drawn_inputs = setup_inputs


def setup_inputs(seed=0):
    import zlib

    import numpy as np

    out = dict(_drawn_inputs(seed))
    spreads = {}
    factors = {'b_mod': 4.473,
     'b_in': 8.0,
     'conv_b': 8.0,
     'ln_a_g': 8.0,
     'ln_a_b': 33.121,
     'b_a': 23.851,
     'ln_v_g': 8.0,
     'ln_v_b': 38.342,
     'b_s': 7.676,
     'b_b': 25.721,
     'b_out': 8.0,
     'b_router': 22.125,
     'b_gu': 8.0,
     'b_dn': 8.0,
     'post2_b': 3.048,
     'pool_b_2': 4.198,
     'gdn_norm_w_2': 25.824,
     'ple_gate_b_2': 8.0}
    for name, (base, spread) in spreads.items():
        noise = np.random.default_rng([zlib.crc32(name.encode()), seed]).standard_normal(out[name].shape)
        drawn = base * np.exp(spread * noise) if base else spread * noise
        out[name] = __import__('jax').numpy.asarray(drawn.astype(out[name].dtype))
    for name, factor in factors.items():
        out[name] = (out[name] * factor).astype(out[name].dtype)
    return out
```

```python
from contextlib import ExitStack

import concourse.bass as bass
from concourse import mybir

F32 = mybir.dt.float32
BF16 = mybir.dt.bfloat16
I32 = mybir.dt.int32
ALU = mybir.AluOpType
ACT = mybir.ActivationFunctionType
AX = mybir.AxisListType

P = 128
BANKS = 8
BANK = 512
UK = 4
RING = 10
KCH = 64
BLK = 64

PE_STEPS = ("gathered", "gate", "up", "spread_T", "act_T0", "act_T1", "down", "scattered")
DVE_STEPS = ("expert_row", "slots0", "slots1", "spread0", "spread1", "tokens", "gate_min", "gated",
             "up_clip", "act0", "act1", "act_T0", "act_T1")
ACT_STEPS = ("sigmoid", "spread_T", "down")


def build(nc, A, out):
    S, D = A["x"].shape[1], A["x"].shape[2]
    NT = S // P
    ND = D // P
    NH = D // BANK
    TAPS = A["conv_w"].shape[1]
    PADC = TAPS - 1
    NE = A["w_router"].shape[2]
    NG = A["w_s"].shape[1]
    TOPK = 4
    EPS = 1e-5
    ALPHA1 = 2.0 ** 0.25
    ALPHA2 = 4.0 ** 0.25
    LIMIT, SWIGLU = 7.0, 1.702
    WINDOWS = (2, 4, 8, 16)
    HEADS = A["gdn_a_log_2"].shape[1]
    DFF = A["mlp_w1_2"].shape[2]
    GTAPS = A["gdn_conv_2"].shape[1]
    NBLK = S // BLK
    assert NT == 2 and D == 1024 and HEADS == ND and NG == ND and NE == 32

    ctx = ExitStack()
    with ctx:
        def sb(name, shape, dt=F32):
            return ctx.enter_context(nc.sbuf_tensor(name, shape, dt))

        def sem(name):
            return ctx.enter_context(nc.semaphore(name))

        ring = sb("ring", [P, RING, UK, BANK])
        area = sb("area", [P, 11 * 2048])
        apad = sb("apad", [P, ND, PADC + S])
        gain_bc = sb("gain_bc", [P, D])
        bias_bc = sb("bias_bc", [P, D])
        cols = sb("cols", [P, BANK])
        ident = sb("ident", [P, P])
        ones = sb("ones", [P, P])
        minus_half = sb("minus_half", [P, 8])
        before = sb("before", [P, P])
        upto = sb("upto", [P, P])
        chunk_ones = sb("chunk_ones", [P, P])
        decay_mask = sb("decay_mask", [P, P])
        level = sb("level", [P, 6, P])
        slot_row = sb("slot_row", [P, NBLK, 2, BLK])
        slot_int = sb("slot_int", [P, NBLK * 2 * BLK], I32)
        inv_pos = sb("inv_pos", [P, 16])
        expert_hot = sb("expert_hot", [96, NE], BF16)
        expert_sel = sb("expert_sel", [96, BLK], BF16)
        zeros = sb("zeros", [P, P], BF16)
        cond = sb("cond", [P, ND])
        modc = sb("modc", [P, 48])
        sc1p = sb("sc1p", [P, ND])
        sc2p = sb("sc2p", [P, ND])
        stats = sb("stats", [P, NT, NH, 6])
        mv = sb("mv", [P, NT, 2])
        rstd = sb("rstd", [P, NT])
        w_router = sb("w_router_sb", [P, ND, NE])
        router_bc = sb("router_bc", [P, NE])
        rt = sb("rt", [P, 10, NT, NE])
        top8 = sb("top8", [P, NT, 8])
        rsum = sb("rsum", [P, NT])
        counts = sb("counts", [1, NE], I32)
        gateT = sb("gateT", [NE, S])
        sm = sb("sm", [P, 16, NT, HEADS])
        alog_bc = sb("alog_bc", [P, HEADS])
        dt_bc = sb("dt_bc", [P, HEADS])
        normw_bc = sb("normw_bc", [P, P])
        w_ba = sb("w_ba", [P, ND, 2 * HEADS])
        banks = [ctx.enter_context(nc.psum_tensor(f"bank{i}", [P, BANK], F32)) for i in range(BANKS)]

        def a(i, w=1):
            return area[:, i * 2048:(i + w) * 2048]

        def feat(i):
            return a(i).rearrange("p (m t) -> p m t", t=S)

        def tok(i):
            return a(i).rearrange("p (t d) -> p t d", d=D)

        def half(i, j):
            return area[:, i * 2048 + j * 1024:i * 2048 + (j + 1) * 1024].rearrange("p (h d) -> p h d", d=P)

        x_tok = tok(0)

        def unit(w, kq, c):
            return w[UK * P * kq:UK * P * (kq + 1), BANK * c:BANK * (c + 1)].rearrange("(k p) n -> p k n", p=P)

        def slabs(w, cs):
            return [unit(w, kq, c) for c in cs for kq in range(w.shape[0] // (UK * P))]

        w_mod, w_in = A["w_mod"][0], A["w_in"][0]
        gdn_in, gdn_out = A["gdn_w_in_2"][0], A["gdn_w_out_2"][0]
        C = D // BANK
        stream = []

        def add(name, units):
            stream.extend((name, u) for u in units)

        add("mod1", slabs(w_mod, range(0, 2 * C)))
        add("a_gate", slabs(w_in, range(C, 2 * C)))
        add("a_val", slabs(w_in, range(0, C)))
        add("v", slabs(w_in, range(3 * C, 4 * C)))
        add("u", slabs(w_in, range(2 * C, 3 * C)))
        add("g_a", slabs(w_in, range(4 * C, 5 * C)))
        add("g_b", slabs(w_in, range(5 * C, 6 * C)))
        add("mod2", slabs(w_mod, range(2 * C, 6 * C)))
        add("w_b", slabs(A["w_b"][0], range(C)))
        add("w_a", slabs(A["w_a"][0], range(C)))
        add("w_out", slabs(A["w_out"][0], range(C)))
        PRE = len(stream)
        assert PRE % RING == 0
        for i in range(2):
            if i == 1:
                add("qkv", slabs(gdn_in, range(0, 3 * C)))
                add("z", slabs(gdn_in, range(3 * C, 4 * C)))
                add("gdn_out", slabs(gdn_out, range(C)))
            add(f"gate{i}", slabs(A["ple_gate_w_2"][i], range(C)))
            add(f"w1_{i}", slabs(A["mlp_w1_2"][i], range(DFF // BANK)))
            add(f"w2_{i}", [unit(A["mlp_w2_2"][i], kq, c) for kq in range(DFF // (UK * P)) for c in range(C)])
        first_unit = {}
        for n, (name, _) in enumerate(stream):
            first_unit.setdefault(name, n)
        EXPERT = [("gu", kq, c) for pair in (0, 2) for kq in range(2) for c in (pair, pair + 1)] + \
                 [("dn", kq, c) for kq in range(2) for c in range(2)]
        NU = len(EXPERT)
        extra = [a(9).rearrange("p (k n) -> p k n", n=BANK), a(10).rearrange("p (k n) -> p k n", n=BANK)]
        eslot = [ring[:, u, :, :] if u < RING else extra[u - RING] for u in range(NU)]

        def slot_of(n):
            return (n if n < PRE else n - PRE) % RING

        def landed_count(n):
            return 16 * (n // RING + 1) if n < PRE else 16 * (PRE // RING + NE + (n - PRE) // RING + 1)

        first_group, total = {}, [0]

        def group(name, n, align=None):
            while align is not None and total[0] % BANKS != align:
                total[0] += 1
            first_group[name] = total[0]
            total[0] += n

        for name, n in (("cols", 1), ("wsT", 2), ("mod1", 1), ("hT", 4), ("a_gate", 4), ("a_val", 4), ("v", 4),
                        ("u", 4), ("g_a", 4), ("g_b", 4), ("mod2", 1), ("convT", 4), ("mix", 4),
                        ("w_b", 4), ("yaT", 4), ("w_a", 4), ("w_out", 4), ("y_tok", 4), ("h2T", 4),
                        ("router", 1), ("h2_tok", 4), ("pos", 1), ("gateT", 1)):
            group(name, n)
        group("moe", 4, align=0)
        group("g2_bc", 2)
        group("x2T", 4)
        group("pool", 4)
        group("pool_tok", 4)
        for i in range(2):
            if i == 1:
                group("x4T", 4)
                for s in range(6):
                    group(f"qkv{s}", 2)
                    if s:
                        group(f"qkvT{s - 1}", 2)
                group("z", 4)
                group("ba", 1)
                group("qkvT5", 2)
                for n in range(NT):
                    for name, k in (("g_col", 1), ("g_row", 2), ("kT", 2), ("qT", 2), ("kbT", 2), ("AT", 2),
                                    ("qkT", 2), ("X1", 2)):
                        group(f"{name}.{n}", k)
                    for s in range(1, 6):
                        group(f"T{s}.{n}", 2)
                        if s < 5:
                            group(f"X{s + 1}.{n}", 2)
                        group(f"XT{s}.{n}", 2)
                    group(f"u.{n}", 2)
                    group(f"wT.{n}", 2)
                    for c in range(2):
                        if 2 * n + c > 0:
                            group(f"wS.{n}.{c}", 2)
                        if 2 * n + c < 3:
                            group(f"S.{n}.{c}", 2)
                        group(f"o.{n}.{c}", 2)
                    group(f"oT.{n}", 2)
                group("gdn_out", 4)
            group(f"xT_{i}", 4)
            group(f"pT_{i}", 1)
            group(f"gate_{i}", 4)
            group(f"proj_{i}", 4)
            group(f"w1_{i}", 2 * DFF // BANK)
            group(f"w2_{i}", 4)

        def G(name, i=0):
            return first_group[name] + i

        def bank(g):
            return banks[g % BANKS]

        used, at = {}, [0] * BANKS
        order = []
        for name, g0 in first_group.items():
            order.append((name, g0))
        names = [n for n, _ in order]
        sizes = {}
        for j, (name, g0) in enumerate(order):
            nxt = order[j + 1][1] if j + 1 < len(order) else total[0]
            sizes[name] = nxt - g0
        sizes["gateT"] = 1
        for name in names:
            for g in range(first_group[name], first_group[name] + sizes[name]):
                at[g % BANKS] += 1
                used[g] = at[g % BANKS]

        bank_full = [sem(f"bank_full{i}") for i in range(BANKS)]
        bank_free = [sem(f"bank_free{i}") for i in range(BANKS)]

        def claim(pe, g):
            if used[g] > 1:
                pe.wait_ge(bank_free[g % BANKS], used[g] - 1)

        def full(eng, g):
            eng.wait_ge(bank_full[g % BANKS], used[g])

        def emptied(eng, g):
            eng.wait_ge(bank_free[g % BANKS], used[g])

        def fills(ins, g):
            ins.then_inc(bank_full[g % BANKS], 1)

        def empties(ins, g):
            ins.then_inc(bank_free[g % BANKS], 1)

        w_full = [sem(f"w_full{u}") for u in range(NU)]
        w_used = sem("w_used")
        root_asked, root_given = sem("root_asked"), sem("root_given")
        x_in = sem("x_in")
        packs_in = sem("packs_in")
        ws_in = sem("ws_in")
        rows_in = sem("rows_in")
        bc_in = sem("bc_in")
        bc_used = sem("bc_used")
        late_in = sem("late_in")
        consts = sem("consts")
        pool_step = sem("pool_step")
        dve_step = sem("dve_step")
        act_step = sem("act_step")
        conv_step = sem("conv_step")
        cond_ready = sem("cond_ready")
        wsT_ready = sem("wsT_ready")
        mod1_ready = sem("mod1_ready")
        hid_ready = sem("hid_ready")
        mod2_ready = sem("mod2_ready")
        xn_ready = sem("xn_ready")
        conv_ready = sem("conv_ready")
        v_ready = sem("v_ready")
        m_ready = sem("m_ready")
        route_ready = sem("route_ready")
        bgu_ready = sem("bgu_ready")
        areas_free = sem("areas_free")
        moe_pe, moe_dve, moe_act = sem("moe_pe"), sem("moe_dve"), sem("moe_act")
        diag_ready = sem("diag_ready")
        pooled_ready = sem("pooled_ready")
        x_ready = sem("x_ready")
        pool_done = sem("pool_done")
        cpad_ready = sem("cpad_ready")
        silu_ready = sem("silu_ready")
        conv4_ready = sem("conv4_ready")
        gdn_dve = sem("gdn_dve")
        gdn_act = sem("gdn_act")
        pe_mark = sem("pe_mark")
        out_done = sem("out_done")

        COL, c0 = {}, 0
        for name, n in (("c", ND), ("b_mod", 48), ("b_in", 48), ("conv_b", ND), ("ln_a_g", ND), ("ln_a_b", ND),
                        ("b_a", ND), ("b_b", ND), ("b_out", ND), ("pool_b", ND), ("pool_scale", ND),
                        ("gdn_conv", 3 * ND * GTAPS), ("conv_w", TAPS * ND)):
            COL[name] = c0
            c0 += n
        assert c0 == BANK
        packs = area[:, 10 * 2048:10 * 2048 + 5 * P].rearrange("p (k n) -> p k n", n=P)
        PACK_ROWS = (128, 40, 96, 128, TAPS * ND - 128)
        b_s_row = area[0:1, 10 * 2048 + 1024:11 * 2048]
        ws_raw, wsT = half(9, 0), half(9, 1)
        row8 = area[0:1, 8 * 2048:8 * 2048 + D]

        def col(name, i):
            return cols[:, COL[name] + i:COL[name] + i + 1]

        def rows(v):
            return v.rearrange("(r n) -> r n", n=P)

        H = {}
        for name, (i, j) in dict(qkT=(1, 0), kbg=(1, 1), kT=(6, 0), kbT=(6, 1), qT=(7, 0), DT=(7, 1), AT=(8, 0),
                                 X=(8, 1), XT=(9, 0), T=(9, 1), state=(10, 0), g_row=(10, 1)).items():
            H[name] = half(i, j)
        H["kb"], H["qdT"], H["wT"], H["M"], H["u"], H["o"] = H["qkT"], H["kT"], H["kbT"], H["kbT"], H["T"], H["DT"]

        w3, w6, w7 = a(3), a(6), a(7)
        h2_tok = tok(2)
        xg = w3[:, 0:512].rearrange("p (d s) -> p d s", s=BLK)
        g_min, g_sig, g_act = w3[:, 512:1024], w3[:, 1024:1536], w3[:, 1536:2048]
        u_clip, e_act = w6[:, 0:512], w6[:, 512:1024]
        actT = w6[:, 1024:1536].rearrange("p (j s) -> p j s", s=P)
        y_blk = w6[:, 1536:2048]
        spread = w7[:, 0:256].rearrange("p (t s) -> p t s", s=P)
        spread_T = w7[:, 256:512]
        slots = w7[:, 512:640].rearrange("p (t s) -> p t s", s=BLK)
        bgu_raw = a(5)[0:96, :]
        bgu_hi, bgu_res = a(8)[0:96, :], a(6)[0:96, :]
        bgu_parts = a(4)[0:96, 1024:2048].bitcast(BF16)
        bgu_tmp = a(7)[0:96, 0:1024].bitcast(BF16)
        b_dn_sb = area[0:NE, 4 * 2048:4 * 2048 + D]

        R = {n: rt[:, i, :, :] for i, n in enumerate(
            ("logits", "above", "equal", "prefix", "tmp", "sel", "ex", "gates", "pos", "tmp2"))}
        s_ = {n: sm[:, i, :, :] for i, n in enumerate(
            ("b", "al", "abs", "sp", "gl", "beta", "g", "last", "eg", "kd", "ssq", "ssk", "sso", "ea", "t0"))}

        M = {n: i + 1 for i, n in enumerate(PE_STEPS)}
        V = {n: i + 1 for i, n in enumerate(DVE_STEPS)}
        Q = {n: i + 1 for i, n in enumerate(ACT_STEPS)}

        def pe_did(eng, k, step):
            eng.wait_ge(moe_pe, len(PE_STEPS) * (k + 1) + (M[step] + 1))

        def dve_did(eng, k, step):
            eng.wait_ge(moe_dve, len(DVE_STEPS) * k + V[step] + 1)

        def act_did(eng, k, step):
            eng.wait_ge(moe_act, len(ACT_STEPS) * k + Q[step] + 1)

        def expert_blocks(eng, own, steps, body, base=1):
            with eng.Fori(0, NE) as e:
                n_tok = eng.value_load(counts[0:1, bass.ds(e, 1)], min_val=0, max_val=S)
                with eng.Fori(1, NBLK) as b:
                    k = e * NBLK + (b - 1)
                    with eng.If(n_tok - b * BLK > 0):
                        body(e, b, k, False)
                    with eng.Else():
                        eng.wait_ge(own, k * len(steps) + base)
                        eng.sem_inc(own, len(steps))
                body(e, 0, e * NBLK + (NBLK - 1), True)

        block = ctx.enter_context(nc.Block())

        @block.sync
        def _(sp):
            def load(n):
                s = slot_of(n)
                if n >= PRE + RING:
                    sp.wait_ge(w_used, NU * NE + n - RING + 1)
                elif n >= PRE:
                    sp.wait_ge(w_used, PRE + NU * (NE - 1) + (n - PRE) + 1)
                elif n >= RING:
                    sp.wait_ge(w_used, n - RING + 1)
                sp.dma_start(ring[:, s, :, :], stream[n][1]).then_inc(w_full[s], 16)

            def expert_source(u, e):
                kind, kq, c = EXPERT[u]
                w = A["w_gu"] if kind == "gu" else A["w_dn"]
                w = w[0, bass.ds(e, 1), :, :] if not isinstance(e, int) else w[0, e:e + 1, :, :]
                return w[:, UK * P * kq:UK * P * (kq + 1), BANK * c:BANK * (c + 1)]\
                    .rearrange("o (k p) n -> p (o k) n", p=P)

            for n in range(PRE):
                load(n)
            for u in range(NU):
                if u < RING:
                    sp.wait_ge(w_used, PRE - RING + u + 1)
                elif u == RING:
                    sp.wait_ge(areas_free, 1)
                sp.dma_start(eslot[u], expert_source(u, 0)).then_inc(w_full[u], 16)
            with sp.Fori(1, NE) as e:
                for u in range(NU):
                    sp.wait_ge(w_used, e * NU + (PRE - NU + u + 1))
                    sp.dma_start(eslot[u], expert_source(u, e)).then_inc(w_full[u], 16)
            for n in range(PRE, len(stream)):
                load(n)
            sp.wait_ge(x_ready, 5)
            sp.dma_start(out[0].rearrange("(t p) d -> p t d", p=P), x_tok).then_inc(out_done, 16)
            sp.wait_ge(out_done, 16)

        @block.gpsimd
        def _(pool):
            n = [0]

            def link(ins):
                n[0] += 1
                ins.then_inc(pool_step, 1)
                pool.wait_ge(pool_step, n[0])

            def masked(t, pattern, base, cm, op, fill):
                link(nc.gpsimd.affine_select(out=t, in_=t, compare_op=op, fill=fill, base=base,
                                             pattern=pattern, channel_multiplier=cm))

            link(nc.gpsimd.memset(ident[:, :], 0.0))
            masked(ident[:, :], [[-1, P]], 0, 1, ALU.not_equal, 1.0)
            link(nc.gpsimd.memset(ones[:, :], 1.0))
            link(nc.gpsimd.memset(minus_half[:, :], -0.5))
            nc.gpsimd.memset(apad[:, :, 0:PADC], 0.0).then_inc(consts, 1)
            roots = [0]

            def inverse_root(t):
                roots[0] += 1
                pool.wait_ge(root_asked, roots[0])
                nc.gpsimd.tensor_tensor(t, t, minus_half[:, 0:t.shape[1]], ALU.pow).then_inc(root_given, 1)

            def norm_root():
                inverse_root(rstd[:, :])

            norm_root()
            link(nc.gpsimd.memset(before[:, :], 1.0))
            masked(before[:, :], [[1, P]], 0, -1, ALU.is_gt, 0.0)
            link(nc.gpsimd.memset(upto[:, :], 1.0))
            masked(upto[:, :], [[1, P]], 0, -1, ALU.is_ge, 0.0)
            link(nc.gpsimd.memset(upto[0:KCH, KCH:P], 0.0))
            link(nc.gpsimd.memset(chunk_ones[:, :], 0.0))
            link(nc.gpsimd.memset(chunk_ones[0:KCH, 0:KCH], 1.0))
            link(nc.gpsimd.memset(chunk_ones[KCH:P, KCH:P], 1.0))
            link(nc.gpsimd.tensor_scalar(decay_mask[:, :], upto[:, :], -1.0, 1e30, ALU.add, ALU.mult))
            link(nc.gpsimd.memset(level[:, :, :], 0.0))
            for i in range(6):
                s = 1 << i
                k = P // (2 * s)
                v = level[:, i, :].rearrange("p (k r) -> p k r", r=2 * s)[:, :, s:2 * s]
                link(nc.gpsimd.memset(v, 1.0))
                masked(v, [[-2 * s, k], [0, s]], 0, 1, ALU.is_ge, 0.0)
                masked(v, [[2 * s, k], [0, s]], s - 1, -1, ALU.is_ge, 0.0)
            link(nc.gpsimd.iota(slot_int[:, :], pattern=[[BLK, NBLK], [0, 2], [1, BLK]], base=0,
                                channel_multiplier=0))
            link(nc.gpsimd.tensor_copy(slot_row[:, :, :, :].rearrange("p b r s -> p (b r s)"), slot_int[:, :]))
            link(nc.gpsimd.iota(slot_int[:, 0:16], pattern=[[1, 16]], base=1, channel_multiplier=0))
            link(nc.gpsimd.tensor_copy(inv_pos[:, :], slot_int[:, 0:16]))
            link(nc.gpsimd.memset(zeros[:, :], 0.0))
            link(nc.gpsimd.memset(expert_hot[:, :], 0.0))
            for r in range(3):
                masked(expert_hot[:, :], [[-1, NE]], -NE * r, 1, ALU.not_equal, 1.0)
            nc.gpsimd.memset(top8[:, :, :], 0.0).then_inc(consts, 1)

            def bc(dst, v):
                pool.dma_start(dst, v.rearrange("(o n) -> o n", o=1).to_broadcast([P, v.shape[0]]))\
                    .then_inc(bc_in, 16)

            norms = [(A["ln_v_g"][0], A["ln_v_b"][0]), (A["post1_g"][0], A["post1_b"][0]),
                     (A["post2_g"][0], A["post2_b"][0])] + \
                    [(A["ln_gain_2"][i, j], A["ln_bias_2"][i, j]) for i in range(2) for j in range(2)]

            def load_norm(i):
                if i:
                    pool.wait_ge(bc_used, i)
                bc(gain_bc[:, :], norms[i][0])
                bc(bias_bc[:, :], norms[i][1])

            late = [0]

            def load(*pairs):
                for dst, src in pairs:
                    late[0] += 16
                    pool.dma_start(dst, src).then_inc(late_in, 16)
                pool.wait_ge(late_in, late[0])

            load_norm(0)
            norm_root()
            load_norm(1)
            norm_root()
            for e in range(4):
                emptied(pool, G("w_b", e))
            load(*[(bgu_raw[NE * r:NE * (r + 1), :], A["b_gu"][0]) for r in range(3)],
                 (b_dn_sb, A["b_dn"][0]))
            norm_root()
            load_norm(2)
            norm_root()
            norm_root()
            for e in range(4):
                emptied(pool, G("moe", e))
            load((a(6).rearrange("p (g k d) -> p g k d", g=4, k=2),
                  A["pool_w_2"][0].rearrange("g (k p) d -> p g k d", p=P)),
                 (alog_bc[:, :], A["gdn_a_log_2"][0:1, :].to_broadcast([P, HEADS])),
                 (dt_bc[:, :], A["gdn_dt_bias_2"][0:1, :].to_broadcast([P, HEADS])),
                 (normw_bc[:, :], A["gdn_norm_w_2"][0:1, :].to_broadcast([P, P])),
                 (w_ba[:, :, :], gdn_in[:, 4 * D:4 * D + 2 * HEADS].rearrange("(k p) n -> p k n", p=P)))
            load_norm(3)
            norm_root()

            def load_ffn(i):
                pool.wait_ge(x_ready, 2 + 2 * i)
                load((tok(7), A["ple_proj_2"][i].rearrange("(k p) n -> p k n", p=P)),
                     (area[:, 8 * 2048:8 * 2048 + 512].rearrange("p (t c) -> p t c", t=NT),
                      A["p_2"][i, 0].rearrange("(t p) c -> p t c", p=P)),
                     (area[0:1, 8 * 2048 + 1024:9 * 2048], A["ple_gate_b_2"][i:i + 1, :]))

            load_ffn(0)
            load_norm(4)
            pool.wait_ge(pool_done, 1)
            cp = apad[:, :, :].rearrange("p m t -> p (m t)")[:, 0:8 * (S + 3)]\
                .rearrange("p (c m t) -> p c m t", c=2, m=4)
            nc.gpsimd.memset(cp[:, :, :, 0:3], 0.0).then_inc(cpad_ready, 1)
            norm_root()
            load_norm(5)
            for n_ in range(NT):
                inverse_root(s_["ssq"][:, n_, :])
                inverse_root(s_["ssk"][:, n_, :])
                inverse_root(s_["sso"][:, n_, :])
            norm_root()
            load_ffn(1)
            load_norm(6)
            norm_root()

        @block.tensor
        def _(pe):
            mm = nc.tensor.matmul

            def transposed(g, pieces):
                claim(pe, g)
                for i, (src, c) in enumerate(pieces):
                    k = src.shape[0]
                    ins = mm(bank(g)[0:src.shape[1], c:c + k], src, ident[0:k, 0:k], is_transpose=True,
                             start=True, stop=True)
                fills(ins, g)

            def unit_ready(n):
                pe.wait_ge(w_full[slot_of(n)], landed_count(n))
                return ring[:, slot_of(n), :, :]

            def feature_major(name, gname, xT, n_slab, after=None):
                n0 = first_unit[name]
                for s in range(n_slab):
                    u = [unit_ready(n0 + 2 * s), unit_ready(n0 + 2 * s + 1)]
                    for q in range(2):
                        g = G(gname, 2 * s + q)
                        claim(pe, g)
                        for m in range(2):
                            for k in range(ND):
                                c = (2 * q + m) * P
                                ins = mm(bank(g)[:, m * S:(m + 1) * S], u[k // UK][:, k % UK, c:c + P],
                                         xT[:, k, :], start=k == 0, stop=k == ND - 1)
                                if q == 1 and m == 1 and k == UK - 1:
                                    ins.then_inc(w_used, 1)
                        fills(ins, g)
                    pe.wait_ge(bank_full[g % BANKS], used[g])
                    pe.sem_inc(w_used, 1)
                    if after:
                        after(s)

            def token_major(name, gname, lhs, n_slab, bias=None):
                n0 = first_unit[name]
                for s in range(n_slab):
                    u = [unit_ready(n0 + 2 * s), unit_ready(n0 + 2 * s + 1)]
                    for t in range(NT):
                        g = G(gname, NT * s + t)
                        claim(pe, g)
                        if bias is not None:
                            mm(bank(g)[:, :], ones[0:1, :], bias[0:1, BANK * s:BANK * (s + 1)],
                               start=True, stop=False)
                        for k in range(ND):
                            ins = mm(bank(g)[:, :], lhs(k, t), u[k // UK][:, k % UK, :],
                                     start=k == 0 and bias is None, stop=k == ND - 1)
                            if t == NT - 1 and k == UK - 1:
                                ins.then_inc(w_used, 1)
                        fills(ins, g)
                    pe.wait_ge(bank_full[g % BANKS], used[g])
                    pe.sem_inc(w_used, 1)

            def tokens_of(xT):
                return lambda k, t: xT[:, k, t * P:(t + 1) * P]

            def to_features(gname, src, first=True):
                for q in range(4):
                    transposed(G(gname, q), [(src[:, t, (2 * q + m) * P:(2 * q + m + 1) * P], m * S + t * P)
                                             for m in range(2) for t in range(NT)])

            def to_tokens(gname, src, wait=None):
                for hf in range(NH):
                    for t in range(NT):
                        if wait:
                            wait(hf)
                        transposed(G(gname, NT * hf + t),
                                   [(src[:, 4 * hf + m, t * P:(t + 1) * P], m * P) for m in range(4)])

            pe.wait_ge(consts, 1)
            pe.wait_ge(packs_in, 16 * 14)
            g = G("cols")
            claim(pe, g)
            c = 0
            for i, r in enumerate(PACK_ROWS):
                ins = mm(bank(g)[:, c:c + r], packs[0:r, i, :], ident[0:r, 0:r], is_transpose=True,
                         start=True, stop=True)
                c += r
            fills(ins, g)
            pe.wait_ge(ws_in, 16)
            for q in range(2):
                transposed(G("wsT", q), [(ws_raw[:, 4 * q + i, :], i * P) for i in range(4)])

            def modulation(name, n_slab):
                g = G(name)
                claim(pe, g)
                for s in range(n_slab):
                    n0 = first_unit[name] + 2 * s
                    u = [unit_ready(n0), unit_ready(n0 + 1)]
                    for m in range(4):
                        for k in range(ND):
                            ins = mm(bank(g)[:, 4 * s + m:4 * s + m + 1], u[k // UK][:, k % UK, m * P:(m + 1) * P],
                                     cond[:, k:k + 1], start=k == 0, stop=k == ND - 1)
                            if m == 3 and k == UK - 1:
                                ins.then_inc(w_used, 1)
                    if s < n_slab - 1:
                        ins.then_inc(w_used, 1)
                fills(ins, g)
                full(pe, g)
                pe.sem_inc(w_used, 1)

            pe.wait_ge(cond_ready, 1)
            modulation("mod1", 2 * C)
            pe.wait_ge(xn_ready, 1)
            to_features("hT", tok(2))
            hT = feat(1)
            for q in range(4):
                emptied(pe, G("hT", q))
            feature_major("a_gate", "a_gate", hT, C)
            feature_major("a_val", "a_val", hT, C)
            pe.wait_ge(rows_in, 64)
            token_major("v", "v", tokens_of(hT), C, bias=row8)
            feature_major("u", "u", hT, C)
            feature_major("g_a", "g_a", hT, C)
            feature_major("g_b", "g_b", hT, C)
            modulation("mod2", 4 * C)
            pe.wait_ge(conv_ready, 1)
            to_tokens("convT", feat(3))
            pe.wait_ge(v_ready, 1)
            pe.wait_ge(wsT_ready, 1)
            vt = tok(4)
            for q in range(4):
                g = G("mix", q)
                claim(pe, g)
                for m in range(2):
                    gr = 2 * q + m
                    for t in range(NT):
                        o = bank(g)[:, m * S + t * P:m * S + (t + 1) * P]
                        mm(o, ones[0:1, :], b_s_row[0:1, gr * P:(gr + 1) * P], start=True, stop=False)
                        ins = mm(o, vt[:, t, gr * P:(gr + 1) * P], wsT[:, gr, :], start=False, stop=True)
                fills(ins, g)
            for q in range(4):
                emptied(pe, G("mix", q))
            feature_major("w_b", "w_b", feat(5), C)
            pe.wait_ge(xn_ready, 2)
            to_features("yaT", tok(8))
            for q in range(4):
                emptied(pe, G("yaT", q))
            feature_major("w_a", "w_a", feat(2), C)
            pe.wait_ge(m_ready, 4)
            feature_major("w_out", "w_out", feat(6), C)
            to_tokens("y_tok", feat(7), wait=lambda hf: (emptied(pe, G("w_out", 2 * hf)),
                                                         emptied(pe, G("w_out", 2 * hf + 1))))
            pe.wait_ge(xn_ready, 3)
            to_features("h2T", tok(3))
            for q in range(4):
                emptied(pe, G("h2T", q))
            h2T = feat(1)
            pe.wait_ge(rows_in, 64)
            g = G("router")
            claim(pe, g)
            for t in range(NT):
                for k in range(ND):
                    ins = mm(bank(g)[:, t * NE:(t + 1) * NE], h2T[:, k, t * P:(t + 1) * P], w_router[:, k, :],
                             start=k == 0, stop=k == ND - 1)
            fills(ins, g)
            to_tokens("h2_tok", h2T)
            pe.wait_ge(route_ready, 1)
            g = G("pos")
            claim(pe, g)
            sel = R["sel"]
            mm(bank(g)[:, 0:NE], before[:, :], sel[:, 0, :], start=True, stop=True)
            mm(bank(g)[:, NE:2 * NE], before[:, :], sel[:, 1, :], start=True, stop=False)
            mm(bank(g)[:, NE:2 * NE], ones[:, :], sel[:, 0, :], start=False, stop=True)
            mm(bank(g)[0:1, 2 * NE:3 * NE], ones[:, 0:1], sel[:, 0, :], start=True, stop=False)
            ins = mm(bank(g)[0:1, 2 * NE:3 * NE], ones[:, 0:1], sel[:, 1, :], start=False, stop=True)
            fills(ins, g)
            pe.wait_ge(route_ready, 2)
            transposed(G("gateT"), [(R["gates"][:, t, :], t * P) for t in range(NT)])

            emptied(pe, G("gateT"))
            pe.wait_ge(route_ready, 3)
            pe.wait_ge(bgu_ready, 1)
            for q in range(4):
                emptied(pe, G("h2_tok", q))
            emptied(pe, G("pos"))
            for i in range(4):
                ins = mm(banks[i][:, :], zeros[0:96, :], bgu_parts[:, 0:BANK], start=True, stop=False)
            ins.then_inc(moe_pe, 1)
            pe.wait_ge(moe_pe, 1)
            pe.sem_inc(moe_pe, len(PE_STEPS))
            bX, bG, bU, bT = banks[4], banks[5], banks[6], banks[7]
            h2 = h2_tok

            def body(e, b, k, last):
                dve_did(pe, k, "slots1")
                pe.wait_ge(moe_act, k * len(ACT_STEPS) + 1)
                for d in range(ND):
                    for t in range(NT):
                        ins = mm(bX[:, d * BLK:(d + 1) * BLK], h2[:, t, d * P:(d + 1) * P], slots[:, t, :],
                                 start=t == 0, stop=t == NT - 1)
                ins.then_inc(moe_pe, 1)
                dve_did(pe, k, "tokens")
                for part, (bk, u0) in enumerate(((bG, 0), (bU, 4))):
                    for hf in range(2):
                        ins = mm(bk[hf * BLK:(hf + 1) * BLK, :], expert_sel[:, :],
                                 bgu_parts[:, (2 * part + hf) * BANK:(2 * part + hf + 1) * BANK],
                                 start=True, stop=False)
                        if part == 1 and hf == 0 and last:
                            ins.then_inc(w_used, 1)
                    for kt in range(ND):
                        for hf in range(2):
                            u = u0 + 2 * (kt // UK) + hf
                            if kt % UK == 0:
                                pe.wait_ge(w_full[u], e * 16 + (16 * (PRE // RING if u < RING else 0) + 16))
                            ins = mm(bk[hf * BLK:(hf + 1) * BLK, :], xg[:, kt, :], eslot[u][:, kt % UK, :],
                                     start=False, stop=kt == ND - 1)
                            if kt == ND - 1 and hf == 1:
                                ins.then_inc(moe_pe, 1)
                            elif kt % UK == UK - 1 and last:
                                ins.then_inc(w_used, 1)
                dve_did(pe, k, "spread1")
                for t in range(NT):
                    ins = mm(bX[:, t * P:(t + 1) * P], spread[:, t, :], ident[:, :], is_transpose=True,
                             start=True, stop=True)
                    if t == 0 and last:
                        ins.then_inc(w_used, 1)
                ins.then_inc(moe_pe, 1)
                for i, bk in enumerate((bT, bU)):
                    dve_did(pe, k, f"act{i}")
                    for j in range(2):
                        ins = mm(bk[:, j * P:(j + 1) * P], e_act[:, (2 * i + j) * P:(2 * i + j + 1) * P],
                                 ident[:, :], is_transpose=True, start=True, stop=True)
                    ins.then_inc(moe_pe, 1)
                kts = (0, 1, 4, 5, 2, 3, 6, 7)
                for n, kt in enumerate(kts):
                    if n == 0:
                        dve_did(pe, k, "act_T0")
                    if n == 4:
                        dve_did(pe, k, "act_T1")
                    for hf in range(2):
                        u = 8 + 2 * (kt // UK) + hf
                        if kt % UK == 0:
                            pe.wait_ge(w_full[u], e * 16 + (16 * (PRE // RING if u < RING else 0) + 16))
                        j, fh = kt % UK, kt // UK
                        ins = mm(bG[hf * BLK:(hf + 1) * BLK, :], actT[:, j, fh * BLK:(fh + 1) * BLK],
                                 eslot[u][:, kt % UK, :], start=n == 0, stop=n == ND - 1)
                        if n == ND - 1 and hf == 1:
                            ins.then_inc(moe_pe, 1)
                        elif kt in (3, 7) and last:
                            ins.then_inc(w_used, 1)
                act_did(pe, k, "down")
                for t in range(NT):
                    for hf in range(2):
                        ins = mm(banks[2 * t + hf][:, :], spread_T[hf * BLK:(hf + 1) * BLK, t * P:(t + 1) * P],
                                 y_blk[hf * BLK:(hf + 1) * BLK, :], start=False, stop=False)
                        if t == 0 and hf == 0 and last:
                            ins.then_inc(w_used, 1)
                ins.then_inc(moe_pe, 1)

            expert_blocks(pe, moe_pe, PE_STEPS, body, base=len(PE_STEPS) + 1)
            for t in range(NT):
                for hf in range(NH):
                    g = G("moe", 2 * t + hf)
                    ins = mm(bank(g)[:, :], gateT[:, t * P:(t + 1) * P], b_dn_sb[:, hf * BANK:(hf + 1) * BANK],
                             start=False, stop=True)
                    fills(ins, g)

            pe.wait_ge(diag_ready, 1)
            diag = half(5, 0)
            for q in range(2):
                g = G("g2_bc", q)
                claim(pe, g)
                for i in range(4):
                    ins = mm(bank(g)[:, i * P:(i + 1) * P], ones[:, :], diag[:, 4 * q + i, :], start=True, stop=True)
                fills(ins, g)
            pe.wait_ge(x_ready, 1)
            to_features("x2T", x_tok)
            pe.wait_ge(pooled_ready, 1)
            pe.wait_ge(late_in, 144)
            pw = a(6).rearrange("p (g k d) -> p g k d", g=4, k=2)
            pooled = feat(8)
            for gi in range(4):
                g = G("pool", gi)
                claim(pe, g)
                for m in range(2):
                    for k in range(2):
                        ins = mm(bank(g)[:, m * S:(m + 1) * S], pw[:, gi, k, m * P:(m + 1) * P],
                                 pooled[:, 2 * gi + k, :], start=k == 0, stop=k == 1)
                fills(ins, g)
            for gi in range(4):
                emptied(pe, G("pool", gi))
            to_tokens("pool_tok", feat(7))

            def ffn(i):
                pe.wait_ge(x_ready, 2 + 2 * i)
                to_features(f"xT_{i}", x_tok)
                pe.wait_ge(late_in, 192 + 48 * i)
                pt = area[:, 8 * 2048:8 * 2048 + 512].rearrange("p (t c) -> p t c", t=NT)
                transposed(G(f"pT_{i}"), [(pt[:, t, m * P:(m + 1) * P], m * S + t * P)
                                          for m in range(2) for t in range(NT)])
                for q in range(4):
                    emptied(pe, G(f"xT_{i}", q))
                xT = feat(1)
                gb = area[0:1, 8 * 2048 + 1024:9 * 2048]
                token_major(f"gate{i}", f"gate_{i}", tokens_of(xT), C, bias=gb)
                emptied(pe, G(f"pT_{i}"))
                pT = area[:, 8 * 2048 + 512:8 * 2048 + 1024].rearrange("p (m t) -> p m t", m=2)
                proj = tok(7)
                for s in range(NH):
                    for t in range(NT):
                        g = G(f"proj_{i}", NT * s + t)
                        claim(pe, g)
                        for k in range(2):
                            ins = mm(bank(g)[:, :], pT[:, k, t * P:(t + 1) * P],
                                     proj[:, k, s * BANK:(s + 1) * BANK], start=k == 0, stop=k == 1)
                        fills(ins, g)
                feature_major(f"w1_{i}", f"w1_{i}", xT, DFF // BANK)
                n0 = first_unit[f"w2_{i}"]
                KQ = DFF // (UK * P)
                for j in range(4):
                    claim(pe, G(f"w2_{i}", j))
                for kq in range(KQ):
                    pe.wait_ge(hid_ready, 2 * (DFF // BANK * i + kq + 1))
                    for c in range(C):
                        u = unit_ready(n0 + C * kq + c)
                        for t in range(NT):
                            g = G(f"w2_{i}", NT * c + t)
                            for k in range(UK):
                                f = UK * kq + k
                                hid = feat(2 + f // 8)[:, f % 8, t * P:(t + 1) * P]
                                ins = mm(bank(g)[:, :], hid, u[:, k, :], start=kq == 0 and k == 0,
                                         stop=kq == KQ - 1 and k == UK - 1)
                            if kq == KQ - 1:
                                fills(ins, g)
                            elif t == NT - 1:
                                ins.then_inc(w_used, 1)
                        if kq == KQ - 1:
                            full(pe, g)
                            pe.sem_inc(w_used, 1)

            ffn(0)

            pe.wait_ge(x_ready, 3)
            to_features("x4T", x_tok)
            for q in range(4):
                emptied(pe, G("x4T", q))
            xT = feat(1)
            sl = [half(6, j).rearrange("p (m u) d -> p m (u d)", m=4) for j in range(2)]

            def qkv_T(s):
                pe.wait_ge(silu_ready, s + 1)
                for t in range(NT):
                    transposed(G(f"qkvT{s}", t), [(sl[s % 2][:, m, t * P:(t + 1) * P], m * P) for m in range(4)])

            n0 = first_unit["qkv"]
            for s in range(6):
                first_unit[f"qkv{s}"] = n0 + 2 * s
                feature_major(f"qkv{s}", f"qkv{s}", xT, 1)
                if s:
                    qkv_T(s - 1)
            token_major("z", "z", tokens_of(xT), C)
            g = G("ba")
            claim(pe, g)
            pe.wait_ge(late_in, 144)
            for t in range(NT):
                for k in range(ND):
                    ins = mm(bank(g)[:, t * 2 * HEADS:(t + 1) * 2 * HEADS], xT[:, k, t * P:(t + 1) * P],
                             w_ba[:, k, :], start=k == 0, stop=k == ND - 1)
            fills(ins, g)
            qkv_T(5)
            kk, qq = tok(3), tok(2)
            ev = [0]

            def dve_step_ready():
                ev[0] += 1
                pe.wait_ge(gdn_dve, ev[0])

            def heads(name, fn):
                for q in range(2):
                    g = G(name, q)
                    claim(pe, g)
                    for i in range(4):
                        ins = fn(bank(g), i, 4 * q + i)
                    fills(ins, g)

            def product(l, r):
                return lambda bk, i, h: mm(bk[:, i * P:(i + 1) * P], l[:, h, :], r[:, h, :], start=True, stop=True)

            def tr(src):
                return lambda bk, i, h: mm(bk[:, i * P:(i + 1) * P], src(h), ident[:, :], is_transpose=True,
                                           start=True, stop=True)

            def both_emptied(name):
                for q in range(2):
                    emptied(pe, G(name, q))

            for n in range(NT):
                dve_step_ready()
                g = G(f"g_col.{n}")
                claim(pe, g)
                mm(bank(g)[:, 0:HEADS], upto[:, :], s_["gl"][:, n, :], start=True, stop=True)
                ins = mm(bank(g)[:, HEADS:2 * HEADS], chunk_ones[:, :], s_["gl"][:, n, :], start=True, stop=True)
                fills(ins, g)
                heads(f"g_row.{n}", lambda bk, i, h: mm(bk[:, i * P:(i + 1) * P], H["M"][:, h, :], upto[:, :],
                                                        start=True, stop=True))
                dve_step_ready()
                heads(f"kT.{n}", tr(lambda h: kk[:, n, h * P:(h + 1) * P]))
                heads(f"qT.{n}", tr(lambda h: qq[:, n, h * P:(h + 1) * P]))
                both_emptied(f"g_row.{n}")
                heads(f"kbT.{n}", tr(lambda h: H["kb"][:, h, :]))
                both_emptied(f"kT.{n}")
                both_emptied(f"kbT.{n}")
                heads(f"AT.{n}", product(H["kT"], H["kbT"]))
                both_emptied(f"qT.{n}")
                heads(f"qkT.{n}", product(H["kT"], H["qT"]))
                dve_step_ready()
                heads(f"X1.{n}", tr(lambda h: H["XT"][:, h, :]))
                both_emptied(f"X1.{n}")
                for s in range(1, 6):
                    dve_step_ready()
                    heads(f"T{s}.{n}", product(H["M"], H["X"]))
                    both_emptied(f"T{s}.{n}")
                    if s < 5:
                        heads(f"X{s + 1}.{n}", product(H["XT"], H["T"]))
                    heads(f"XT{s}.{n}", product(H["T"], H["XT"]))
                    if s < 5:
                        both_emptied(f"X{s + 1}.{n}")
                    both_emptied(f"XT{s}.{n}")
                dve_step_ready()
                vb = tok(4)[:, n, :].rearrange("p (h d) -> p h d", d=P)
                kd = tok(3)[:, n, :].rearrange("p (h d) -> p h d", d=P)
                heads(f"u.{n}", product(H["XT"], vb))
                heads(f"wT.{n}", product(H["kbg"], H["XT"]))
                both_emptied(f"u.{n}")
                both_emptied(f"wT.{n}")
                for c in range(2):
                    r = slice(c * KCH, (c + 1) * KCH)
                    first = 2 * n + c == 0
                    if not first:
                        dve_step_ready()
                        heads(f"wS.{n}.{c}", lambda bk, i, h: mm(
                            bk[r, i * P:(i + 1) * P], H["wT"][:, h, r], H["state"][:, h, :], start=True, stop=True))
                        both_emptied(f"wS.{n}.{c}")

                    def o_of(bk, i, h):
                        if not first:
                            mm(bk[r, i * P:(i + 1) * P], H["qdT"][:, h, r], H["state"][:, h, :],
                               start=True, stop=False)
                        return mm(bk[r, i * P:(i + 1) * P], H["qkT"][r, h, r], H["u"][r, h, :],
                                  start=first, stop=True)

                    if 2 * n + c < 3:
                        heads(f"S.{n}.{c}", lambda bk, i, h: mm(
                            bk[:, i * P:(i + 1) * P], kd[r, h, :], H["u"][r, h, :], start=True, stop=True))
                    heads(f"o.{n}.{c}", o_of)
                dve_step_ready()
                heads(f"oT.{n}", tr(lambda h: H["o"][:, h, :]))
            for n in range(NT):
                both_emptied(f"oT.{n}")
            oT = tok(2)
            token_major("gdn_out", "gdn_out", lambda k, t: oT[:, t, k * P:(k + 1) * P], C)
            ffn(1)

        @block.scalar
        def _(act):
            f = nc.scalar.activation
            n = [0]

            def link(ins):
                n[0] += 1
                ins.then_inc(act_step, 1)
                act.wait_ge(act_step, n[0])

            def load(dst, src, s):
                act.dma_start(dst, src).then_inc(s, 16)

            load(x_tok, A["x"][0].rearrange("(t p) d -> p t d", p=P), x_in)
            r = 0
            for v in (A["c"][0], A["b_mod"][0], A["b_in"][0], A["conv_b"][0], A["ln_a_g"][0], A["ln_a_b"][0]):
                k = v.shape[0] // P
                load(packs[r:r + k, 0, :], rows(v), packs_in)
                r += k
            r = 0
            for v in (A["b_a"][0], A["b_b"][0], A["b_out"][0],
                      A["pool_b_2"][0].rearrange("g d -> (g d)"), A["pool_scale_2"][0]):
                load(packs[r:r + ND, 1, :], rows(v), packs_in)
                r += ND
            load(packs[0:96, 2, :], A["gdn_conv_2"][0].rearrange("j (m n) -> (j m) n", n=P), packs_in)
            cw = A["conv_w"][0].rearrange("j (m n) -> (j m) n", n=P)
            load(packs[0:P, 3, :], cw[0:P, :], packs_in)
            load(packs[0:PACK_ROWS[4], 4, :], cw[P:TAPS * ND, :], packs_in)
            load(ws_raw, A["w_s"][0].rearrange("g i j -> i g j"), ws_in)
            load(row8, A["b_in"][0:1, 3 * D:4 * D], rows_in)
            load(b_s_row, A["b_s"][0].rearrange("(o g) i -> o (g i)", o=1), rows_in)
            load(w_router[:, :, :], A["w_router"][0].rearrange("(k p) e -> p k e", p=P), rows_in)
            load(router_bc[:, :], A["b_router"][0:1, :].to_broadcast([P, NE]), rows_in)

            emptied(act, G("cols"))
            f(cond[:, :], cols[:, COL["c"]:COL["c"] + ND], ACT.Silu).then_inc(cond_ready, 1)

            def pairs(gname, fn):
                for q in range(4):
                    g = G(gname, q)
                    full(act, g)
                    for m in range(2):
                        ins = fn(2 * q + m, bank(g)[:, m * S:(m + 1) * S])
                    empties(ins, g)

            act.wait_ge(mod1_ready, 1)
            pairs("hT", lambda m, ps: f(feat(1)[:, m, :], ps, ACT.Identity, bias=modc[:, m:m + 1],
                                        scale=sc1p[:, m:m + 1]))
            pairs("a_gate", lambda m, ps: f(feat(3)[:, m, :], ps, ACT.Sigmoid, bias=col("b_in", ND + m)))
            for s in range(C):
                for t in range(NT):
                    g = G("v", NT * s + t)
                    full(act, g)
                    empties(f(tok(4)[:, t, s * BANK:(s + 1) * BANK], bank(g)[:, :], ACT.Gelu), g)
            pairs("u", lambda m, ps: f(feat(5)[:, m, :], ps, ACT.Gelu, bias=col("b_in", 2 * ND + m)))
            pairs("g_a", lambda m, ps: f(feat(6)[:, m, :], ps, ACT.Sigmoid, bias=col("b_in", 4 * ND + m)))
            pairs("g_b", lambda m, ps: f(feat(7)[:, m, :], ps, ACT.Sigmoid, bias=col("b_in", 5 * ND + m)))
            for hf in range(NH):
                for t in range(NT):
                    g = G("convT", NT * hf + t)
                    full(act, g)
                    empties(f(tok(8)[:, t, hf * BANK:(hf + 1) * BANK], bank(g)[:, :], ACT.Copy), g)
            pairs("yaT", lambda m, ps: f(feat(2)[:, m, :], ps, ACT.Silu, bias=col("ln_a_b", m),
                                         scale=col("ln_a_g", m)))
            act.wait_ge(mod2_ready, 1)
            pairs("h2T", lambda m, ps: f(feat(1)[:, m, :], ps, ACT.Identity, bias=modc[:, 24 + m:25 + m],
                                         scale=sc2p[:, m:m + 1]))
            for hf in range(NH):
                for t in range(NT):
                    g = G("h2_tok", NT * hf + t)
                    full(act, g)
                    empties(f(h2_tok[:, t, hf * BANK:(hf + 1) * BANK], bank(g)[:, :], ACT.Copy), g)
            act.wait_ge(route_ready, 1)
            for t in range(NT):
                ins = f(R["ex"][:, t, :], R["tmp"][:, t, :], ACT.Exp)
            ins.then_inc(moe_act, 1)

            def body(e, b, k, last):
                dve_did(act, k, "gate_min")
                f(g_sig, g_min, ACT.Sigmoid, scale=SWIGLU).then_inc(moe_act, 1)
                pe_did(act, k, "spread_T")
                f(spread_T, banks[4][:, 0:S], ACT.Copy).then_inc(moe_act, 1)
                pe_did(act, k, "down")
                f(y_blk, banks[5][:, :], ACT.Copy).then_inc(moe_act, 1)

            act.wait_ge(route_ready, 3)
            expert_blocks(act, moe_act, ACT_STEPS, body)

            for q in range(4):
                g = G("x2T", q)
                full(act, g)
                empties(f(apad[:, 2 * q:2 * q + 2, PADC:PADC + S],
                          bank(g)[:, :].rearrange("p (m t) -> p m t", m=2), ACT.Copy), g)

            def copy_T(gname, dst):
                for q in range(4):
                    g = G(gname, q)
                    full(act, g)
                    empties(f(dst[:, 2 * q:2 * q + 2, :], bank(g)[:, :].rearrange("p (m t) -> p m t", m=2),
                              ACT.Copy), g)

            def ffn(i):
                copy_T(f"xT_{i}", feat(1))
                g = G(f"pT_{i}")
                full(act, g)
                empties(f(area[:, 8 * 2048 + 512:8 * 2048 + 1024], bank(g)[:, :], ACT.Copy), g)
                for s in range(NH):
                    for t in range(NT):
                        g = G(f"gate_{i}", NT * s + t)
                        full(act, g)
                        empties(f(tok(6)[:, t, s * BANK:(s + 1) * BANK], bank(g)[:, :], ACT.Sigmoid), g)
                for q in range(2 * DFF // BANK):
                    g = G(f"w1_{i}", q)
                    full(act, g)
                    empties(f(area[:, 2 * 2048 + q * BANK:2 * 2048 + (q + 1) * BANK], bank(g)[:, :], ACT.Relu), g)

            ffn(0)
            copy_T("x4T", feat(1))
            cp = apad[:, :, :].rearrange("p m t -> p (m t)")[:, 0:8 * (S + 3)]\
                .rearrange("p (c m t) -> p c m t", c=2, m=4)
            sl = [half(6, j).rearrange("p (m u) d -> p m (u d)", m=4) for j in range(2)]
            act.wait_ge(cpad_ready, 1)

            def silu(s):
                act.wait_ge(conv4_ready, s + 1)
                f(sl[s % 2], sl[s % 2], ACT.Silu).then_inc(silu_ready, 1)

            for s in range(6):
                if s >= 2:
                    act.wait_ge(conv4_ready, s - 1)
                for q in range(2):
                    g = G(f"qkv{s}", q)
                    full(act, g)
                    empties(f(cp[:, s % 2, 2 * q:2 * q + 2, 3:3 + S],
                              bank(g)[:, :].rearrange("p (m t) -> p m t", m=2), ACT.Copy), g)
                if s:
                    silu(s - 1)
            silu(5)
            for s in range(NH):
                for t in range(NT):
                    g = G("z", NT * s + t)
                    full(act, g)
                    empties(f(tok(5)[:, t, s * BANK:(s + 1) * BANK], bank(g)[:, :], ACT.Silu), g)
            act.wait_ge(gdn_act, 1)
            link(f(s_["beta"], s_["b"], ACT.Sigmoid))
            link(f(s_["abs"], s_["abs"], ACT.Exp, scale=-1.0))
            link(f(s_["ea"][:, 0, :], alog_bc[:, :], ACT.Exp))
            f(s_["sp"], s_["abs"], ACT.Ln, bias=1.0).then_inc(gdn_act, 1)
            ev = [2]

            def dve_gave():
                ev[0] += 1
                act.wait_ge(gdn_act, ev[0])

            def copy_heads(name, dst):
                for q in range(2):
                    g = G(name, q)
                    full(act, g)
                    empties(f(dst[:, 4 * q:4 * q + 4, :],
                              bank(g)[:, :].rearrange("p (h d) -> p h d", d=P), ACT.Copy), g)

            for n_ in range(NT):
                dve_gave()
                link(f(s_["eg"][:, n_, :], s_["g"][:, n_, :], ACT.Exp))
                f(s_["kd"][:, n_, :], s_["kd"][:, n_, :], ACT.Exp).then_inc(gdn_act, 1)
                ev[0] += 1
                dve_gave()
                link(f(H["DT"], H["DT"], ACT.Exp))
                f(H["g_row"], H["g_row"], ACT.Exp).then_inc(gdn_act, 1)
                ev[0] += 1
                copy_heads(f"kT.{n_}", H["kT"])
                copy_heads(f"qT.{n_}", H["qT"])
                copy_heads(f"kbT.{n_}", H["kbT"])
                copy_heads(f"X1.{n_}", H["X"])
                for s in range(1, 6):
                    copy_heads(f"T{s}.{n_}", H["T"])
                copy_heads(f"u.{n_}", H["u"])
                copy_heads(f"wT.{n_}", H["wT"])
                for c in range(2):
                    r = slice(c * KCH, (c + 1) * KCH)
                    for q in range(2):
                        g = G(f"o.{n_}.{c}", q)
                        full(act, g)
                        empties(f(H["o"][r, 4 * q:4 * q + 4, :],
                                  bank(g)[r, :].rearrange("p (h d) -> p h d", d=P), ACT.Copy), g)
                copy_heads(f"oT.{n_}", tok(2)[:, n_, :].rearrange("p (h d) -> p h d", d=P))
            ffn(1)

        @block.vector
        def _(dve):
            v = nc.vector
            n = [0]

            def link(ins):
                n[0] += 1
                ins.then_inc(dve_step, 1)
                dve.wait_ge(dve_step, n[0])

            roots = [0]

            def inverse_root():
                roots[0] += 1
                dve.sem_inc(root_asked, 1)
                dve.wait_ge(root_given, roots[0])

            def moments(src):
                for t in range(NT):
                    for hf in range(NH):
                        link(v.bn_stats(stats[:, t, hf, :], src[:, t, hf * BANK:(hf + 1) * BANK]))
                for t in range(NT):
                    link(v.bn_aggr(mv[:, t, :], stats[:, t, :, :].rearrange("p a b -> p (a b)")))
                link(v.tensor_scalar(rstd[:, :], mv[:, :, 1], EPS, None, ALU.add))
                inverse_root()

            def normalised(dst, src, t):
                return v.tensor_scalar(dst[:, t, :], src[:, t, :], mv[:, t, 0:1], rstd[:, t:t + 1],
                                       ALU.subtract, ALU.mult)

            norm = [0]

            def layer_norm(x, done):
                norm[0] += 1
                moments(x)
                for t in range(NT):
                    link(normalised(x, x, t))
                dve.wait_ge(bc_in, 32 * norm[0])
                for t in range(NT):
                    link(v.tensor_tensor(x[:, t, :], x[:, t, :], gain_bc[:, :], ALU.mult))
                for t in range(NT):
                    link(v.tensor_tensor(x[:, t, :], x[:, t, :], bias_bc[:, :], ALU.add))
                done()

            def tick(s, k=1):
                dve.sem_inc(s, k)

            g = G("cols")
            full(dve, g)
            empties(v.tensor_copy(cols[:, :], bank(g)[:, :]), g)
            for q in range(2):
                g = G("wsT", q)
                full(dve, g)
                empties(v.tensor_copy(wsT[:, 4 * q:4 * q + 4, :],
                                      bank(g)[:, :].rearrange("p (h d) -> p h d", d=P)), g)
                emptied(dve, g)
            v.memset(wsT[KCH:P, :, 0:KCH], 0.0).then_inc(wsT_ready, 1)
            dve.wait_ge(x_in, 16)
            moments(x_tok)
            for t in range(NT):
                link(normalised(tok(2), x_tok, t))
            tick(xn_ready)
            emptied(dve, G("cols"))
            g = G("mod1")
            full(dve, g)
            empties(v.tensor_tensor(modc[:, 0:16], bank(g)[:, 0:16], cols[:, COL["b_mod"]:COL["b_mod"] + 16],
                                    ALU.add), g)
            emptied(dve, g)
            v.tensor_scalar(sc1p[:, :], modc[:, 8:16], 1.0, None, ALU.add).then_inc(mod1_ready, 1)
            dve.wait_ge(consts, 1)
            for q in range(4):
                emptied(dve, G("a_gate", q))
            for q in range(4):
                g = G("a_val", q)
                full(dve, g)
                for m in range(2):
                    ins = v.scalar_tensor_tensor(apad[:, 2 * q + m, PADC:PADC + S], bank(g)[:, m * S:(m + 1) * S],
                                                 col("b_in", 2 * q + m), feat(3)[:, 2 * q + m, :], ALU.add, ALU.mult)
                    if m == 0:
                        link(ins)
                empties(ins, g)
                emptied(dve, g)
            acc = feat(3)
            for m in range(ND):
                v.tensor_scalar(acc[:, m, :], apad[:, m, 0:S], col("conv_w", m), col("conv_b", m),
                                ALU.mult, ALU.add).then_inc(conv_step, 1)
            with dve.Fori(1, TAPS) as j:
                for m in range(ND):
                    dve.wait_ge(conv_step, j * ND + (m + 1 - ND))
                    v.scalar_tensor_tensor(acc[:, m, :], apad[:, m, bass.ds(j, S)],
                                           cols[:, bass.ds(j * ND + (COL["conv_w"] + m), 1)], acc[:, m, :],
                                           ALU.mult, ALU.add).then_inc(conv_step, 1)
            dve.wait_ge(conv_step, TAPS * ND)
            tick(conv_ready)
            for q in range(4):
                emptied(dve, G("v", q))
            layer_norm(tok(4), lambda: (tick(v_ready), tick(bc_used)))
            g = G("mod2")
            full(dve, g)
            empties(v.tensor_tensor(modc[:, 16:48], bank(g)[:, 0:32], cols[:, COL["b_mod"] + 16:COL["b_mod"] + 48],
                                    ALU.add), g)
            emptied(dve, g)
            v.tensor_scalar(sc2p[:, :], modc[:, 32:40], 1.0, None, ALU.add).then_inc(mod2_ready, 1)
            dve.wait_ge(mod2_ready, 1)
            for q in range(4):
                emptied(dve, G("convT", q))
            moments(tok(8))
            for t in range(NT):
                link(normalised(tok(8), tok(8), t))
            tick(xn_ready)
            for q in range(4):
                emptied(dve, G("u", q))
            for q in range(4):
                g = G("mix", q)
                full(dve, g)
                empties(v.tensor_tensor(feat(5)[:, 2 * q:2 * q + 2, :],
                                        bank(g)[:, :].rearrange("p (m t) -> p m t", m=2),
                                        feat(5)[:, 2 * q:2 * q + 2, :], ALU.mult), g)
            tick(areas_free)
            for nm, i in (("w_b", 7), ("w_a", 6)):
                for q in range(4):
                    emptied(dve, G("g_b" if nm == "w_b" else "g_a", q))
                    g = G(nm, q)
                    full(dve, g)
                    for m in range(2):
                        mi = 2 * q + m
                        ins = v.scalar_tensor_tensor(feat(i)[:, mi, :], bank(g)[:, m * S:(m + 1) * S],
                                                     col("b_b" if nm == "w_b" else "b_a", mi), feat(i)[:, mi, :],
                                                     ALU.add, ALU.mult)
                        if m == 0:
                            link(ins)
                    empties(ins, g)
                    if nm == "w_a":
                        emptied(dve, g)
                        emptied(dve, G("w_b", q))
                        v.tensor_tensor(feat(6)[:, 2 * q:2 * q + 2, :], feat(6)[:, 2 * q:2 * q + 2, :],
                                        feat(7)[:, 2 * q:2 * q + 2, :], ALU.add).then_inc(m_ready, 1)
            dve.wait_ge(m_ready, 4)
            for q in range(4):
                g = G("w_out", q)
                full(dve, g)
                for m in range(2):
                    mi = 2 * q + m
                    ins = v.tensor_scalar(feat(7)[:, mi, :], bank(g)[:, m * S:(m + 1) * S], col("b_out", mi),
                                          modc[:, 16 + mi:17 + mi], ALU.add, ALU.mult)
                    if m == 0:
                        link(ins)
                empties(ins, g)

            def residual(gname, alpha):
                for hf in range(NH):
                    for t in range(NT):
                        g = G(gname, NT * hf + t)
                        full(dve, g)
                        xs = x_tok[:, t, hf * BANK:(hf + 1) * BANK]
                        empties(v.scalar_tensor_tensor(xs, xs, alpha, bank(g)[:, :], ALU.mult, ALU.add), g)
                for i in range(4):
                    emptied(dve, G(gname, i))

            residual("y_tok", ALPHA1)
            layer_norm(x_tok, lambda: tick(bc_used))
            moments(x_tok)
            for t in range(NT):
                link(normalised(tok(3), x_tok, t))
            tick(xn_ready)
            dve.wait_ge(late_in, 64)
            dve.wait_ge(consts, 2)
            for r in range(3):
                ps = slice(NE * r, NE * (r + 1))
                for hf in range(2):
                    cs = slice(hf * 1024, (hf + 1) * 1024)
                    src = bgu_raw[ps, cs]
                    for i in range(r):
                        link(v.tensor_copy(bgu_tmp[ps, 0:1024], src))
                        link(v.tensor_tensor(bgu_res[ps, cs], src, bgu_tmp[ps, 0:1024], ALU.subtract))
                        src = bgu_res[ps, cs]
                    link(v.tensor_copy(bgu_parts[ps, cs], src))
            tick(bgu_ready)
            g = G("router")
            full(dve, g)
            dve.wait_ge(rows_in, 64)
            L = R["logits"]
            for t in range(NT):
                ins = v.tensor_tensor(L[:, t, :], bank(g)[:, t * NE:(t + 1) * NE], router_bc[:, :], ALU.add)
                if t == 0:
                    link(ins)
            empties(ins, g)
            emptied(dve, g)
            for t in range(NT):
                link(v.max(top8[:, t, :], L[:, t, :]))
            for t in range(NT):
                fourth = top8[:, t, TOPK - 1:TOPK]
                link(v.tensor_scalar(R["above"][:, t, :], L[:, t, :], fourth, None, ALU.is_gt))
                link(v.tensor_scalar(R["equal"][:, t, :], L[:, t, :], fourth, None, ALU.is_equal))
                link(v.tensor_reduce(rsum[:, t:t + 1], R["above"][:, t, :], AX.X, ALU.add))
                link(v.tensor_tensor_scan(R["prefix"][:, t, :], R["equal"][:, t, :], R["equal"][:, t, :], 0.0,
                                          ALU.add, ALU.bypass))
                link(v.tensor_scalar(R["tmp2"][:, t, :], R["prefix"][:, t, :], rsum[:, t:t + 1], float(TOPK),
                                     ALU.add, ALU.is_le))
                link(v.tensor_tensor(R["tmp2"][:, t, :], R["tmp2"][:, t, :], R["equal"][:, t, :], ALU.mult))
                link(v.tensor_tensor(R["sel"][:, t, :], R["tmp2"][:, t, :], R["above"][:, t, :], ALU.add))
                link(v.tensor_scalar(R["tmp"][:, t, :], L[:, t, :], top8[:, t, 0:1], None, ALU.subtract))
            tick(route_ready)
            dve.wait_ge(moe_act, 1)
            for t in range(NT):
                link(v.tensor_tensor(R["gates"][:, t, :], R["ex"][:, t, :], R["sel"][:, t, :], ALU.mult))
                link(v.tensor_reduce(rsum[:, t:t + 1], R["gates"][:, t, :], AX.X, ALU.add))
                link(v.reciprocal(rsum[:, t:t + 1], rsum[:, t:t + 1]))
                link(v.tensor_scalar(R["gates"][:, t, :], R["gates"][:, t, :], rsum[:, t:t + 1], None, ALU.mult))
            tick(route_ready)
            g = G("pos")
            full(dve, g)
            link(v.tensor_copy(counts[:, :], bank(g)[0:1, 2 * NE:3 * NE]))
            empties(v.scalar_tensor_tensor(R["pos"], bank(g)[:, 0:2 * NE].rearrange("p (t e) -> p t e", t=NT), 1.0,
                                           R["sel"], ALU.add, ALU.mult), g)
            emptied(dve, g)
            link(v.tensor_scalar(R["pos"], R["pos"], -1.0, None, ALU.add))
            g = G("gateT")
            full(dve, g)
            empties(v.tensor_copy(gateT[:, :], bank(g)[0:NE, 0:S]), g)
            emptied(dve, g)
            tick(route_ready)
            tick(moe_dve)

            def body(e, b, k, last):
                def step(ins):
                    ins.then_inc(moe_dve, 1)

                dve.wait_ge(moe_pe, k * len(PE_STEPS) + (M["spread_T"] + 1))
                step(v.tensor_copy(expert_sel[:, :], expert_hot[:, bass.ds(e, 1)].to_broadcast([96, BLK])))
                for t in range(NT):
                    step(v.tensor_scalar(slots[:, t, :], slot_row[:, b, 0, :] if isinstance(b, int) else
                                         slot_row[:, bass.ds(b, 1), 0, :].rearrange("p o s -> p (o s)"),
                                         R["pos"][:, t, bass.ds(e, 1)], None, ALU.is_equal))
                for t in range(NT):
                    row = slot_row[:, b, :, :] if isinstance(b, int) else \
                        slot_row[:, bass.ds(b, 1), :, :].rearrange("p o r s -> p (o r) s")
                    step(v.tensor_scalar(spread[:, t, :].rearrange("p (r s) -> p r s", r=2), row,
                                         R["pos"][:, t, bass.ds(e, 1)], R["gates"][:, t, bass.ds(e, 1)],
                                         ALU.is_equal, ALU.mult))
                pe_did(dve, k, "gathered")
                step(v.tensor_copy(xg[:, :, :], banks[4][:, :].rearrange("p (d s) -> p d s", s=BLK)))
                pe_did(dve, k, "gate")
                step(v.tensor_scalar(g_min, banks[5][:, :], LIMIT, None, ALU.min))
                act_did(dve, k, "sigmoid")
                step(v.tensor_tensor(g_act, g_min, g_sig, ALU.mult))
                pe_did(dve, k, "up")
                step(v.tensor_scalar(u_clip, banks[6][:, :], LIMIT, -LIMIT, ALU.min, ALU.max))
                dve_did(dve, k, "up_clip")
                for i in range(2):
                    cs = slice(i * 256, (i + 1) * 256)
                    step(v.scalar_tensor_tensor(e_act[:, cs], u_clip[:, cs], 1.0, g_act[:, cs], ALU.add, ALU.mult))
                for i, bk in enumerate((banks[7], banks[6])):
                    pe_did(dve, k, f"act_T{i}")
                    step(v.tensor_copy(actT[:, 2 * i:2 * i + 2, :],
                                       bk[:, 0:256].rearrange("p (j s) -> p j s", s=P)))

            expert_blocks(dve, moe_dve, DVE_STEPS, body)

            diag = half(5, 0)
            for m in range(ND):
                link(v.tensor_scalar(diag[:, m, :], ident[:, :], modc[:, 40 + m:41 + m], None, ALU.mult))
            tick(diag_ready)
            g2_bc = a(3)[:, 0:D]
            for q in range(2):
                g = G("g2_bc", q)
                full(dve, g)
                empties(v.tensor_copy(g2_bc[:, q * BANK:(q + 1) * BANK], bank(g)[:, :]), g)
                emptied(dve, g)
            ytmp = tok(4)
            for t in range(NT):
                for hf in range(NH):
                    g = G("moe", 2 * t + hf)
                    full(dve, g)
                    cs = slice(hf * BANK, (hf + 1) * BANK)
                    empties(v.tensor_tensor(ytmp[:, t, cs], bank(g)[:, :], g2_bc[:, cs], ALU.mult), g)
                    emptied(dve, g)
                    link(v.scalar_tensor_tensor(x_tok[:, t, cs], x_tok[:, t, cs], ALPHA1, ytmp[:, t, cs],
                                                ALU.mult, ALU.add))
            layer_norm(x_tok, lambda: (tick(x_ready), tick(bc_used)))

            for q in range(4):
                emptied(dve, G("x2T", q))
            link(v.reciprocal(inv_pos[:, :], inv_pos[:, :]))
            W = PADC + S
            wide = [area[:, i * 2048:i * 2048 + ND * (W - 16)].rearrange("p (m t) -> p m t", m=ND) for i in (2, 4)]

            def win(i, m, lo, hi=W):
                return wide[i][:, m:ND, lo - 16:hi - 16]

            src = None
            pooled = feat(8)
            lo, reach = 16, 1
            for gi, w in enumerate(WINDOWS):
                m0 = 2 * gi
                i = gi % 2
                if gi == 0:
                    link(v.tensor_tensor(win(0, 0, lo), apad[:, 0:ND, lo:W], apad[:, 0:ND, lo - 1:W - 1], ALU.add))
                else:
                    step_ = w // 2
                    lo = lo + step_
                    link(v.tensor_tensor(win(i, m0, lo), win(1 - i, m0, lo), win(1 - i, m0, lo - step_, W - step_),
                                         ALU.add))
                s_w = wide[i][:, m0:m0 + 2, PADC - 16:W - 16]
                xs = apad[:, m0:m0 + 2, PADC:W]
                link(v.scalar_tensor_tensor(pooled[:, m0:m0 + 2, :], s_w, 1.0 / w, xs, ALU.mult, ALU.subtract))
                e = w - 1
                inv = inv_pos[:, 0:e].unsqueeze(1).to_broadcast([P, 2, e])
                link(v.tensor_tensor(pooled[:, m0:m0 + 2, 0:e], s_w[:, :, 0:e], inv, ALU.mult))
                link(v.tensor_tensor(pooled[:, m0:m0 + 2, 0:e], pooled[:, m0:m0 + 2, 0:e], xs[:, :, 0:e],
                                     ALU.subtract))
            tick(pooled_ready)
            tick(pool_done)
            for gi in range(4):
                g = G("pool", gi)
                full(dve, g)
                for m in range(2):
                    mi = 2 * gi + m
                    ins = v.tensor_scalar(feat(7)[:, mi, :], bank(g)[:, m * S:(m + 1) * S], col("pool_b", mi),
                                          col("pool_scale", mi), ALU.add, ALU.mult)
                    if m == 0:
                        link(ins)
                empties(ins, g)
            residual("pool_tok", ALPHA2)
            layer_norm(x_tok, lambda: (tick(x_ready), tick(bc_used)))

            def ffn(i):
                pe_part = tok(6)
                for s in range(NH):
                    for t in range(NT):
                        emptied(dve, G(f"gate_{i}", NT * s + t))
                        g = G(f"proj_{i}", NT * s + t)
                        full(dve, g)
                        cs = slice(s * BANK, (s + 1) * BANK)
                        empties(v.tensor_tensor(pe_part[:, t, cs], bank(g)[:, :], pe_part[:, t, cs], ALU.mult), g)
                for q in range(2 * DFF // BANK):
                    emptied(dve, G(f"w1_{i}", q))
                    h = area[:, 2 * 2048 + q * BANK:2 * 2048 + (q + 1) * BANK]
                    v.tensor_tensor(h, h, h, ALU.mult).then_inc(hid_ready, 1)
                for s in range(NH):
                    for t in range(NT):
                        emptied(dve, G(f"proj_{i}", NT * s + t))
                        g = G(f"w2_{i}", NT * s + t)
                        full(dve, g)
                        cs = slice(s * BANK, (s + 1) * BANK)
                        empties(v.tensor_tensor(pe_part[:, t, cs], bank(g)[:, :], pe_part[:, t, cs], ALU.add), g)
                        emptied(dve, g)
                        link(v.scalar_tensor_tensor(x_tok[:, t, cs], x_tok[:, t, cs], ALPHA2, pe_part[:, t, cs],
                                                    ALU.mult, ALU.add))
                layer_norm(x_tok, lambda: (tick(x_ready), tick(bc_used)))

            ffn(0)

            cp = apad[:, :, :].rearrange("p m t -> p (m t)")[:, 0:8 * (S + 3)]\
                .rearrange("p (c m t) -> p c m t", c=2, m=4)
            sl = [half(6, j).rearrange("p (m u) d -> p m (u d)", m=4) for j in range(2)]

            def qkv_tokens(s):
                for t in range(NT):
                    g = G(f"qkvT{s}", t)
                    full(dve, g)
                    dst = tok(2 + s // 2)[:, t, (s % 2) * BANK:(s % 2 + 1) * BANK]
                    empties(v.tensor_copy(dst, bank(g)[:, :]), g)

            for s in range(6):
                if s >= 2:
                    qkv_tokens(s - 2)
                for q in range(2):
                    emptied(dve, G(f"qkv{s}", q))
                for j in range(GTAPS):
                    for m in range(4):
                        w = col("gdn_conv", j * 3 * ND + 4 * s + m)
                        src, dst = cp[:, s % 2, m, j:j + S], sl[s % 2][:, m, :]
                        if j == 0:
                            ins = v.tensor_scalar(dst, src, w, None, ALU.mult)
                        else:
                            ins = v.scalar_tensor_tensor(dst, src, w, dst, ALU.mult, ALU.add)
                        n[0] += 1
                        ins.then_inc(dve_step, 1)
                    dve.wait_ge(dve_step, n[0])
                tick(conv4_ready)
            qkv_tokens(4)
            g = G("ba")
            full(dve, g)
            ba = bank(g)[:, 0:4 * HEADS].rearrange("p (t c) -> p t c", t=NT)
            link(v.tensor_copy(s_["b"], ba[:, :, 0:HEADS]))
            empties(v.tensor_tensor(s_["al"], ba[:, :, HEADS:2 * HEADS],
                                    dt_bc[:, :].unsqueeze(1).to_broadcast([P, NT, HEADS]), ALU.add), g)
            emptied(dve, g)
            link(v.tensor_scalar(s_["abs"], s_["al"], -1.0, None, ALU.mult))
            link(v.tensor_tensor(s_["abs"], s_["abs"], s_["al"], ALU.max))
            tick(gdn_act)
            qkv_tokens(5)
            for i in range(2):
                emptied(dve, G("qkvT5", i))
            dve.wait_ge(gdn_act, 2)
            link(v.scalar_tensor_tensor(s_["sp"], s_["al"], 0.0, s_["sp"], ALU.max, ALU.add))
            link(v.scalar_tensor_tensor(s_["gl"], s_["sp"], -1.0,
                                        s_["ea"][:, 0, :].unsqueeze(1).to_broadcast([P, NT, HEADS]),
                                        ALU.mult, ALU.mult))
            qq, kk, vv, zz = tok(2), tok(3), tok(4), tok(5)
            ev = [2]

            def by_head(x, n_):
                return x[:, n_, :].rearrange("p (h d) -> p h d", d=P)

            def spread_head(c):
                return c.unsqueeze(2).to_broadcast([P, HEADS, P])

            def masked_by(i):
                return level[:, i, :].unsqueeze(1).to_broadcast([P, HEADS, P])

            for n_ in range(NT):
                link(v.tensor_copy(H["M"], spread_head(s_["gl"][:, n_, :])))
                tick(gdn_dve)
                for x, ss, scale in ((by_head(qq, n_), s_["ssq"][:, n_, :], P ** -0.5),
                                     (by_head(kk, n_), s_["ssk"][:, n_, :], 1.0)):
                    link(v.tensor_tensor(H["T"], x, x, ALU.mult))
                    link(v.tensor_reduce(ss, H["T"], AX.X, ALU.add))
                    link(v.tensor_scalar(ss, ss, 1e-6, None, ALU.add))
                    inverse_root()
                    if scale != 1.0:
                        link(v.tensor_scalar(ss, ss, scale, None, ALU.mult))
                    link(v.tensor_tensor(x, x, spread_head(ss), ALU.mult))
                link(v.tensor_tensor(H["kb"], by_head(kk, n_), spread_head(s_["beta"][:, n_, :]), ALU.mult))
                tick(gdn_dve)
                g = G(f"g_col.{n_}")
                full(dve, g)
                link(v.tensor_copy(s_["g"][:, n_, :], bank(g)[:, 0:HEADS]))
                empties(v.tensor_tensor(s_["kd"][:, n_, :], bank(g)[:, HEADS:2 * HEADS], s_["g"][:, n_, :],
                                        ALU.subtract), g)
                emptied(dve, g)
                tick(gdn_act)
                ev[0] += 1
                dve.wait_ge(gdn_act, ev[0] + 1)
                ev[0] += 1
                for q in range(2):
                    g = G(f"g_row.{n_}", q)
                    full(dve, g)
                    link(v.tensor_copy(H["g_row"][:, 4 * q:4 * q + 4, :],
                                       bank(g)[:, :].rearrange("p (h d) -> p h d", d=P)))
                    for i in range(4):
                        h = 4 * q + i
                        ins = v.scalar_tensor_tensor(H["DT"][:, h, :], bank(g)[:, i * P:(i + 1) * P],
                                                     s_["g"][:, n_, h:h + 1], decay_mask[:, :],
                                                     ALU.subtract, ALU.add)
                        if i < 3:
                            link(ins)
                    empties(ins, g)
                    emptied(dve, g)
                tick(gdn_act)
                ev[0] += 1
                dve.wait_ge(gdn_act, ev[0] + 1)
                ev[0] += 1
                link(v.tensor_tensor(by_head(vv, n_), by_head(vv, n_), spread_head(s_["beta"][:, n_, :]), ALU.mult))
                link(v.tensor_tensor(H["kbg"], H["kb"], spread_head(s_["eg"][:, n_, :]), ALU.mult))
                for nm, dst in (("AT", H["AT"]), ("qkT", H["qkT"])):
                    for q in range(2):
                        g = G(f"{nm}.{n_}", q)
                        full(dve, g)
                        empties(v.tensor_tensor(dst[:, 4 * q:4 * q + 4, :],
                                                bank(g)[:, :].rearrange("p (h d) -> p h d", d=P),
                                                H["DT"][:, 4 * q:4 * q + 4, :], ALU.mult), g)
                        emptied(dve, g)
                link(v.tensor_tensor(by_head(kk, n_), by_head(kk, n_), spread_head(s_["kd"][:, n_, :]), ALU.mult))
                for q in range(2):
                    full(dve, G(f"qkT.{n_}", q))
                link(v.tensor_tensor(H["qdT"], H["qT"], H["g_row"], ALU.mult))
                link(v.tensor_tensor(H["M"], H["AT"], masked_by(0), ALU.mult))
                link(v.tensor_tensor(H["XT"], ident[:, :].unsqueeze(1).to_broadcast([P, HEADS, P]), H["M"],
                                     ALU.subtract))
                tick(gdn_dve)
                for s in range(1, 6):
                    link(v.tensor_tensor(H["M"], H["AT"], masked_by(s), ALU.mult))
                    tick(gdn_dve)
                    for q in range(2):
                        full(dve, G(f"XT{s}.{n_}", q))
                    pairs_ = ([(f"X{s + 1}", H["X"])] if s < 5 else []) + [(f"XT{s}", H["XT"])]
                    for nm, dst in pairs_:
                        for q in range(2):
                            g = G(f"{nm}.{n_}", q)
                            full(dve, g)
                            d4 = dst[:, 4 * q:4 * q + 4, :]
                            empties(v.tensor_tensor(d4, d4, bank(g)[:, :].rearrange("p (h d) -> p h d", d=P),
                                                    ALU.subtract), g)
                            emptied(dve, g)
                tick(gdn_dve)
                for c in range(2):
                    r = slice(c * KCH, (c + 1) * KCH)
                    if 2 * n_ + c > 0:
                        tick(gdn_dve)
                        for q in range(2):
                            emptied(dve, G(f"u.{n_}", q))
                            g = G(f"wS.{n_}.{c}", q)
                            full(dve, g)
                            d4 = H["u"][r, 4 * q:4 * q + 4, :]
                            empties(v.tensor_tensor(d4, d4, bank(g)[r, :].rearrange("p (h d) -> p h d", d=P),
                                                    ALU.subtract), g)
                    if 2 * n_ + c < 3:
                        for q in range(2):
                            full(dve, G(f"o.{n_}.{c}", 1))
                            g = G(f"S.{n_}.{c}", q)
                            full(dve, g)
                            if 2 * n_ + c == 0:
                                empties(v.tensor_copy(H["state"][:, 4 * q:4 * q + 4, :],
                                                      bank(g)[:, :].rearrange("p (h d) -> p h d", d=P)), g)
                            else:
                                for i in range(4):
                                    h = 4 * q + i
                                    ins = v.scalar_tensor_tensor(
                                        H["state"][:, h, :], H["state"][:, h, :],
                                        H["g_row"][:, h, (c + 1) * KCH - 1:(c + 1) * KCH],
                                        bank(g)[:, i * P:(i + 1) * P], ALU.mult, ALU.add)
                                    if i < 3:
                                        link(ins)
                                empties(ins, g)
                            emptied(dve, g)
                for c in range(2):
                    for q in range(2):
                        emptied(dve, G(f"o.{n_}.{c}", q))
                so = s_["sso"][:, n_, :]
                link(v.tensor_tensor(H["X"], H["o"], H["o"], ALU.mult))
                link(v.tensor_reduce(so, H["X"], AX.X, ALU.add))
                link(v.tensor_scalar(so, so, 1.0 / P, 1e-6, ALU.mult, ALU.add))
                inverse_root()
                link(v.tensor_tensor(H["o"], H["o"], spread_head(so), ALU.mult))
                link(v.tensor_tensor(H["o"], H["o"], normw_bc[:, :].unsqueeze(1).to_broadcast([P, HEADS, P]),
                                     ALU.mult))
                for i in range(NT * NH):
                    emptied(dve, G("z", i))
                link(v.tensor_tensor(H["o"], H["o"], by_head(zz, n_), ALU.mult))
                tick(gdn_dve)
                if n_ == 0:
                    for q in range(2):
                        full(dve, G("oT.0", q))
            residual("gdn_out", ALPHA2)
            layer_norm(x_tok, lambda: (tick(x_ready), tick(bc_used)))
            ffn(1)


def kernel(**inputs):
    import numpy as np
    import concourse.bacc as bacc
    from concourse.bass_utils import run_bass_kernel_spmd

    nc = bacc.Bacc("TRN2", target_bir_lowering=False, num_devices=1)
    arrays, A = {}, {}
    for name, value in inputs.items():
        array = np.ascontiguousarray(value)
        arrays[f"in_{name}"] = array
        A[name] = nc.dram_tensor(f"in_{name}", array.shape, mybir.dt.from_np(array.dtype), kind="ExternalInput").ap()
    out = nc.dram_tensor("out", inputs["x"].shape, F32, kind="ExternalOutput").ap()
    build(nc, A, out)
    got = run_bass_kernel_spmd(nc, [arrays], core_ids=[0])
    return got.results[0]["out"]
```

```python
from contextlib import ExitStack

import concourse.bass as bass
from concourse import mybir

F32 = mybir.dt.float32
BF16 = mybir.dt.bfloat16
I32 = mybir.dt.int32
ALU = mybir.AluOpType
ACT = mybir.ActivationFunctionType
AX = mybir.AxisListType

P = 128
BANKS = 8
BANK = 512
UK = 4
RING = 10
KCH = 64
BLK = 64

PE_MAIN = ("gate", "scattered", "up", "next_gathered", "act_T0", "act_T1", "spread_T")
PE_OVER = ("gathered", "gate", "up", "spread_T", "act_T0", "act_T1", "down", "scattered")
DVE_MAIN = ("gate_min", "next_slots0", "next_slots1", "spread0", "spread1", "gated", "up_clip", "act0", "act1",
            "next_tokens", "next_row", "act_T0", "act_T1")
DVE_OVER = ("slots0", "slots1", "spread0", "spread1", "tokens", "gate_min", "gated", "up_clip", "act0", "act1",
            "act_T0", "act_T1")
ACT_MAIN = ACT_OVER = ("sigmoid", "spread_T", "down")

def build(nc, A, out):
    S, D = A["x"].shape[1], A["x"].shape[2]
    NT = S // P
    ND = D // P
    NH = D // BANK
    TAPS = A["conv_w"].shape[1]
    PADC = TAPS - 1
    NE = A["w_router"].shape[2]
    NG = A["w_s"].shape[1]
    TOPK = 4
    EPS = 1e-5
    ALPHA1 = 2.0 ** 0.25
    ALPHA2 = 4.0 ** 0.25
    LIMIT, SWIGLU = 7.0, 1.702
    WINDOWS = (2, 4, 8, 16)
    HEADS = A["gdn_a_log_2"].shape[1]
    DFF = A["mlp_w1_2"].shape[2]
    GTAPS = A["gdn_conv_2"].shape[1]
    NBLK = S // BLK
    assert NT == 2 and D == 1024 and HEADS == ND and NG == ND and NE == 32

    ctx = ExitStack()
    with ctx:
        def sb(name, shape, dt=F32):
            return ctx.enter_context(nc.sbuf_tensor(name, shape, dt))

        def sem(name):
            return ctx.enter_context(nc.semaphore(name))

        ring = sb("ring", [P, RING, UK, BANK])
        area = sb("area", [P, 11 * 2048])
        apad = sb("apad", [P, ND, PADC + S])
        gain_bc = sb("gain_bc", [P, D])
        bias_bc = sb("bias_bc", [P, D])
        cols = sb("cols", [P, BANK])
        ident = sb("ident", [P, P])
        ones = sb("ones", [P, P])
        minus_half = sb("minus_half", [P, 8])
        before = sb("before", [P, P])
        upto = sb("upto", [P, P])
        chunk_ones = sb("chunk_ones", [P, P])
        decay_mask = sb("decay_mask", [P, P])
        level = sb("level", [P, 6, P])
        slot_row = sb("slot_row", [P, NBLK, 2, BLK])
        slot_int = sb("slot_int", [P, NBLK * 2 * BLK], I32)
        inv_pos = sb("inv_pos", [P, 16])
        expert_hot = sb("expert_hot", [96, NE + 1], BF16)
        expert_sel = sb("expert_sel", [96, BLK], BF16)
        zeros = sb("zeros", [P, P], BF16)
        cond = sb("cond", [P, ND, 32])
        modc = sb("modc", [P, 48])
        sc1p = sb("sc1p", [P, ND])
        sc2p = sb("sc2p", [P, ND])
        stats = sb("stats", [P, NT, NH, 6])
        mv = sb("mv", [P, NT, 2])
        rstd = sb("rstd", [P, NT])
        w_router = sb("w_router_sb", [P, ND, NE])
        router_bc = sb("router_bc", [P, NE])
        rt = sb("rt", [P, 10, NT, NE])
        top8 = sb("top8", [P, NT, 8])
        rsum = sb("rsum", [P, NT])
        counts = sb("counts", [1, NE], I32)
        gateT = sb("gateT", [NE, S])
        place = sb("place", [P, NT, NE + 1])
        gate_of = sb("gate_of", [P, NT, NE + 1])
        sm = sb("sm", [P, 16, NT, HEADS])
        alog_bc = sb("alog_bc", [P, HEADS])
        dt_bc = sb("dt_bc", [P, HEADS])
        normw_bc = sb("normw_bc", [P, P])
        w_ba = sb("w_ba", [P, ND, 2 * HEADS])
        banks = [ctx.enter_context(nc.psum_tensor(f"bank{i}", [P, BANK], F32)) for i in range(BANKS)]

        def a(i, w=1):
            return area[:, i * 2048:(i + w) * 2048]

        def feat(i):
            return a(i).rearrange("p (m t) -> p m t", t=S)

        def tok(i):
            return a(i).rearrange("p (t d) -> p t d", d=D)

        def half(i, j):
            return area[:, i * 2048 + j * 1024:i * 2048 + (j + 1) * 1024].rearrange("p (h d) -> p h d", d=P)

        x_tok = tok(0)

        def unit(w, kq, c):
            return w[UK * P * kq:UK * P * (kq + 1), BANK * c:BANK * (c + 1)].rearrange("(k p) n -> p k n", p=P)

        def fours(w, cs):
            return [unit(w, kq, c) for c0 in cs for kq in range(2) for c in range(c0, c0 + 4)]

        def slabs(w, cs):
            return [unit(w, kq, c) for c in cs for kq in range(w.shape[0] // (UK * P))]

        w_mod, w_in = A["w_mod"][0], A["w_in"][0]
        gdn_in, gdn_out = A["gdn_w_in_2"][0], A["gdn_w_out_2"][0]
        C = D // BANK
        stream = []

        def add(name, units):
            stream.extend((name, u) for u in units)

        add("mod1", fours(w_mod, (0,)))
        add("a_gate", slabs(w_in, range(C, 2 * C)))
        add("a_val", slabs(w_in, range(0, C)))
        add("v", slabs(w_in, range(3 * C, 4 * C)))
        add("u", slabs(w_in, range(2 * C, 3 * C)))
        add("g_a", slabs(w_in, range(4 * C, 5 * C)))
        add("g_b", slabs(w_in, range(5 * C, 6 * C)))
        add("mod2", fours(w_mod, (4, 8)))
        add("w_b", slabs(A["w_b"][0], range(C)))
        add("w_a", slabs(A["w_a"][0], range(C)))
        add("w_out", slabs(A["w_out"][0], range(C)))
        PRE = len(stream)
        assert PRE % RING == 0
        for i in range(2):
            if i == 1:
                add("qkv", slabs(gdn_in, range(0, 3 * C)))
                add("z", slabs(gdn_in, range(3 * C, 4 * C)))
                add("gdn_out", slabs(gdn_out, range(C)))
            add(f"gate{i}", slabs(A["ple_gate_w_2"][i], range(C)))
            add(f"w1_{i}", slabs(A["mlp_w1_2"][i], range(DFF // BANK)))
            add(f"w2_{i}", [unit(A["mlp_w2_2"][i], kq, c) for kq in range(DFF // (UK * P)) for c in range(C)])
        first_unit = {}
        for n, (name, _) in enumerate(stream):
            first_unit.setdefault(name, n)
        EXPERT = [("gu", kq, c) for pair in (0, 2) for kq in range(2) for c in (pair, pair + 1)] + \
                 [("dn", kq, c) for kq in range(2) for c in range(2)]
        NU = len(EXPERT)
        extra = [a(9).rearrange("p (k n) -> p k n", n=BANK), a(10).rearrange("p (k n) -> p k n", n=BANK)]
        eslot = [ring[:, u, :, :] if u < RING else extra[u - RING] for u in range(NU)]

        def slot_of(n):
            return (n if n < PRE else n - PRE) % RING

        def landed_count(n):
            return 16 * (n // RING + 1) if n < PRE else 16 * (PRE // RING + NE + (n - PRE) // RING + 1)

        first_group, total = {}, [0]

        def group(name, n, align=None):
            while align is not None and total[0] % BANKS != align:
                total[0] += 1
            first_group[name] = total[0]
            total[0] += n

        for name, n in (("cols", 1), ("wsT", 2), ("mod1", 1), ("mod1T", 1), ("hT", 4), ("a_gate", 4), ("a_val", 4), ("v", 4),
                        ("u", 4), ("g_a", 4), ("g_b", 4), ("mod2", 2), ("mod2T", 2), ("convT", 4), ("mix", 4),
                        ("w_b", 4), ("yaT", 4), ("w_a", 4), ("w_out", 4), ("y_tok", 4), ("h2T", 4),
                        ("router", 1), ("h2_tok", 4), ("pos", 1), ("gateT", 1)):
            group(name, n)
        group("moe", 4, align=0)
        group("g2_bc", 2)
        group("x2T", 4)
        group("pool", 4)
        group("pool_tok", 4)
        for i in range(2):
            if i == 1:
                group("x4T", 4)
                for s in range(6):
                    group(f"qkv{s}", 2)
                    if s:
                        group(f"qkvT{s - 1}", 2)
                group("z", 4)
                group("ba", 1)
                group("qkvT5", 2)
                for n in range(NT):
                    for name, k in (("g_col", 1), ("g_row", 2), ("kT", 2), ("qT", 2), ("kbT", 2), ("AT", 2),
                                    ("qkT", 2), ("X1", 2)):
                        group(f"{name}.{n}", k)
                    for s in range(1, 6):
                        group(f"T{s}.{n}", 2)
                        group(f"XX{s}.{n}", 4 if s < 5 else 2)
                    group(f"u.{n}", 2)
                    group(f"wT.{n}", 2)
                    for c in range(2):
                        if 2 * n + c > 0:
                            group(f"wS.{n}.{c}", 2)
                        if 2 * n + c < 3:
                            group(f"S.{n}.{c}", 2)
                        group(f"o.{n}.{c}", 2)
                    group(f"oT.{n}", 2)
                group("gdn_out", 4)
            group(f"xT_{i}", 4)
            group(f"pT_{i}", 1)
            group(f"gate_{i}", 4)
            group(f"proj_{i}", 4)
            group(f"w1_{i}", 2 * DFF // BANK)
            group(f"w2_{i}", 4)

        def G(name, i=0):
            return first_group[name] + i

        def bank(g):
            return banks[g % BANKS]

        used, at = {}, [0] * BANKS
        order = []
        for name, g0 in first_group.items():
            order.append((name, g0))
        names = [n for n, _ in order]
        sizes = {}
        for j, (name, g0) in enumerate(order):
            nxt = order[j + 1][1] if j + 1 < len(order) else total[0]
            sizes[name] = nxt - g0
        sizes["gateT"] = 1
        for name in names:
            for g in range(first_group[name], first_group[name] + sizes[name]):
                at[g % BANKS] += 1
                used[g] = at[g % BANKS]

        bank_full = [sem(f"bank_full{i}") for i in range(BANKS)]
        bank_free = [sem(f"bank_free{i}") for i in range(BANKS)]

        def claim(pe, g):
            if used[g] > 1:
                pe.wait_ge(bank_free[g % BANKS], used[g] - 1)

        def full(eng, g):
            eng.wait_ge(bank_full[g % BANKS], used[g])

        def emptied(eng, g):
            eng.wait_ge(bank_free[g % BANKS], used[g])

        def fills(ins, g):
            ins.then_inc(bank_full[g % BANKS], 1)

        def empties(ins, g):
            ins.then_inc(bank_free[g % BANKS], 1)

        w_full = [sem(f"w_full{u}") for u in range(NU)]
        w_used = sem("w_used")
        root_asked, root_given = sem("root_asked"), sem("root_given")
        x_in = sem("x_in")
        packs_in = sem("packs_in")
        ws_in = sem("ws_in")
        rows_in = sem("rows_in")
        bc_in = sem("bc_in")
        bc_used = sem("bc_used")
        late_in = sem("late_in")
        consts = sem("consts")
        pool_step = sem("pool_step")
        dve_step = sem("dve_step")
        act_step = sem("act_step")
        conv_step = sem("conv_step")
        cond_ready = sem("cond_ready")
        wsT_ready = sem("wsT_ready")
        mod1_ready = sem("mod1_ready")
        hid_ready = sem("hid_ready")
        mod2_ready = sem("mod2_ready")
        xn_ready = sem("xn_ready")
        conv_ready = sem("conv_ready")
        v_ready = sem("v_ready")
        m_ready = sem("m_ready")
        route_ready = sem("route_ready")
        bgu_ready = sem("bgu_ready")
        areas_free = sem("areas_free")
        moe_pe, moe_dve, moe_act = sem("moe_pe"), sem("moe_dve"), sem("moe_act")
        diag_ready = sem("diag_ready")
        pooled_ready = sem("pooled_ready")
        x_ready = sem("x_ready")
        pool_done = sem("pool_done")
        cpad_ready = sem("cpad_ready")
        silu_ready = sem("silu_ready")
        conv4_ready = sem("conv4_ready")
        gdn_dve = sem("gdn_dve")
        gdn_act = sem("gdn_act")
        pe_mark = sem("pe_mark")
        out_done = sem("out_done")

        COL, c0 = {}, 0
        for name, n in (("c", ND), ("b_mod", 48), ("b_in", 48), ("conv_b", ND), ("ln_a_g", ND), ("ln_a_b", ND),
                        ("b_a", ND), ("b_b", ND), ("b_out", ND), ("pool_b", ND), ("pool_scale", ND),
                        ("gdn_conv", 3 * ND * GTAPS), ("conv_w", TAPS * ND)):
            COL[name] = c0
            c0 += n
        assert c0 == BANK
        packs = area[:, 10 * 2048:10 * 2048 + 5 * P].rearrange("p (k n) -> p k n", n=P)
        PACK_ROWS = (128, 40, 96, 128, TAPS * ND - 128)
        b_s_row = area[0:1, 10 * 2048 + 1024:11 * 2048]
        ws_raw, wsT = half(9, 0), half(9, 1)
        mod_row = area[:, 8 * 2048 + 1024:9 * 2048].rearrange("p (r n) -> p r n", n=BANK)
        row8 = area[0:1, 8 * 2048:8 * 2048 + D]

        def col(name, i):
            return cols[:, COL[name] + i:COL[name] + i + 1]

        def rows(v):
            return v.rearrange("(r n) -> r n", n=P)

        H = {}
        for name, (i, j) in dict(qkT=(1, 0), kbg=(1, 1), kT=(6, 0), kbT=(6, 1), qT=(7, 0), DT=(7, 1), AT=(8, 0),
                                 X=(8, 1), XT=(9, 0), T=(9, 1), state=(10, 0), g_row=(10, 1)).items():
            H[name] = half(i, j)
        H["kb"], H["qdT"], H["wT"], H["M"], H["u"], H["o"] = H["qkT"], H["kT"], H["kbT"], H["kbT"], H["T"], H["DT"]

        w3, w6, w7 = a(3), a(6), a(7)
        h2_tok = tok(2)
        xg = w3[:, 0:512].rearrange("p (d s) -> p d s", s=BLK)
        g_min, g_sig, g_act = w3[:, 512:1024], w3[:, 1024:1536], w3[:, 1536:2048]
        u_clip, e_act = w6[:, 0:512], w6[:, 512:1024]
        actT = w6[:, 1024:1536].rearrange("p (j s) -> p j s", s=P)
        y_blk = w6[:, 1536:2048]
        spread = w7[:, 0:256].rearrange("p (t s) -> p t s", s=P)
        spread_T = w7[:, 256:512]
        slots = w7[:, 512:640].rearrange("p (t s) -> p t s", s=BLK)
        xg_o = w7[:, 640:1152].rearrange("p (d s) -> p d s", s=BLK)
        y_blk_o = w7[:, 1152:1664]
        spread_T_o = w7[:, 1664:1920]
        slots_o = w7[:, 1920:2048].rearrange("p (t s) -> p t s", s=BLK)
        spread_o = area[:, 5 * 2048:5 * 2048 + 256].rearrange("p (t s) -> p t s", s=P)
        bgu_raw = a(5)[0:96, :]
        bgu_hi, bgu_res = a(8)[0:96, :], a(6)[0:96, :]
        bgu_parts = a(4)[0:96, 1024:2048].bitcast(BF16)
        bgu_tmp = a(7)[0:96, 0:1024].bitcast(BF16)
        b_dn_sb = area[0:NE, 4 * 2048:4 * 2048 + D]

        R = {n: rt[:, i, :, :] for i, n in enumerate(
            ("logits", "above", "equal", "prefix", "tmp", "sel", "ex", "gates", "pos", "tmp2"))}
        s_ = {n: sm[:, i, :, :] for i, n in enumerate(
            ("b", "al", "abs", "sp", "gl", "beta", "g", "last", "eg", "kd", "ssq", "ssk", "sso", "ea", "t0"))}

        class Steps:

            def __init__(self, sem_, main, over, base):
                self.sem, self.base, self.over_len = sem_, base, len(over)
                self.per = len(main) + (NBLK - 1) * len(over)
                self.main = {n: (NBLK - 1) * len(over) + i + 1 for i, n in enumerate(main)}
                self.over = {n: i + 1 for i, n in enumerate(over)}

            def did(self, eng, where, step):
                e, b = where
                if isinstance(b, int):
                    eng.wait_ge(self.sem, e * self.per + (self.base + self.main[step]))
                else:
                    eng.wait_ge(self.sem, e * self.per + b * self.over_len +
                                (self.base - self.over_len + self.over[step]))

            def started(self, eng, where):
                e, b = where
                if isinstance(b, int):
                    eng.wait_ge(self.sem, e * self.per + (self.base + (NBLK - 1) * self.over_len))
                else:
                    eng.wait_ge(self.sem, e * self.per + b * self.over_len + (self.base - self.over_len))

        PE = Steps(moe_pe, PE_MAIN, PE_OVER, 2)
        DV = Steps(moe_dve, DVE_MAIN, DVE_OVER, 2)
        AC = Steps(moe_act, ACT_MAIN, ACT_OVER, 1)

        def experts(eng, steps, overflow, last_block):
            with eng.Fori(0, NE) as e:
                n_tok = eng.value_load(counts[0:1, bass.ds(e, 1)], min_val=0, max_val=S)
                with eng.Fori(1, NBLK) as b:
                    with eng.If(n_tok - b * BLK > 0):
                        overflow((e, b))
                    with eng.Else():
                        steps.started(eng, (e, b))
                        eng.sem_inc(steps.sem, steps.over_len)
                last_block((e, 0))

        block = ctx.enter_context(nc.Block())

        @block.sync
        def _(sp):
            def load(n):
                s = slot_of(n)
                if n >= PRE + RING:
                    sp.wait_ge(w_used, NU * NE + n - RING + 1)
                elif n >= PRE:
                    sp.wait_ge(w_used, PRE + NU * (NE - 1) + (n - PRE) + 1)
                elif n >= RING:
                    sp.wait_ge(w_used, n - RING + 1)
                sp.dma_start(ring[:, s, :, :], stream[n][1]).then_inc(w_full[s], 16)

            def expert_source(u, e):
                kind, kq, c = EXPERT[u]
                w = A["w_gu"] if kind == "gu" else A["w_dn"]
                w = w[0, bass.ds(e, 1), :, :] if not isinstance(e, int) else w[0, e:e + 1, :, :]
                return w[:, UK * P * kq:UK * P * (kq + 1), BANK * c:BANK * (c + 1)]\
                    .rearrange("o (k p) n -> p (o k) n", p=P)

            for n in range(PRE):
                load(n)
            for u in range(NU):
                if u < RING:
                    sp.wait_ge(w_used, PRE - RING + u + 1)
                elif u == RING:
                    sp.wait_ge(areas_free, 1)
                sp.dma_start(eslot[u], expert_source(u, 0)).then_inc(w_full[u], 16)
            with sp.Fori(1, NE) as e:
                for u in range(NU):
                    sp.wait_ge(w_used, e * NU + (PRE - NU + u + 1))
                    sp.dma_start(eslot[u], expert_source(u, e)).then_inc(w_full[u], 16)
            for n in range(PRE, len(stream)):
                load(n)
            sp.wait_ge(x_ready, 5)
            sp.dma_start(out[0].rearrange("(t p) d -> p t d", p=P), x_tok).then_inc(out_done, 16)
            sp.wait_ge(out_done, 16)

        @block.gpsimd
        def _(pool):
            n = [0]

            def link(ins):
                n[0] += 1
                ins.then_inc(pool_step, 1)
                pool.wait_ge(pool_step, n[0])

            def masked(t, pattern, base, cm, op, fill):
                link(nc.gpsimd.affine_select(out=t, in_=t, compare_op=op, fill=fill, base=base,
                                             pattern=pattern, channel_multiplier=cm))

            link(nc.gpsimd.memset(ident[:, :], 0.0))
            masked(ident[:, :], [[-1, P]], 0, 1, ALU.not_equal, 1.0)
            link(nc.gpsimd.memset(ones[:, :], 1.0))
            link(nc.gpsimd.memset(minus_half[:, :], -0.5))
            nc.gpsimd.memset(apad[:, :, 0:PADC], 0.0).then_inc(consts, 1)
            roots = [0]

            def inverse_root(t):
                roots[0] += 1
                pool.wait_ge(root_asked, roots[0])
                nc.gpsimd.tensor_tensor(t, t, minus_half[:, 0:t.shape[1]], ALU.pow).then_inc(root_given, 1)

            def norm_root():
                inverse_root(rstd[:, :])

            norm_root()
            link(nc.gpsimd.memset(before[:, :], 1.0))
            masked(before[:, :], [[1, P]], 0, -1, ALU.is_gt, 0.0)
            link(nc.gpsimd.memset(upto[:, :], 1.0))
            masked(upto[:, :], [[1, P]], 0, -1, ALU.is_ge, 0.0)
            link(nc.gpsimd.memset(upto[0:KCH, KCH:P], 0.0))
            link(nc.gpsimd.memset(chunk_ones[:, :], 0.0))
            link(nc.gpsimd.memset(chunk_ones[0:KCH, 0:KCH], 1.0))
            link(nc.gpsimd.memset(chunk_ones[KCH:P, KCH:P], 1.0))
            link(nc.gpsimd.tensor_scalar(decay_mask[:, :], upto[:, :], -1.0, 1e30, ALU.add, ALU.mult))
            link(nc.gpsimd.memset(level[:, :, :], 0.0))
            for i in range(6):
                s = 1 << i
                k = P // (2 * s)
                v = level[:, i, :].rearrange("p (k r) -> p k r", r=2 * s)[:, :, s:2 * s]
                link(nc.gpsimd.memset(v, 1.0))
                masked(v, [[-2 * s, k], [0, s]], 0, 1, ALU.is_ge, 0.0)
                masked(v, [[2 * s, k], [0, s]], s - 1, -1, ALU.is_ge, 0.0)
            link(nc.gpsimd.iota(slot_int[:, :], pattern=[[BLK, NBLK], [0, 2], [1, BLK]], base=0,
                                channel_multiplier=0))
            link(nc.gpsimd.tensor_copy(slot_row[:, :, :, :].rearrange("p b r s -> p (b r s)"), slot_int[:, :]))
            link(nc.gpsimd.iota(slot_int[:, 0:16], pattern=[[1, 16]], base=1, channel_multiplier=0))
            link(nc.gpsimd.tensor_copy(inv_pos[:, :], slot_int[:, 0:16]))
            link(nc.gpsimd.memset(zeros[:, :], 0.0))
            link(nc.gpsimd.memset(expert_hot[:, :], 0.0))
            for r in range(3):
                masked(expert_hot[:, 0:NE], [[-1, NE]], -NE * r, 1, ALU.not_equal, 1.0)
            nc.gpsimd.memset(top8[:, :, :], 0.0).then_inc(consts, 1)

            def bc(dst, v):
                pool.dma_start(dst, v.rearrange("(o n) -> o n", o=1).to_broadcast([P, v.shape[0]]))\
                    .then_inc(bc_in, 16)

            norms = [(A["ln_v_g"][0], A["ln_v_b"][0]), (A["post1_g"][0], A["post1_b"][0]),
                     (A["post2_g"][0], A["post2_b"][0])] + \
                    [(A["ln_gain_2"][i, j], A["ln_bias_2"][i, j]) for i in range(2) for j in range(2)]

            def load_norm(i):
                if i:
                    pool.wait_ge(bc_used, i)
                bc(gain_bc[:, :], norms[i][0])
                bc(bias_bc[:, :], norms[i][1])

            late = [0]

            def load(*pairs):
                for dst, src in pairs:
                    late[0] += 16
                    pool.dma_start(dst, src).then_inc(late_in, 16)
                pool.wait_ge(late_in, late[0])

            load_norm(0)
            norm_root()
            load_norm(1)
            norm_root()
            for e in range(4):
                emptied(pool, G("w_b", e))
            load(*[(bgu_raw[NE * r:NE * (r + 1), :], A["b_gu"][0]) for r in range(3)],
                 (b_dn_sb, A["b_dn"][0]))
            norm_root()
            load_norm(2)
            norm_root()
            norm_root()
            for e in range(4):
                emptied(pool, G("moe", e))
            load((a(6).rearrange("p (g k d) -> p g k d", g=4, k=2),
                  A["pool_w_2"][0].rearrange("g (k p) d -> p g k d", p=P)),
                 (alog_bc[:, :], A["gdn_a_log_2"][0:1, :].to_broadcast([P, HEADS])),
                 (dt_bc[:, :], A["gdn_dt_bias_2"][0:1, :].to_broadcast([P, HEADS])),
                 (normw_bc[:, :], A["gdn_norm_w_2"][0:1, :].to_broadcast([P, P])),
                 (w_ba[:, :, :], gdn_in[:, 4 * D:4 * D + 2 * HEADS].rearrange("(k p) n -> p k n", p=P)))
            load_norm(3)
            norm_root()

            def load_ffn(i):
                pool.wait_ge(x_ready, 2 + 2 * i)
                load((tok(7), A["ple_proj_2"][i].rearrange("(k p) n -> p k n", p=P)),
                     (area[:, 8 * 2048:8 * 2048 + 512].rearrange("p (t c) -> p t c", t=NT),
                      A["p_2"][i, 0].rearrange("(t p) c -> p t c", p=P)),
                     (area[0:1, 8 * 2048 + 1024:9 * 2048], A["ple_gate_b_2"][i:i + 1, :]))

            load_ffn(0)
            load_norm(4)
            pool.wait_ge(pool_done, 1)
            cp = apad[:, :, :].rearrange("p m t -> p (m t)")[:, 0:8 * (S + 3)]\
                .rearrange("p (c m t) -> p c m t", c=2, m=4)
            nc.gpsimd.memset(cp[:, :, :, 0:3], 0.0).then_inc(cpad_ready, 1)
            norm_root()
            load_norm(5)
            for n_ in range(NT):
                inverse_root(s_["ssq"][:, n_, :])
                inverse_root(s_["ssk"][:, n_, :])
                inverse_root(s_["sso"][:, n_, :])
            norm_root()
            load_ffn(1)
            load_norm(6)
            norm_root()

        @block.tensor
        def _(pe):
            mm = nc.tensor.matmul
            owed = [False]

            def settle(ins):
                if owed[0]:
                    ins.then_inc(w_used, 1)
                    owed[0] = False

            def transposed(g, pieces):
                claim(pe, g)
                for i, (src, c) in enumerate(pieces):
                    k = src.shape[0]
                    ins = mm(bank(g)[0:src.shape[1], c:c + k], src, ident[0:k, 0:k], is_transpose=True,
                             start=True, stop=True)
                    if i == 0:
                        settle(ins)
                fills(ins, g)

            def unit_ready(n):
                pe.wait_ge(w_full[slot_of(n)], landed_count(n))
                return ring[:, slot_of(n), :, :]

            def feature_major(name, gname, xT, n_slab):
                n0 = first_unit[name]
                for s in range(n_slab):
                    u = [unit_ready(n0 + 2 * s), unit_ready(n0 + 2 * s + 1)]
                    for q in range(2):
                        g = G(gname, 2 * s + q)
                        claim(pe, g)
                        for m in range(2):
                            for k in range(ND):
                                c = (2 * q + m) * P
                                ins = mm(bank(g)[:, m * S:(m + 1) * S], u[k // UK][:, k % UK, c:c + P],
                                         xT[:, k, :], start=k == 0, stop=k == ND - 1)
                                settle(ins)
                                if q == 1 and m == 1 and k == UK - 1:
                                    ins.then_inc(w_used, 1)
                        fills(ins, g)
                    owed[0] = True

            def token_major(name, gname, lhs, n_slab, bias=None):
                n0 = first_unit[name]
                for s in range(n_slab):
                    u = [unit_ready(n0 + 2 * s), unit_ready(n0 + 2 * s + 1)]
                    for t in range(NT):
                        g = G(gname, NT * s + t)
                        claim(pe, g)
                        if bias is not None:
                            mm(bank(g)[:, :], ones[0:1, :], bias[0:1, BANK * s:BANK * (s + 1)],
                               start=True, stop=False)
                        for k in range(ND):
                            ins = mm(bank(g)[:, :], lhs(k, t), u[k // UK][:, k % UK, :],
                                     start=k == 0 and bias is None, stop=k == ND - 1)
                            settle(ins)
                            if t == NT - 1 and k == UK - 1:
                                ins.then_inc(w_used, 1)
                        fills(ins, g)
                    owed[0] = True

            def tokens_of(xT):
                return lambda k, t: xT[:, k, t * P:(t + 1) * P]

            def to_features(gname, src, first=True):
                for q in range(4):
                    transposed(G(gname, q), [(src[:, t, (2 * q + m) * P:(2 * q + m + 1) * P], m * S + t * P)
                                             for m in range(2) for t in range(NT)])

            def to_tokens(gname, src, wait=None):
                for hf in range(NH):
                    for t in range(NT):
                        if wait:
                            wait(hf)
                        transposed(G(gname, NT * hf + t),
                                   [(src[:, 4 * hf + m, t * P:(t + 1) * P], m * P) for m in range(4)])

            pe.wait_ge(consts, 1)
            pe.wait_ge(packs_in, 16 * 14)
            g = G("cols")
            claim(pe, g)
            c = 0
            for i, r in enumerate(PACK_ROWS):
                ins = mm(bank(g)[:, c:c + r], packs[0:r, i, :], ident[0:r, 0:r], is_transpose=True,
                         start=True, stop=True)
                c += r
            fills(ins, g)
            pe.wait_ge(ws_in, 16)
            for q in range(2):
                transposed(G("wsT", q), [(ws_raw[:, 4 * q + i, :], i * P) for i in range(4)])

            def modulation(name, rounds):
                for r in range(rounds):
                    g = G(name, r)
                    claim(pe, g)
                    for kq in range(2):
                        n0 = first_unit[name] + 8 * r + 4 * kq
                        u = [unit_ready(n0 + j) for j in range(4)]
                        for k in range(UK):
                            for j in range(4):
                                ins = mm(bank(g)[32 * j:32 * j + 32, :], cond[:, UK * kq + k, :], u[j][:, k, :],
                                         start=kq == 0 and k == 0, stop=kq == 1 and k == UK - 1)
                                settle(ins)
                                if k == UK - 1 and not (kq == 1 and j == 3):
                                    ins.then_inc(w_used, 1)
                    fills(ins, g)
                    owed[0] = True
                for r in range(rounds):
                    emptied(pe, G(name, r))
                    transposed(G(name + "T", r), [(mod_row[:, r, i * P:(i + 1) * P], i * P) for i in range(4)])

            pe.wait_ge(cond_ready, 1)
            modulation("mod1", 1)
            pe.wait_ge(xn_ready, 1)
            to_features("hT", tok(2))
            hT = feat(1)
            for q in range(4):
                emptied(pe, G("hT", q))
            feature_major("a_gate", "a_gate", hT, C)
            feature_major("a_val", "a_val", hT, C)
            pe.wait_ge(rows_in, 64)
            token_major("v", "v", tokens_of(hT), C, bias=row8)
            feature_major("u", "u", hT, C)
            feature_major("g_a", "g_a", hT, C)
            feature_major("g_b", "g_b", hT, C)
            modulation("mod2", 2)
            pe.wait_ge(conv_ready, 1)
            to_tokens("convT", feat(3))
            pe.wait_ge(v_ready, 1)
            pe.wait_ge(wsT_ready, 1)
            vt = tok(4)
            for q in range(4):
                g = G("mix", q)
                claim(pe, g)
                for m in range(2):
                    gr = 2 * q + m
                    for t in range(NT):
                        o = bank(g)[:, m * S + t * P:m * S + (t + 1) * P]
                        mm(o, ones[0:1, :], b_s_row[0:1, gr * P:(gr + 1) * P], start=True, stop=False)
                        ins = mm(o, vt[:, t, gr * P:(gr + 1) * P], wsT[:, gr, :], start=False, stop=True)
                fills(ins, g)
            for q in range(4):
                emptied(pe, G("mix", q))
            feature_major("w_b", "w_b", feat(5), C)
            pe.wait_ge(xn_ready, 2)
            to_features("yaT", tok(8))
            for q in range(4):
                emptied(pe, G("yaT", q))
            feature_major("w_a", "w_a", feat(2), C)
            pe.wait_ge(m_ready, 4)
            feature_major("w_out", "w_out", feat(6), C)
            to_tokens("y_tok", feat(7), wait=lambda hf: (emptied(pe, G("w_out", 2 * hf)),
                                                         emptied(pe, G("w_out", 2 * hf + 1))))
            pe.wait_ge(xn_ready, 3)
            to_features("h2T", tok(3))
            for q in range(4):
                emptied(pe, G("h2T", q))
            h2T = feat(1)
            pe.wait_ge(rows_in, 64)
            g = G("router")
            claim(pe, g)
            for t in range(NT):
                for k in range(ND):
                    ins = mm(bank(g)[:, t * NE:(t + 1) * NE], h2T[:, k, t * P:(t + 1) * P], w_router[:, k, :],
                             start=k == 0, stop=k == ND - 1)
            fills(ins, g)
            to_tokens("h2_tok", h2T)
            pe.wait_ge(route_ready, 1)
            g = G("pos")
            claim(pe, g)
            sel = R["sel"]
            mm(bank(g)[:, 0:NE], before[:, :], sel[:, 0, :], start=True, stop=True)
            mm(bank(g)[:, NE:2 * NE], before[:, :], sel[:, 1, :], start=True, stop=False)
            mm(bank(g)[:, NE:2 * NE], ones[:, :], sel[:, 0, :], start=False, stop=True)
            mm(bank(g)[0:1, 2 * NE:3 * NE], ones[:, 0:1], sel[:, 0, :], start=True, stop=False)
            ins = mm(bank(g)[0:1, 2 * NE:3 * NE], ones[:, 0:1], sel[:, 1, :], start=False, stop=True)
            fills(ins, g)
            pe.wait_ge(route_ready, 2)
            transposed(G("gateT"), [(R["gates"][:, t, :], t * P) for t in range(NT)])

            emptied(pe, G("gateT"))
            pe.wait_ge(route_ready, 3)
            pe.wait_ge(bgu_ready, 1)
            for q in range(4):
                emptied(pe, G("h2_tok", q))
            emptied(pe, G("pos"))
            for i in range(4):
                ins = mm(banks[i][:, :], zeros[0:96, :], bgu_parts[:, 0:BANK], start=True, stop=False)
            ins.then_inc(moe_pe, 1)
            bX, bG, bU, bT = banks[4], banks[5], banks[6], banks[7]

            def step(ins):
                ins.then_inc(moe_pe, 1)

            def gather(s_):
                for d in range(ND):
                    for t in range(NT):
                        ins = mm(bX[:, d * BLK:(d + 1) * BLK], h2_tok[:, t, d * P:(d + 1) * P], s_[:, t, :],
                                 start=t == 0, stop=t == NT - 1)
                        if d == 0 and t == 0:
                            first = ins
                step(ins)
                return first

            def gate_or_up(e, bk, u0, part, x, last):
                for hf in range(2):
                    ins = mm(bk[hf * BLK:(hf + 1) * BLK, :], expert_sel[:, :],
                             bgu_parts[:, (2 * part + hf) * BANK:(2 * part + hf + 1) * BANK],
                             start=True, stop=False)
                for kt in range(ND):
                    for hf in range(2):
                        u = u0 + 2 * (kt // UK) + hf
                        if kt % UK == 0:
                            weights(e, u)
                        ins = mm(bk[hf * BLK:(hf + 1) * BLK, :], x[:, kt, :], eslot[u][:, kt % UK, :],
                                 start=False, stop=kt == ND - 1)
                        if kt == ND - 1 and hf == 1:
                            step(ins)
                        elif kt % UK == UK - 1 and last:
                            ins.then_inc(w_used, 1)

            def weights(e, u):
                pe.wait_ge(w_full[u], e * 16 + (16 * (PRE // RING if u < RING else 0) + 16))

            def activation_T(w, i, bk):
                DV.did(pe, w, f"act{i}")
                for j in range(2):
                    ins = mm(bk[:, j * P:(j + 1) * P], e_act[:, (2 * i + j) * P:(2 * i + j + 1) * P],
                             ident[:, :], is_transpose=True, start=True, stop=True)
                step(ins)

            def spread_transposed(w, src):
                DV.did(pe, w, "spread1")
                for t in range(NT):
                    ins = mm(bX[:, t * P:(t + 1) * P], src[:, t, :], ident[:, :], is_transpose=True,
                             start=True, stop=True)
                step(ins)

            def down(w, last):
                for n, kt in enumerate((0, 1, 4, 5, 2, 3, 6, 7)):
                    if n % 4 == 0:
                        DV.did(pe, w, f"act_T{n // 4}")
                    for hf in range(2):
                        u = 8 + 2 * (kt // UK) + hf
                        if kt % UK == 0:
                            weights(w[0], u)
                        j, fh = kt % UK, kt // UK
                        ins = mm(bT[hf * BLK:(hf + 1) * BLK, :], actT[:, j, fh * BLK:(fh + 1) * BLK],
                                 eslot[u][:, kt % UK, :], start=n == 0, stop=n == ND - 1)
                        if kt in (3, 7) and last:
                            ins.then_inc(w_used, 1)
                        elif n == ND - 1 and hf == 1:
                            step(ins)

            def scatter(st, y):
                for t in range(NT):
                    for hf in range(2):
                        ins = mm(banks[2 * t + hf][:, :], st[hf * BLK:(hf + 1) * BLK, t * P:(t + 1) * P],
                                 y[hf * BLK:(hf + 1) * BLK, :], start=False, stop=False)
                        if t == 0 and hf == 0:
                            first = ins
                step(ins)
                return first

            pe.wait_ge(moe_dve, 1)
            gather(slots)

            def overflow(w):
                DV.did(pe, w, "slots1")
                AC.started(pe, w)
                gather(slots_o)
                DV.did(pe, w, "tokens")
                gate_or_up(w[0], bG, 0, 0, xg_o, False)
                gate_or_up(w[0], bU, 4, 1, xg_o, False)
                spread_transposed(w, spread_o)
                activation_T(w, 0, bG)
                activation_T(w, 1, bU)
                down(w, False)
                AC.did(pe, w, "down")
                scatter(spread_T_o, y_blk_o)

            def last_block(w):
                e = w[0]
                DV.started(pe, w)
                gate_or_up(e, bG, 0, 0, xg, True)
                AC.started(pe, w)
                scatter(spread_T, y_blk).then_inc(w_used, 1)
                gate_or_up(e, bU, 4, 1, xg, True)
                DV.did(pe, w, "next_slots1")
                gather(slots).then_inc(w_used, 1)
                activation_T(w, 0, bG)
                activation_T(w, 1, bU)
                DV.did(pe, w, "next_tokens")
                spread_transposed(w, spread)
                down(w, True)

            experts(pe, PE, overflow, last_block)
            pe.wait_ge(moe_act, AC.base + NE * AC.per)
            scatter(spread_T, y_blk)
            for t in range(NT):
                for hf in range(NH):
                    g = G("moe", 2 * t + hf)
                    ins = mm(bank(g)[:, :], gateT[:, t * P:(t + 1) * P], b_dn_sb[:, hf * BANK:(hf + 1) * BANK],
                             start=False, stop=True)
                    fills(ins, g)

            pe.wait_ge(diag_ready, 1)
            diag = half(5, 0)
            for q in range(2):
                g = G("g2_bc", q)
                claim(pe, g)
                for i in range(4):
                    ins = mm(bank(g)[:, i * P:(i + 1) * P], ones[:, :], diag[:, 4 * q + i, :], start=True, stop=True)
                fills(ins, g)
            pe.wait_ge(x_ready, 1)
            to_features("x2T", x_tok)
            pe.wait_ge(pooled_ready, 1)
            pe.wait_ge(late_in, 144)
            pw = a(6).rearrange("p (g k d) -> p g k d", g=4, k=2)
            pooled = feat(8)
            for gi in range(4):
                g = G("pool", gi)
                claim(pe, g)
                for m in range(2):
                    for k in range(2):
                        ins = mm(bank(g)[:, m * S:(m + 1) * S], pw[:, gi, k, m * P:(m + 1) * P],
                                 pooled[:, 2 * gi + k, :], start=k == 0, stop=k == 1)
                fills(ins, g)
            for gi in range(4):
                emptied(pe, G("pool", gi))
            to_tokens("pool_tok", feat(7))

            def ffn(i):
                pe.wait_ge(x_ready, 2 + 2 * i)
                to_features(f"xT_{i}", x_tok)
                pe.wait_ge(late_in, 192 + 48 * i)
                pt = area[:, 8 * 2048:8 * 2048 + 512].rearrange("p (t c) -> p t c", t=NT)
                transposed(G(f"pT_{i}"), [(pt[:, t, m * P:(m + 1) * P], m * S + t * P)
                                          for m in range(2) for t in range(NT)])
                for q in range(4):
                    emptied(pe, G(f"xT_{i}", q))
                xT = feat(1)
                gb = area[0:1, 8 * 2048 + 1024:9 * 2048]
                token_major(f"gate{i}", f"gate_{i}", tokens_of(xT), C, bias=gb)
                emptied(pe, G(f"pT_{i}"))
                pT = area[:, 8 * 2048 + 512:8 * 2048 + 1024].rearrange("p (m t) -> p m t", m=2)
                proj = tok(7)
                for s in range(NH):
                    for t in range(NT):
                        g = G(f"proj_{i}", NT * s + t)
                        claim(pe, g)
                        for k in range(2):
                            ins = mm(bank(g)[:, :], pT[:, k, t * P:(t + 1) * P],
                                     proj[:, k, s * BANK:(s + 1) * BANK], start=k == 0, stop=k == 1)
                        fills(ins, g)
                feature_major(f"w1_{i}", f"w1_{i}", xT, DFF // BANK)
                n0 = first_unit[f"w2_{i}"]
                KQ = DFF // (UK * P)
                for j in range(4):
                    claim(pe, G(f"w2_{i}", j))
                for kq in range(KQ):
                    pe.wait_ge(hid_ready, 2 * (DFF // BANK * i + kq + 1))
                    for c in range(C):
                        u = unit_ready(n0 + C * kq + c)
                        for t in range(NT):
                            g = G(f"w2_{i}", NT * c + t)
                            for k in range(UK):
                                f = UK * kq + k
                                hid = feat(2 + f // 8)[:, f % 8, t * P:(t + 1) * P]
                                ins = mm(bank(g)[:, :], hid, u[:, k, :], start=kq == 0 and k == 0,
                                         stop=kq == KQ - 1 and k == UK - 1)
                                settle(ins)
                            if kq == KQ - 1:
                                fills(ins, g)
                            elif t == NT - 1:
                                ins.then_inc(w_used, 1)
                        if kq == KQ - 1:
                            owed[0] = True

            ffn(0)

            pe.wait_ge(x_ready, 3)
            to_features("x4T", x_tok)
            for q in range(4):
                emptied(pe, G("x4T", q))
            xT = feat(1)
            sl = [half(6, j).rearrange("p (m u) d -> p m (u d)", m=4) for j in range(2)]

            def qkv_T(s):
                pe.wait_ge(silu_ready, s + 1)
                for t in range(NT):
                    transposed(G(f"qkvT{s}", t), [(sl[s % 2][:, m, t * P:(t + 1) * P], m * P) for m in range(4)])

            n0 = first_unit["qkv"]
            for s in range(6):
                first_unit[f"qkv{s}"] = n0 + 2 * s
                feature_major(f"qkv{s}", f"qkv{s}", xT, 1)
                if s:
                    qkv_T(s - 1)
            token_major("z", "z", tokens_of(xT), C)
            g = G("ba")
            claim(pe, g)
            pe.wait_ge(late_in, 144)
            for t in range(NT):
                for k in range(ND):
                    ins = mm(bank(g)[:, t * 2 * HEADS:(t + 1) * 2 * HEADS], xT[:, k, t * P:(t + 1) * P],
                             w_ba[:, k, :], start=k == 0, stop=k == ND - 1)
            fills(ins, g)
            qkv_T(5)
            kk, qq = tok(3), tok(2)
            ev = [0]

            def dve_step_ready():
                ev[0] += 1
                pe.wait_ge(gdn_dve, ev[0])

            def heads(name, fn, qs=(0, 1), at=0, ready=None):
                for q in qs:
                    g = G(name, at + q)
                    if ready:
                        ready(q)
                    claim(pe, g)
                    for i in range(4):
                        ins = fn(bank(g), i, 4 * q + i)
                        settle(ins) if i == 0 else None
                    fills(ins, g)

            def product(l, r):
                return lambda bk, i, h: mm(bk[:, i * P:(i + 1) * P], l[:, h, :], r[:, h, :], start=True, stop=True)

            def tr(src):
                return lambda bk, i, h: mm(bk[:, i * P:(i + 1) * P], src(h), ident[:, :], is_transpose=True,
                                           start=True, stop=True)

            def both_emptied(name):
                for q in range(2):
                    emptied(pe, G(name, q))

            for n in range(NT):
                dve_step_ready()
                g = G(f"g_col.{n}")
                claim(pe, g)
                mm(bank(g)[:, 0:HEADS], upto[:, :], s_["gl"][:, n, :], start=True, stop=True)
                ins = mm(bank(g)[:, HEADS:2 * HEADS], chunk_ones[:, :], s_["gl"][:, n, :], start=True, stop=True)
                fills(ins, g)
                heads(f"g_row.{n}", lambda bk, i, h: mm(bk[:, i * P:(i + 1) * P], H["M"][:, h, :], upto[:, :],
                                                        start=True, stop=True))
                dve_step_ready()
                heads(f"kT.{n}", tr(lambda h: kk[:, n, h * P:(h + 1) * P]))
                heads(f"qT.{n}", tr(lambda h: qq[:, n, h * P:(h + 1) * P]))
                both_emptied(f"g_row.{n}")
                heads(f"kbT.{n}", tr(lambda h: H["kb"][:, h, :]))
                both_emptied(f"kT.{n}")
                both_emptied(f"kbT.{n}")
                heads(f"AT.{n}", product(H["kT"], H["kbT"]))
                both_emptied(f"qT.{n}")
                heads(f"qkT.{n}", product(H["kT"], H["qT"]))
                dve_step_ready()
                heads(f"X1.{n}", tr(lambda h: H["XT"][:, h, :]))
                for s in range(1, 6):
                    dve_step_ready()
                    heads(f"T{s}.{n}", product(H["M"], H["X"]),
                          ready=lambda q: emptied(pe, G(f"X1.{n}", q) if s == 1 else G(f"XX{s - 1}.{n}", 2 * q)))
                    for q in range(2):
                        emptied(pe, G(f"T{s}.{n}", q))
                        if s < 5:
                            if s > 1:
                                emptied(pe, G(f"XX{s - 1}.{n}", 2 * q + 1))
                            heads(f"XX{s}.{n}", product(H["XT"], H["T"]), (q,), at=q)
                            heads(f"XX{s}.{n}", product(H["T"], H["XT"]), (q,), at=q + 1)
                        else:
                            emptied(pe, G(f"XX{s - 1}.{n}", 2 * q + 1))
                            heads(f"XX{s}.{n}", product(H["T"], H["XT"]), (q,))
                dve_step_ready()
                vb = tok(4)[:, n, :].rearrange("p (h d) -> p h d", d=P)
                kd = tok(3)[:, n, :].rearrange("p (h d) -> p h d", d=P)
                heads(f"u.{n}", product(H["XT"], vb))
                heads(f"wT.{n}", product(H["kbg"], H["XT"]))
                both_emptied(f"u.{n}")
                both_emptied(f"wT.{n}")
                for c in range(2):
                    r = slice(c * KCH, (c + 1) * KCH)
                    first = 2 * n + c == 0
                    if not first:
                        dve_step_ready()
                        heads(f"wS.{n}.{c}", lambda bk, i, h: mm(
                            bk[r, i * P:(i + 1) * P], H["wT"][:, h, r], H["state"][:, h, :], start=True, stop=True))
                        both_emptied(f"wS.{n}.{c}")

                    def o_of(bk, i, h):
                        if not first:
                            mm(bk[r, i * P:(i + 1) * P], H["qdT"][:, h, r], H["state"][:, h, :],
                               start=True, stop=False)
                        return mm(bk[r, i * P:(i + 1) * P], H["qkT"][r, h, r], H["u"][r, h, :],
                                  start=first, stop=True)

                    if 2 * n + c < 3:
                        heads(f"S.{n}.{c}", lambda bk, i, h: mm(
                            bk[:, i * P:(i + 1) * P], kd[r, h, :], H["u"][r, h, :], start=True, stop=True))
                    heads(f"o.{n}.{c}", o_of)
                dve_step_ready()
                heads(f"oT.{n}", tr(lambda h: H["o"][:, h, :]))
            for n in range(NT):
                both_emptied(f"oT.{n}")
            oT = tok(2)
            token_major("gdn_out", "gdn_out", lambda k, t: oT[:, t, k * P:(k + 1) * P], C)
            ffn(1)

        @block.scalar
        def _(act):
            f = nc.scalar.activation
            n = [0]

            def link(ins):
                n[0] += 1
                ins.then_inc(act_step, 1)
                act.wait_ge(act_step, n[0])

            def load(dst, src, s):
                act.dma_start(dst, src).then_inc(s, 16)

            load(x_tok, A["x"][0].rearrange("(t p) d -> p t d", p=P), x_in)
            r = 0
            for v in (A["c"][0], A["b_mod"][0], A["b_in"][0], A["conv_b"][0], A["ln_a_g"][0], A["ln_a_b"][0]):
                k = v.shape[0] // P
                load(packs[r:r + k, 0, :], rows(v), packs_in)
                r += k
            r = 0
            for v in (A["b_a"][0], A["b_b"][0], A["b_out"][0],
                      A["pool_b_2"][0].rearrange("g d -> (g d)"), A["pool_scale_2"][0]):
                load(packs[r:r + ND, 1, :], rows(v), packs_in)
                r += ND
            load(packs[0:96, 2, :], A["gdn_conv_2"][0].rearrange("j (m n) -> (j m) n", n=P), packs_in)
            cw = A["conv_w"][0].rearrange("j (m n) -> (j m) n", n=P)
            load(packs[0:P, 3, :], cw[0:P, :], packs_in)
            load(packs[0:PACK_ROWS[4], 4, :], cw[P:TAPS * ND, :], packs_in)
            load(ws_raw, A["w_s"][0].rearrange("g i j -> i g j"), ws_in)
            load(row8, A["b_in"][0:1, 3 * D:4 * D], rows_in)
            load(b_s_row, A["b_s"][0].rearrange("(o g) i -> o (g i)", o=1), rows_in)
            load(w_router[:, :, :], A["w_router"][0].rearrange("(k p) e -> p k e", p=P), rows_in)
            load(router_bc[:, :], A["b_router"][0:1, :].to_broadcast([P, NE]), rows_in)

            emptied(act, G("cols"))
            f(cond[:, :, :], cols[:, COL["c"]:COL["c"] + ND].unsqueeze(2).to_broadcast([P, ND, 32]), ACT.Silu)\
                .then_inc(cond_ready, 1)
            g = G("mod1")
            full(act, g)
            empties(f(mod_row[:, 0, :], bank(g)[:, :], ACT.Copy), g)

            def pairs(gname, fn):
                for q in range(4):
                    g = G(gname, q)
                    full(act, g)
                    for m in range(2):
                        ins = fn(2 * q + m, bank(g)[:, m * S:(m + 1) * S])
                    empties(ins, g)

            act.wait_ge(mod1_ready, 1)
            pairs("hT", lambda m, ps: f(feat(1)[:, m, :], ps, ACT.Identity, bias=modc[:, m:m + 1],
                                        scale=sc1p[:, m:m + 1]))
            pairs("a_gate", lambda m, ps: f(feat(3)[:, m, :], ps, ACT.Sigmoid, bias=col("b_in", ND + m)))
            for s in range(C):
                for t in range(NT):
                    g = G("v", NT * s + t)
                    full(act, g)
                    empties(f(tok(4)[:, t, s * BANK:(s + 1) * BANK], bank(g)[:, :], ACT.Gelu), g)
            pairs("u", lambda m, ps: f(feat(5)[:, m, :], ps, ACT.Gelu, bias=col("b_in", 2 * ND + m)))
            pairs("g_a", lambda m, ps: f(feat(6)[:, m, :], ps, ACT.Sigmoid, bias=col("b_in", 4 * ND + m)))
            pairs("g_b", lambda m, ps: f(feat(7)[:, m, :], ps, ACT.Sigmoid, bias=col("b_in", 5 * ND + m)))
            for r in range(2):
                g = G("mod2", r)
                full(act, g)
                empties(f(mod_row[:, r, :], bank(g)[:, :], ACT.Copy), g)
            for hf in range(NH):
                for t in range(NT):
                    g = G("convT", NT * hf + t)
                    full(act, g)
                    empties(f(tok(8)[:, t, hf * BANK:(hf + 1) * BANK], bank(g)[:, :], ACT.Copy), g)
            pairs("yaT", lambda m, ps: f(feat(2)[:, m, :], ps, ACT.Silu, bias=col("ln_a_b", m),
                                         scale=col("ln_a_g", m)))
            act.wait_ge(mod2_ready, 1)
            pairs("h2T", lambda m, ps: f(feat(1)[:, m, :], ps, ACT.Identity, bias=modc[:, 24 + m:25 + m],
                                         scale=sc2p[:, m:m + 1]))
            for hf in range(NH):
                for t in range(NT):
                    g = G("h2_tok", NT * hf + t)
                    full(act, g)
                    empties(f(h2_tok[:, t, hf * BANK:(hf + 1) * BANK], bank(g)[:, :], ACT.Copy), g)
            act.wait_ge(route_ready, 1)
            for t in range(NT):
                ins = f(R["ex"][:, t, :], R["tmp"][:, t, :], ACT.Exp)
            ins.then_inc(moe_act, 1)

            def act_block(w, st, y):
                DV.did(act, w, "gate_min")
                f(g_sig, g_min, ACT.Sigmoid, scale=SWIGLU).then_inc(moe_act, 1)
                PE.did(act, w, "spread_T")
                f(st, banks[4][:, 0:S], ACT.Copy).then_inc(moe_act, 1)
                if isinstance(w[1], int):
                    act.wait_ge(w_used, w[0] * NU + (PRE + NU))
                else:
                    PE.did(act, w, "down")
                f(y, banks[7][:, :], ACT.Copy).then_inc(moe_act, 1)

            act.wait_ge(route_ready, 3)
            experts(act, AC, lambda w: act_block(w, spread_T_o, y_blk_o), lambda w: act_block(w, spread_T, y_blk))

            for q in range(4):
                g = G("x2T", q)
                full(act, g)
                empties(f(apad[:, 2 * q:2 * q + 2, PADC:PADC + S],
                          bank(g)[:, :].rearrange("p (m t) -> p m t", m=2), ACT.Copy), g)

            def copy_T(gname, dst):
                for q in range(4):
                    g = G(gname, q)
                    full(act, g)
                    empties(f(dst[:, 2 * q:2 * q + 2, :], bank(g)[:, :].rearrange("p (m t) -> p m t", m=2),
                              ACT.Copy), g)

            def ffn(i):
                copy_T(f"xT_{i}", feat(1))
                g = G(f"pT_{i}")
                full(act, g)
                empties(f(area[:, 8 * 2048 + 512:8 * 2048 + 1024], bank(g)[:, :], ACT.Copy), g)
                for s in range(NH):
                    for t in range(NT):
                        g = G(f"gate_{i}", NT * s + t)
                        full(act, g)
                        empties(f(tok(6)[:, t, s * BANK:(s + 1) * BANK], bank(g)[:, :], ACT.Sigmoid), g)
                for q in range(2 * DFF // BANK):
                    g = G(f"w1_{i}", q)
                    full(act, g)
                    empties(f(area[:, 2 * 2048 + q * BANK:2 * 2048 + (q + 1) * BANK], bank(g)[:, :], ACT.Relu), g)

            ffn(0)
            copy_T("x4T", feat(1))
            cp = apad[:, :, :].rearrange("p m t -> p (m t)")[:, 0:8 * (S + 3)]\
                .rearrange("p (c m t) -> p c m t", c=2, m=4)
            sl = [half(6, j).rearrange("p (m u) d -> p m (u d)", m=4) for j in range(2)]
            act.wait_ge(cpad_ready, 1)

            def silu(s):
                act.wait_ge(conv4_ready, s + 1)
                f(sl[s % 2], sl[s % 2], ACT.Silu).then_inc(silu_ready, 1)

            for s in range(6):
                if s >= 2:
                    act.wait_ge(conv4_ready, s - 1)
                for q in range(2):
                    g = G(f"qkv{s}", q)
                    full(act, g)
                    empties(f(cp[:, s % 2, 2 * q:2 * q + 2, 3:3 + S],
                              bank(g)[:, :].rearrange("p (m t) -> p m t", m=2), ACT.Copy), g)
                if s:
                    silu(s - 1)
            silu(5)
            for s in range(NH):
                for t in range(NT):
                    g = G("z", NT * s + t)
                    full(act, g)
                    empties(f(tok(5)[:, t, s * BANK:(s + 1) * BANK], bank(g)[:, :], ACT.Silu), g)
            act.wait_ge(gdn_act, 1)
            link(f(s_["beta"], s_["b"], ACT.Sigmoid))
            link(f(s_["abs"], s_["abs"], ACT.Exp, scale=-1.0))
            link(f(s_["ea"][:, 0, :], alog_bc[:, :], ACT.Exp))
            f(s_["sp"], s_["abs"], ACT.Ln, bias=1.0).then_inc(gdn_act, 1)
            ev = [2]

            def dve_gave():
                ev[0] += 1
                act.wait_ge(gdn_act, ev[0])

            def copy_heads(name, dst):
                for q in range(2):
                    g = G(name, q)
                    full(act, g)
                    empties(f(dst[:, 4 * q:4 * q + 4, :],
                              bank(g)[:, :].rearrange("p (h d) -> p h d", d=P), ACT.Copy), g)

            for n_ in range(NT):
                dve_gave()
                link(f(s_["eg"][:, n_, :], s_["g"][:, n_, :], ACT.Exp))
                f(s_["kd"][:, n_, :], s_["kd"][:, n_, :], ACT.Exp).then_inc(gdn_act, 1)
                ev[0] += 1
                dve_gave()
                link(f(H["DT"], H["DT"], ACT.Exp))
                f(H["g_row"], H["g_row"], ACT.Exp).then_inc(gdn_act, 1)
                ev[0] += 1
                copy_heads(f"kT.{n_}", H["kT"])
                copy_heads(f"qT.{n_}", H["qT"])
                copy_heads(f"kbT.{n_}", H["kbT"])
                copy_heads(f"X1.{n_}", H["X"])
                for s in range(1, 6):
                    copy_heads(f"T{s}.{n_}", H["T"])
                copy_heads(f"u.{n_}", H["u"])
                copy_heads(f"wT.{n_}", H["wT"])
                for c in range(2):
                    r = slice(c * KCH, (c + 1) * KCH)
                    for q in range(2):
                        g = G(f"o.{n_}.{c}", q)
                        full(act, g)
                        empties(f(H["o"][r, 4 * q:4 * q + 4, :],
                                  bank(g)[r, :].rearrange("p (h d) -> p h d", d=P), ACT.Copy), g)
                copy_heads(f"oT.{n_}", tok(2)[:, n_, :].rearrange("p (h d) -> p h d", d=P))
            ffn(1)

        @block.vector
        def _(dve):
            v = nc.vector
            n = [0]

            def link(ins):
                n[0] += 1
                ins.then_inc(dve_step, 1)
                dve.wait_ge(dve_step, n[0])

            roots = [0]

            def inverse_root():
                roots[0] += 1
                dve.sem_inc(root_asked, 1)
                dve.wait_ge(root_given, roots[0])

            def moments(src):
                for t in range(NT):
                    for hf in range(NH):
                        link(v.bn_stats(stats[:, t, hf, :], src[:, t, hf * BANK:(hf + 1) * BANK]))
                for t in range(NT):
                    link(v.bn_aggr(mv[:, t, :], stats[:, t, :, :].rearrange("p a b -> p (a b)")))
                link(v.tensor_scalar(rstd[:, :], mv[:, :, 1], EPS, None, ALU.add))
                inverse_root()

            def normalised(dst, src, t):
                return v.tensor_scalar(dst[:, t, :], src[:, t, :], mv[:, t, 0:1], rstd[:, t:t + 1],
                                       ALU.subtract, ALU.mult)

            norm = [0]

            def layer_norm(x, done):
                norm[0] += 1
                moments(x)
                for t in range(NT):
                    link(normalised(x, x, t))
                dve.wait_ge(bc_in, 32 * norm[0])
                for t in range(NT):
                    link(v.tensor_tensor(x[:, t, :], x[:, t, :], gain_bc[:, :], ALU.mult))
                for t in range(NT):
                    link(v.tensor_tensor(x[:, t, :], x[:, t, :], bias_bc[:, :], ALU.add))
                done()

            def tick(s, k=1):
                dve.sem_inc(s, k)

            g = G("cols")
            full(dve, g)
            empties(v.tensor_copy(cols[:, :], bank(g)[:, :]), g)
            for q in range(2):
                g = G("wsT", q)
                full(dve, g)
                empties(v.tensor_copy(wsT[:, 4 * q:4 * q + 4, :],
                                      bank(g)[:, :].rearrange("p (h d) -> p h d", d=P)), g)
                emptied(dve, g)
            v.memset(wsT[KCH:P, :, 0:KCH], 0.0).then_inc(wsT_ready, 1)
            dve.wait_ge(x_in, 16)
            moments(x_tok)
            for t in range(NT):
                link(normalised(tok(2), x_tok, t))
            tick(xn_ready)
            emptied(dve, G("cols"))
            def mod_columns(g, r):
                full(dve, g)
                c = slice(16 * r, 16 * r + 16)
                empties(v.tensor_tensor(modc[:, c].rearrange("p (j i) -> p j i", i=4),
                                        bank(g)[:, :].rearrange("p (i j r) -> p j i r", i=4, r=32)[:, :, :, 0],
                                        cols[:, COL["b_mod"]:COL["b_mod"] + 48][:, c]
                                        .rearrange("p (j i) -> p j i", i=4), ALU.add), g)
                emptied(dve, g)

            mod_columns(G("mod1T"), 0)
            v.tensor_scalar(sc1p[:, :], modc[:, 8:16], 1.0, None, ALU.add).then_inc(mod1_ready, 1)
            dve.wait_ge(consts, 1)
            for q in range(4):
                emptied(dve, G("a_gate", q))
            for q in range(4):
                g = G("a_val", q)
                full(dve, g)
                for m in range(2):
                    ins = v.scalar_tensor_tensor(apad[:, 2 * q + m, PADC:PADC + S], bank(g)[:, m * S:(m + 1) * S],
                                                 col("b_in", 2 * q + m), feat(3)[:, 2 * q + m, :], ALU.add, ALU.mult)
                    if m == 0:
                        link(ins)
                empties(ins, g)
                emptied(dve, g)
            acc = feat(3)
            for m in range(ND):
                v.tensor_scalar(acc[:, m, :], apad[:, m, 0:S], col("conv_w", m), col("conv_b", m),
                                ALU.mult, ALU.add).then_inc(conv_step, 1)
            with dve.Fori(1, TAPS) as j:
                for m in range(ND):
                    dve.wait_ge(conv_step, j * ND + (m + 1 - ND))
                    v.scalar_tensor_tensor(acc[:, m, :], apad[:, m, bass.ds(j, S)],
                                           cols[:, bass.ds(j * ND + (COL["conv_w"] + m), 1)], acc[:, m, :],
                                           ALU.mult, ALU.add).then_inc(conv_step, 1)
            dve.wait_ge(conv_step, TAPS * ND)
            tick(conv_ready)
            for q in range(4):
                emptied(dve, G("v", q))
            layer_norm(tok(4), lambda: (tick(v_ready), tick(bc_used)))
            for r in range(2):
                mod_columns(G("mod2T", r), 1 + r)
            v.tensor_scalar(sc2p[:, :], modc[:, 32:40], 1.0, None, ALU.add).then_inc(mod2_ready, 1)
            dve.wait_ge(mod2_ready, 1)
            for q in range(4):
                emptied(dve, G("convT", q))
            moments(tok(8))
            for t in range(NT):
                link(normalised(tok(8), tok(8), t))
            tick(xn_ready)
            for q in range(4):
                emptied(dve, G("u", q))
            for q in range(4):
                g = G("mix", q)
                full(dve, g)
                empties(v.tensor_tensor(feat(5)[:, 2 * q:2 * q + 2, :],
                                        bank(g)[:, :].rearrange("p (m t) -> p m t", m=2),
                                        feat(5)[:, 2 * q:2 * q + 2, :], ALU.mult), g)
            tick(areas_free)
            for nm, i in (("w_b", 7), ("w_a", 6)):
                for q in range(4):
                    emptied(dve, G("g_b" if nm == "w_b" else "g_a", q))
                    g = G(nm, q)
                    full(dve, g)
                    for m in range(2):
                        mi = 2 * q + m
                        ins = v.scalar_tensor_tensor(feat(i)[:, mi, :], bank(g)[:, m * S:(m + 1) * S],
                                                     col("b_b" if nm == "w_b" else "b_a", mi), feat(i)[:, mi, :],
                                                     ALU.add, ALU.mult)
                        if m == 0:
                            link(ins)
                    empties(ins, g)
                    if nm == "w_a":
                        emptied(dve, g)
                        emptied(dve, G("w_b", q))
                        v.tensor_tensor(feat(6)[:, 2 * q:2 * q + 2, :], feat(6)[:, 2 * q:2 * q + 2, :],
                                        feat(7)[:, 2 * q:2 * q + 2, :], ALU.add).then_inc(m_ready, 1)
            dve.wait_ge(m_ready, 4)
            for q in range(4):
                g = G("w_out", q)
                full(dve, g)
                for m in range(2):
                    mi = 2 * q + m
                    ins = v.tensor_scalar(feat(7)[:, mi, :], bank(g)[:, m * S:(m + 1) * S], col("b_out", mi),
                                          modc[:, 16 + mi:17 + mi], ALU.add, ALU.mult)
                    if m == 0:
                        link(ins)
                empties(ins, g)

            def residual(gname, alpha):
                for hf in range(NH):
                    for t in range(NT):
                        g = G(gname, NT * hf + t)
                        full(dve, g)
                        xs = x_tok[:, t, hf * BANK:(hf + 1) * BANK]
                        empties(v.scalar_tensor_tensor(xs, xs, alpha, bank(g)[:, :], ALU.mult, ALU.add), g)
                for i in range(4):
                    emptied(dve, G(gname, i))

            residual("y_tok", ALPHA1)
            layer_norm(x_tok, lambda: tick(bc_used))
            moments(x_tok)
            for t in range(NT):
                link(normalised(tok(3), x_tok, t))
            tick(xn_ready)
            dve.wait_ge(late_in, 64)
            dve.wait_ge(consts, 2)
            for r in range(3):
                ps = slice(NE * r, NE * (r + 1))
                for hf in range(2):
                    cs = slice(hf * 1024, (hf + 1) * 1024)
                    src = bgu_raw[ps, cs]
                    for i in range(r):
                        link(v.tensor_copy(bgu_tmp[ps, 0:1024], src))
                        link(v.tensor_tensor(bgu_res[ps, cs], src, bgu_tmp[ps, 0:1024], ALU.subtract))
                        src = bgu_res[ps, cs]
                    link(v.tensor_copy(bgu_parts[ps, cs], src))
            tick(bgu_ready)
            g = G("router")
            full(dve, g)
            dve.wait_ge(rows_in, 64)
            L = R["logits"]
            for t in range(NT):
                ins = v.tensor_tensor(L[:, t, :], bank(g)[:, t * NE:(t + 1) * NE], router_bc[:, :], ALU.add)
                if t == 0:
                    link(ins)
            empties(ins, g)
            emptied(dve, g)
            for t in range(NT):
                link(v.max(top8[:, t, :], L[:, t, :]))
            for t in range(NT):
                fourth = top8[:, t, TOPK - 1:TOPK]
                link(v.tensor_scalar(R["above"][:, t, :], L[:, t, :], fourth, None, ALU.is_gt))
                link(v.tensor_scalar(R["equal"][:, t, :], L[:, t, :], fourth, None, ALU.is_equal))
                link(v.tensor_reduce(rsum[:, t:t + 1], R["above"][:, t, :], AX.X, ALU.add))
                link(v.tensor_tensor_scan(R["prefix"][:, t, :], R["equal"][:, t, :], R["equal"][:, t, :], 0.0,
                                          ALU.add, ALU.bypass))
                link(v.tensor_scalar(R["tmp2"][:, t, :], R["prefix"][:, t, :], rsum[:, t:t + 1], float(TOPK),
                                     ALU.add, ALU.is_le))
                link(v.tensor_tensor(R["tmp2"][:, t, :], R["tmp2"][:, t, :], R["equal"][:, t, :], ALU.mult))
                link(v.tensor_tensor(R["sel"][:, t, :], R["tmp2"][:, t, :], R["above"][:, t, :], ALU.add))
                link(v.tensor_scalar(R["tmp"][:, t, :], L[:, t, :], top8[:, t, 0:1], None, ALU.subtract))
            tick(route_ready)
            dve.wait_ge(moe_act, 1)
            for t in range(NT):
                link(v.tensor_tensor(R["gates"][:, t, :], R["ex"][:, t, :], R["sel"][:, t, :], ALU.mult))
                link(v.tensor_reduce(rsum[:, t:t + 1], R["gates"][:, t, :], AX.X, ALU.add))
                link(v.reciprocal(rsum[:, t:t + 1], rsum[:, t:t + 1]))
                link(v.tensor_scalar(R["gates"][:, t, :], R["gates"][:, t, :], rsum[:, t:t + 1], None, ALU.mult))
            tick(route_ready)
            g = G("pos")
            full(dve, g)
            link(v.tensor_copy(counts[:, :], bank(g)[0:1, 2 * NE:3 * NE]))
            empties(v.scalar_tensor_tensor(R["pos"], bank(g)[:, 0:2 * NE].rearrange("p (t e) -> p t e", t=NT), 1.0,
                                           R["sel"], ALU.add, ALU.mult), g)
            emptied(dve, g)
            link(v.tensor_scalar(R["pos"], R["pos"], -1.0, None, ALU.add))
            g = G("gateT")
            full(dve, g)
            empties(v.tensor_copy(gateT[:, :], bank(g)[0:NE, 0:S]), g)
            emptied(dve, g)
            tick(route_ready)
            link(v.memset(place[:, :, :], -1.0))
            link(v.memset(gate_of[:, :, :], 0.0))
            link(v.tensor_copy(place[:, :, 0:NE], R["pos"]))
            link(v.tensor_copy(gate_of[:, :, 0:NE], R["gates"]))
            link(v.memset(w6[:, :], 0.0))
            link(v.memset(w7[:, :], 0.0))

            def step(ins):
                ins.then_inc(moe_dve, 1)

            def find_slots(dst, e, b):
                row = slot_row[:, 0, 0, :] if isinstance(b, int) else \
                    slot_row[:, bass.ds(b, 1), 0, :].rearrange("p o s -> p (o s)")
                for t in range(NT):
                    step(v.tensor_scalar(dst[:, t, :], row, place[:, t, bass.ds(e, 1)], None, ALU.is_equal))

            def find_spread(dst, e, b):
                row = slot_row[:, 0, :, :] if isinstance(b, int) else \
                    slot_row[:, bass.ds(b, 1), :, :].rearrange("p o r s -> p (o r) s")
                for t in range(NT):
                    step(v.tensor_scalar(dst[:, t, :].rearrange("p (r s) -> p r s", r=2), row,
                                         place[:, t, bass.ds(e, 1)], gate_of[:, t, bass.ds(e, 1)],
                                         ALU.is_equal, ALU.mult))

            def copy_tokens(dst):
                step(v.tensor_copy(dst, banks[4][:, :].rearrange("p (d s) -> p d s", s=BLK)))

            def expert_row(e):
                step(v.tensor_copy(expert_sel[:, :], expert_hot[:, bass.ds(e, 1)].to_broadcast([96, BLK])))

            def gate_min(w):
                PE.did(dve, w, "gate")
                step(v.tensor_scalar(g_min, banks[5][:, :], LIMIT, None, ALU.min))

            def gated_and_up(w):
                AC.did(dve, w, "sigmoid")
                step(v.tensor_tensor(g_act, g_min, g_sig, ALU.mult))
                PE.did(dve, w, "up")
                step(v.tensor_scalar(u_clip, banks[6][:, :], LIMIT, -LIMIT, ALU.min, ALU.max))
                DV.did(dve, w, "up_clip")
                for i in range(2):
                    cs = slice(i * 256, (i + 1) * 256)
                    step(v.scalar_tensor_tensor(e_act[:, cs], u_clip[:, cs], 1.0, g_act[:, cs], ALU.add, ALU.mult))

            def copy_act_T(w):
                for i, bk in enumerate((banks[5], banks[6])):
                    PE.did(dve, w, f"act_T{i}")
                    step(v.tensor_copy(actT[:, 2 * i:2 * i + 2, :],
                                       bk[:, 0:256].rearrange("p (j s) -> p j s", s=P)))

            for t in range(NT):
                link(v.tensor_scalar(slots[:, t, :], slot_row[:, 0, 0, :], place[:, t, 0:1], None, ALU.is_equal))
            tick(moe_dve)
            dve.wait_ge(moe_pe, 2)
            link(v.tensor_copy(xg[:, :, :], banks[4][:, :].rearrange("p (d s) -> p d s", s=BLK)))
            link(v.tensor_copy(expert_sel[:, :], expert_hot[:, 0:1].to_broadcast([96, BLK])))
            tick(moe_dve)

            def overflow(w):
                e, b = w
                PE.started(dve, w)
                find_slots(slots_o, e, b)
                find_spread(spread_o, e, b)
                PE.did(dve, w, "gathered")
                copy_tokens(xg_o)
                gate_min(w)
                gated_and_up(w)
                copy_act_T(w)

            def last_block(w):
                e = w[0]
                gate_min(w)
                find_slots(slots, e + 1, 0)
                find_spread(spread, e, 0)
                gated_and_up(w)
                PE.did(dve, w, "next_gathered")
                copy_tokens(xg)
                expert_row(e + 1)
                copy_act_T(w)

            experts(dve, DV, overflow, last_block)

            diag = half(5, 0)
            for m in range(ND):
                link(v.tensor_scalar(diag[:, m, :], ident[:, :], modc[:, 40 + m:41 + m], None, ALU.mult))
            tick(diag_ready)
            g2_bc = a(3)[:, 0:D]
            for q in range(2):
                g = G("g2_bc", q)
                full(dve, g)
                empties(v.tensor_copy(g2_bc[:, q * BANK:(q + 1) * BANK], bank(g)[:, :]), g)
                emptied(dve, g)
            ytmp = tok(4)
            for t in range(NT):
                for hf in range(NH):
                    g = G("moe", 2 * t + hf)
                    full(dve, g)
                    cs = slice(hf * BANK, (hf + 1) * BANK)
                    empties(v.tensor_tensor(ytmp[:, t, cs], bank(g)[:, :], g2_bc[:, cs], ALU.mult), g)
                    emptied(dve, g)
                    link(v.scalar_tensor_tensor(x_tok[:, t, cs], x_tok[:, t, cs], ALPHA1, ytmp[:, t, cs],
                                                ALU.mult, ALU.add))
            layer_norm(x_tok, lambda: (tick(x_ready), tick(bc_used)))

            for q in range(4):
                emptied(dve, G("x2T", q))
            link(v.reciprocal(inv_pos[:, :], inv_pos[:, :]))
            W = PADC + S
            wide = [area[:, i * 2048:i * 2048 + ND * (W - 16)].rearrange("p (m t) -> p m t", m=ND) for i in (2, 4)]

            def win(i, m, lo, hi=W):
                return wide[i][:, m:ND, lo - 16:hi - 16]

            src = None
            pooled = feat(8)
            lo, reach = 16, 1
            for gi, w in enumerate(WINDOWS):
                m0 = 2 * gi
                i = gi % 2
                if gi == 0:
                    link(v.tensor_tensor(win(0, 0, lo), apad[:, 0:ND, lo:W], apad[:, 0:ND, lo - 1:W - 1], ALU.add))
                else:
                    step_ = w // 2
                    lo = lo + step_
                    link(v.tensor_tensor(win(i, m0, lo), win(1 - i, m0, lo), win(1 - i, m0, lo - step_, W - step_),
                                         ALU.add))
                s_w = wide[i][:, m0:m0 + 2, PADC - 16:W - 16]
                xs = apad[:, m0:m0 + 2, PADC:W]
                link(v.scalar_tensor_tensor(pooled[:, m0:m0 + 2, :], s_w, 1.0 / w, xs, ALU.mult, ALU.subtract))
                e = w - 1
                inv = inv_pos[:, 0:e].unsqueeze(1).to_broadcast([P, 2, e])
                link(v.tensor_tensor(pooled[:, m0:m0 + 2, 0:e], s_w[:, :, 0:e], inv, ALU.mult))
                link(v.tensor_tensor(pooled[:, m0:m0 + 2, 0:e], pooled[:, m0:m0 + 2, 0:e], xs[:, :, 0:e],
                                     ALU.subtract))
            tick(pooled_ready)
            tick(pool_done)
            for gi in range(4):
                g = G("pool", gi)
                full(dve, g)
                for m in range(2):
                    mi = 2 * gi + m
                    ins = v.tensor_scalar(feat(7)[:, mi, :], bank(g)[:, m * S:(m + 1) * S], col("pool_b", mi),
                                          col("pool_scale", mi), ALU.add, ALU.mult)
                    if m == 0:
                        link(ins)
                empties(ins, g)
            residual("pool_tok", ALPHA2)
            layer_norm(x_tok, lambda: (tick(x_ready), tick(bc_used)))

            def ffn(i):
                pe_part = tok(6)
                for s in range(NH):
                    for t in range(NT):
                        emptied(dve, G(f"gate_{i}", NT * s + t))
                        g = G(f"proj_{i}", NT * s + t)
                        full(dve, g)
                        cs = slice(s * BANK, (s + 1) * BANK)
                        empties(v.tensor_tensor(pe_part[:, t, cs], bank(g)[:, :], pe_part[:, t, cs], ALU.mult), g)
                for q in range(2 * DFF // BANK):
                    emptied(dve, G(f"w1_{i}", q))
                    h = area[:, 2 * 2048 + q * BANK:2 * 2048 + (q + 1) * BANK]
                    v.tensor_tensor(h, h, h, ALU.mult).then_inc(hid_ready, 1)
                for s in range(NH):
                    for t in range(NT):
                        emptied(dve, G(f"proj_{i}", NT * s + t))
                        g = G(f"w2_{i}", NT * s + t)
                        full(dve, g)
                        cs = slice(s * BANK, (s + 1) * BANK)
                        empties(v.tensor_tensor(pe_part[:, t, cs], bank(g)[:, :], pe_part[:, t, cs], ALU.add), g)
                        emptied(dve, g)
                        link(v.scalar_tensor_tensor(x_tok[:, t, cs], x_tok[:, t, cs], ALPHA2, pe_part[:, t, cs],
                                                    ALU.mult, ALU.add))
                layer_norm(x_tok, lambda: (tick(x_ready), tick(bc_used)))

            ffn(0)

            cp = apad[:, :, :].rearrange("p m t -> p (m t)")[:, 0:8 * (S + 3)]\
                .rearrange("p (c m t) -> p c m t", c=2, m=4)
            sl = [half(6, j).rearrange("p (m u) d -> p m (u d)", m=4) for j in range(2)]

            def qkv_tokens(s):
                for t in range(NT):
                    g = G(f"qkvT{s}", t)
                    full(dve, g)
                    dst = tok(2 + s // 2)[:, t, (s % 2) * BANK:(s % 2 + 1) * BANK]
                    empties(v.tensor_copy(dst, bank(g)[:, :]), g)

            for s in range(6):
                if s >= 2:
                    qkv_tokens(s - 2)
                for q in range(2):
                    emptied(dve, G(f"qkv{s}", q))
                for j in range(GTAPS):
                    for m in range(4):
                        w = col("gdn_conv", j * 3 * ND + 4 * s + m)
                        src, dst = cp[:, s % 2, m, j:j + S], sl[s % 2][:, m, :]
                        if j == 0:
                            ins = v.tensor_scalar(dst, src, w, None, ALU.mult)
                        else:
                            ins = v.scalar_tensor_tensor(dst, src, w, dst, ALU.mult, ALU.add)
                        n[0] += 1
                        ins.then_inc(dve_step, 1)
                    dve.wait_ge(dve_step, n[0])
                tick(conv4_ready)
            qkv_tokens(4)
            g = G("ba")
            full(dve, g)
            ba = bank(g)[:, 0:4 * HEADS].rearrange("p (t c) -> p t c", t=NT)
            link(v.tensor_copy(s_["b"], ba[:, :, 0:HEADS]))
            empties(v.tensor_tensor(s_["al"], ba[:, :, HEADS:2 * HEADS],
                                    dt_bc[:, :].unsqueeze(1).to_broadcast([P, NT, HEADS]), ALU.add), g)
            emptied(dve, g)
            link(v.tensor_scalar(s_["abs"], s_["al"], -1.0, None, ALU.mult))
            link(v.tensor_tensor(s_["abs"], s_["abs"], s_["al"], ALU.max))
            tick(gdn_act)
            qkv_tokens(5)
            for i in range(2):
                emptied(dve, G("qkvT5", i))
            dve.wait_ge(gdn_act, 2)
            link(v.scalar_tensor_tensor(s_["sp"], s_["al"], 0.0, s_["sp"], ALU.max, ALU.add))
            link(v.scalar_tensor_tensor(s_["gl"], s_["sp"], -1.0,
                                        s_["ea"][:, 0, :].unsqueeze(1).to_broadcast([P, NT, HEADS]),
                                        ALU.mult, ALU.mult))
            qq, kk, vv, zz = tok(2), tok(3), tok(4), tok(5)
            ev = [2]

            def by_head(x, n_):
                return x[:, n_, :].rearrange("p (h d) -> p h d", d=P)

            def spread_head(c):
                return c.unsqueeze(2).to_broadcast([P, HEADS, P])

            def masked_by(i):
                return level[:, i, :].unsqueeze(1).to_broadcast([P, HEADS, P])

            for n_ in range(NT):
                link(v.tensor_copy(H["M"], spread_head(s_["gl"][:, n_, :])))
                tick(gdn_dve)
                for x, ss, scale in ((by_head(qq, n_), s_["ssq"][:, n_, :], P ** -0.5),
                                     (by_head(kk, n_), s_["ssk"][:, n_, :], 1.0)):
                    link(v.tensor_tensor(H["T"], x, x, ALU.mult))
                    link(v.tensor_reduce(ss, H["T"], AX.X, ALU.add))
                    link(v.tensor_scalar(ss, ss, 1e-6, None, ALU.add))
                    inverse_root()
                    if scale != 1.0:
                        link(v.tensor_scalar(ss, ss, scale, None, ALU.mult))
                    link(v.tensor_tensor(x, x, spread_head(ss), ALU.mult))
                link(v.tensor_tensor(H["kb"], by_head(kk, n_), spread_head(s_["beta"][:, n_, :]), ALU.mult))
                tick(gdn_dve)
                g = G(f"g_col.{n_}")
                full(dve, g)
                link(v.tensor_copy(s_["g"][:, n_, :], bank(g)[:, 0:HEADS]))
                empties(v.tensor_tensor(s_["kd"][:, n_, :], bank(g)[:, HEADS:2 * HEADS], s_["g"][:, n_, :],
                                        ALU.subtract), g)
                emptied(dve, g)
                tick(gdn_act)
                ev[0] += 1
                dve.wait_ge(gdn_act, ev[0] + 1)
                ev[0] += 1
                for q in range(2):
                    g = G(f"g_row.{n_}", q)
                    full(dve, g)
                    link(v.tensor_copy(H["g_row"][:, 4 * q:4 * q + 4, :],
                                       bank(g)[:, :].rearrange("p (h d) -> p h d", d=P)))
                    for i in range(4):
                        h = 4 * q + i
                        ins = v.scalar_tensor_tensor(H["DT"][:, h, :], bank(g)[:, i * P:(i + 1) * P],
                                                     s_["g"][:, n_, h:h + 1], decay_mask[:, :],
                                                     ALU.subtract, ALU.add)
                        if i < 3:
                            link(ins)
                    empties(ins, g)
                    emptied(dve, g)
                tick(gdn_act)
                ev[0] += 1
                dve.wait_ge(gdn_act, ev[0] + 1)
                ev[0] += 1
                link(v.tensor_tensor(by_head(vv, n_), by_head(vv, n_), spread_head(s_["beta"][:, n_, :]), ALU.mult))
                link(v.tensor_tensor(H["kbg"], H["kb"], spread_head(s_["eg"][:, n_, :]), ALU.mult))
                for nm, dst in (("AT", H["AT"]), ("qkT", H["qkT"])):
                    for q in range(2):
                        g = G(f"{nm}.{n_}", q)
                        full(dve, g)
                        empties(v.tensor_tensor(dst[:, 4 * q:4 * q + 4, :],
                                                bank(g)[:, :].rearrange("p (h d) -> p h d", d=P),
                                                H["DT"][:, 4 * q:4 * q + 4, :], ALU.mult), g)
                        emptied(dve, g)
                link(v.tensor_tensor(by_head(kk, n_), by_head(kk, n_), spread_head(s_["kd"][:, n_, :]), ALU.mult))
                for q in range(2):
                    full(dve, G(f"qkT.{n_}", q))
                link(v.tensor_tensor(H["qdT"], H["qT"], H["g_row"], ALU.mult))
                link(v.tensor_tensor(H["M"], H["AT"], masked_by(0), ALU.mult))
                link(v.tensor_tensor(H["XT"], ident[:, :].unsqueeze(1).to_broadcast([P, HEADS, P]), H["M"],
                                     ALU.subtract))
                tick(gdn_dve)
                link(v.tensor_tensor(H["M"], H["AT"], masked_by(1), ALU.mult))
                tick(gdn_dve)
                for s in range(1, 6):
                    if s < 5:
                        for q in range(2):
                            full(dve, G(f"T{s}.{n_}", q))
                        link(v.tensor_tensor(H["M"], H["AT"], masked_by(s + 1), ALU.mult))
                        tick(gdn_dve)
                    for q in range(2):
                        todo = [(2 * q, H["X"]), (2 * q + 1, H["XT"])] if s < 5 else [(q, H["XT"])]
                        full(dve, G(f"XX{s}.{n_}", todo[-1][0]))
                        for i, dst in todo:
                            g = G(f"XX{s}.{n_}", i)
                            full(dve, g)
                            d4 = dst[:, 4 * q:4 * q + 4, :]
                            empties(v.tensor_tensor(d4, d4, bank(g)[:, :].rearrange("p (h d) -> p h d", d=P),
                                                    ALU.subtract), g)
                            emptied(dve, g)
                tick(gdn_dve)
                for c in range(2):
                    r = slice(c * KCH, (c + 1) * KCH)
                    if 2 * n_ + c > 0:
                        tick(gdn_dve)
                        for q in range(2):
                            emptied(dve, G(f"u.{n_}", q))
                            g = G(f"wS.{n_}.{c}", q)
                            full(dve, g)
                            d4 = H["u"][r, 4 * q:4 * q + 4, :]
                            empties(v.tensor_tensor(d4, d4, bank(g)[r, :].rearrange("p (h d) -> p h d", d=P),
                                                    ALU.subtract), g)
                    if 2 * n_ + c < 3:
                        for q in range(2):
                            full(dve, G(f"o.{n_}.{c}", 1))
                            g = G(f"S.{n_}.{c}", q)
                            full(dve, g)
                            if 2 * n_ + c == 0:
                                empties(v.tensor_copy(H["state"][:, 4 * q:4 * q + 4, :],
                                                      bank(g)[:, :].rearrange("p (h d) -> p h d", d=P)), g)
                            else:
                                for i in range(4):
                                    h = 4 * q + i
                                    ins = v.scalar_tensor_tensor(
                                        H["state"][:, h, :], H["state"][:, h, :],
                                        H["g_row"][:, h, (c + 1) * KCH - 1:(c + 1) * KCH],
                                        bank(g)[:, i * P:(i + 1) * P], ALU.mult, ALU.add)
                                    if i < 3:
                                        link(ins)
                                empties(ins, g)
                            emptied(dve, g)
                for c in range(2):
                    for q in range(2):
                        emptied(dve, G(f"o.{n_}.{c}", q))
                so = s_["sso"][:, n_, :]
                link(v.tensor_tensor(H["X"], H["o"], H["o"], ALU.mult))
                link(v.tensor_reduce(so, H["X"], AX.X, ALU.add))
                link(v.tensor_scalar(so, so, 1.0 / P, 1e-6, ALU.mult, ALU.add))
                inverse_root()
                link(v.tensor_tensor(H["o"], H["o"], spread_head(so), ALU.mult))
                link(v.tensor_tensor(H["o"], H["o"], normw_bc[:, :].unsqueeze(1).to_broadcast([P, HEADS, P]),
                                     ALU.mult))
                for i in range(NT * NH):
                    emptied(dve, G("z", i))
                link(v.tensor_tensor(H["o"], H["o"], by_head(zz, n_), ALU.mult))
                tick(gdn_dve)
                if n_ == 0:
                    for q in range(2):
                        full(dve, G("oT.0", q))
            residual("gdn_out", ALPHA2)
            layer_norm(x_tok, lambda: (tick(x_ready), tick(bc_used)))
            ffn(1)


def kernel(**inputs):
    import numpy as np
    import concourse.bacc as bacc
    from concourse.bass_utils import run_bass_kernel_spmd

    nc = bacc.Bacc("TRN2", target_bir_lowering=False, num_devices=1)
    arrays, A = {}, {}
    for name, value in inputs.items():
        array = np.ascontiguousarray(value)
        arrays[f"in_{name}"] = array
        A[name] = nc.dram_tensor(f"in_{name}", array.shape, mybir.dt.from_np(array.dtype), kind="ExternalInput").ap()
    out = nc.dram_tensor("out", inputs["x"].shape, F32, kind="ExternalOutput").ap()
    build(nc, A, out)
    got = run_bass_kernel_spmd(nc, [arrays], core_ids=[0])
    return got.results[0]["out"]
```

```python
from contextlib import ExitStack

import concourse.bass as bass
from concourse import mybir

F32 = mybir.dt.float32
F32R = mybir.dt.float32r
BF16 = mybir.dt.bfloat16
I32 = mybir.dt.int32
ALU = mybir.AluOpType
ACT = mybir.ActivationFunctionType
AX = mybir.AxisListType

P = 128
BANKS = 8
BANK = 512
UK = 4
RING = 10
RING2 = 4
SPLITS = 3
KCH = 64
BLK = 64

PE_MAIN = ("gate", "scattered", "up", "next_gathered", "act_T0", "act_T1", "spread_T")
PE_OVER = ("gathered", "gate", "up", "spread_T", "act_T0", "act_T1", "down", "scattered")
DVE_MAIN = ("gate_min", "next_slots0", "next_slots1", "spread0", "spread1", "gated", "up_clip", "act0", "act1",
            "next_tokens", "next_row", "act_T0", "act_T1")
DVE_OVER = ("slots0", "slots1", "spread0", "spread1", "tokens", "gate_min", "gated", "up_clip", "act0", "act1",
            "act_T0", "act_T1")
ACT_MAIN = ACT_OVER = ("sigmoid", "spread_T", "down")

def build(nc, A, out):
    S, D = A["x"].shape[1], A["x"].shape[2]
    NT = S // P
    ND = D // P
    NH = D // BANK
    TAPS = A["conv_w"].shape[1]
    PADC = TAPS - 1
    NE = A["w_router"].shape[2]
    NG = A["w_s"].shape[1]
    TOPK = 4
    EPS = 1e-5
    ALPHA1 = 2.0 ** 0.25
    ALPHA2 = 4.0 ** 0.25
    LIMIT, SWIGLU = 7.0, 1.702
    WINDOWS = (2, 4, 8, 16)
    HEADS = A["gdn_a_log_2"].shape[1]
    DFF = A["mlp_w1_2"].shape[2]
    GTAPS = A["gdn_conv_2"].shape[1]
    NBLK = S // BLK
    assert NT == 2 and D == 1024 and HEADS == ND and NG == ND and NE == 32

    ctx = ExitStack()
    with ctx:
        def sb(name, shape, dt=F32):
            return ctx.enter_context(nc.sbuf_tensor(name, shape, dt))

        def sem(name):
            return ctx.enter_context(nc.semaphore(name))

        ring_base = -(-nc.sbuf_base // 32) * 32
        ring = sb("ring", [P, RING, UK, BANK])
        ring_r = nc.alloc_sbuf_tensor_at("ring_r", [P, RING, UK, BANK], F32R, offset=ring_base)
        area_base = -(-nc.sbuf_base // 32) * 32
        area = sb("area", [P, 11 * 2048])
        area_r = nc.alloc_sbuf_tensor_at("area_r", [P, 11 * 2048], F32R, offset=area_base)
        apad = sb("apad", [P, ND, PADC + S])
        gain_bc = sb("gain_bc", [P, D])
        bias_bc = sb("bias_bc", [P, D])
        g2_bc = sb("g2_bc", [P, D])
        cols = sb("cols", [P, BANK])
        ident = sb("ident", [P, P])
        ones = sb("ones", [P, P])
        minus_half = sb("minus_half", [P, 8])
        before = sb("before", [P, P])
        upto = sb("upto", [P, P])
        chunk_ones = sb("chunk_ones", [P, P])
        decay_mask = sb("decay_mask", [P, P])
        level = sb("level", [P, 6, P])
        slot_row = sb("slot_row", [P, NBLK, 2, BLK])
        slot_int = g2_bc[:, 0:NBLK * 2 * BLK].bitcast(I32)
        inv_pos = sb("inv_pos", [P, 16])
        expert_hot = sb("expert_hot", [96, NE + 1], BF16)
        expert_sel = sb("expert_sel", [96, BLK], BF16)
        cond = sb("cond", [P, ND, 32])
        modc = sb("modc", [P, 48])
        sc1p = sb("sc1p", [P, ND])
        sc2p = sb("sc2p", [P, ND])
        stats = sb("stats", [P, NT, NH, 6])
        mv = sb("mv", [P, NT, 2])
        rstd = sb("rstd", [P, NT])
        w_router = sb("w_router_sb", [P, ND, NE])
        router_bc = sb("router_bc", [P, NE])
        rt = sb("rt", [P, 10, NT, NE])
        top8 = sb("top8", [P, NT, 8])
        rsum = sb("rsum", [P, NT])
        counts = sb("counts", [1, NE], I32)
        gateT = sb("gateT", [NE, S])
        place = sb("place", [P, NT, NE + 1])
        gate_of = sb("gate_of", [P, NT, NE + 1])
        sm = sb("sm", [P, 16, NT, HEADS])
        alog_bc = sb("alog_bc", [P, HEADS])
        dt_bc = sb("dt_bc", [P, HEADS])
        normw_bc = sb("normw_bc", [P, P])
        w_ba = rt[:, 0:2, :, :].rearrange("p i t (k n) -> p (i t k) n", n=2 * HEADS)
        banks = [ctx.enter_context(nc.psum_tensor(f"bank{i}", [P, BANK], F32)) for i in range(BANKS)]

        def a(i, w=1):
            return area[:, i * 2048:(i + w) * 2048]

        def feat(i):
            return a(i).rearrange("p (m t) -> p m t", t=S)

        def tok(i):
            return a(i).rearrange("p (t d) -> p t d", d=D)

        def half(i, j):
            return area[:, i * 2048 + j * 1024:i * 2048 + (j + 1) * 1024].rearrange("p (h d) -> p h d", d=P)

        def feat_r(i):
            return area_r[:, i * 2048:(i + 1) * 2048].rearrange("p (m t) -> p m t", t=S)

        def tok_r(i):
            return area_r[:, i * 2048:(i + 1) * 2048].rearrange("p (t d) -> p t d", d=D)

        x_tok = tok(0)
        X_HIGH, X_LOW = 1, 9
        HID = 2
        HID_HIGH = (10, 7, 8, X_HIGH)

        def unit(w, kq, c):
            return w[UK * P * kq:UK * P * (kq + 1), BANK * c:BANK * (c + 1)].rearrange("(k p) n -> p k n", p=P)

        def fours(w, cs):
            return [unit(w, kq, c) for c0 in cs for kq in range(2) for c in range(c0, c0 + 4)]

        def slabs(w, cs):
            return [unit(w, kq, c) for c in cs for kq in range(w.shape[0] // (UK * P))]

        w_mod, w_in = A["w_mod"][0], A["w_in"][0]
        gdn_in, gdn_out = A["gdn_w_in_2"][0], A["gdn_w_out_2"][0]
        C = D // BANK
        stream = []

        def add(name, units):
            stream.extend((name, u) for u in units)

        add("mod1", fours(w_mod, (0,)))
        add("a_gate", slabs(w_in, range(C, 2 * C)))
        add("a_val", slabs(w_in, range(0, C)))
        add("v", slabs(w_in, range(3 * C, 4 * C)))
        add("u", slabs(w_in, range(2 * C, 3 * C)))
        add("g_a", slabs(w_in, range(4 * C, 5 * C)))
        add("g_b", slabs(w_in, range(5 * C, 6 * C)))
        add("mod2", fours(w_mod, (4, 8)))
        add("w_b", slabs(A["w_b"][0], range(C)))
        add("w_a", slabs(A["w_a"][0], range(C)))
        add("w_out", slabs(A["w_out"][0], range(C)))
        PRE = len(stream)
        assert PRE % RING == 0
        for i in range(2):
            if i == 1:
                add("qkv", slabs(gdn_in, range(0, 3 * C)))
                add("z", slabs(gdn_in, range(3 * C, 4 * C)))
                add("gdn_out", slabs(gdn_out, range(C)))
            add(f"gate{i}", slabs(A["ple_gate_w_2"][i], range(C)))
            add(f"w1_{i}", slabs(A["mlp_w1_2"][i], range(DFF // BANK)))
            add(f"w2_{i}", [unit(A["mlp_w2_2"][i], kq, c) for kq in range(DFF // (UK * P)) for c in range(C)])
        first_unit = {}
        for n, (name, _) in enumerate(stream):
            first_unit.setdefault(name, n)
        EXPERT = [("gu", kq, c) for pair in (0, 2) for kq in range(2) for c in (pair, pair + 1)] + \
                 [("dn", kq, c) for kq in range(2) for c in range(2)]
        NU = len(EXPERT)
        extra = [a(9).rearrange("p (k n) -> p k n", n=BANK), a(10).rearrange("p (k n) -> p k n", n=BANK)]
        eslot = [ring[:, u, :, :] if u < RING else extra[u - RING] for u in range(NU)]

        LATE = {name: n - PRE for name, n in first_unit.items() if n >= PRE}

        def slot_of(n):
            return n % RING if n < PRE else (n - PRE) % RING2

        def landed_count(n):
            return 16 * (n // RING + 1) if n < PRE else 16 * (PRE // RING + NE + (n - PRE) // RING2 + 1)

        def unit_high(i):
            return ring_r[:, RING2 + 2 * (i % SPLITS), :, :]

        def unit_low(i):
            return ring_r[:, RING2 + 2 * (i % SPLITS) + 1, :, :]

        assert RING2 + 2 * SPLITS == RING

        def split_unit(eng, i, part):
            raw = ring[:, i % RING2, :, :]
            if part == "high":
                eng.wait_ge(w_full[i % RING2], landed_count(PRE + i))
                eng.wait_ge(w_used, PRE + NU * NE + max(i - SPLITS + 1, 0))
                nc.scalar.activation(unit_high(i), raw, ACT.Copy).then_inc(w_high, 1)
            else:
                eng.wait_ge(w_high, i + 1)
                nc.vector.tensor_tensor(unit_low(i), raw, unit_high(i), ALU.subtract).then_inc(w_split, 1)

        class Splitter:

            def __init__(self, eng, part):
                self.eng, self.part, self.next = eng, part, 0

            def below(self, end):
                for i in range(self.next, min(end, len(stream) - PRE)):
                    split_unit(self.eng, i, self.part)
                self.next = max(self.next, end)

        first_group, total = {}, [0]

        def group(name, n, align=None):
            while align is not None and total[0] % BANKS != align:
                total[0] += 1
            first_group[name] = total[0]
            total[0] += n

        for name, n in (("cols", 1), ("wsT", 2), ("mod1", 1), ("mod1T", 1), ("hT", 4), ("a_gate", 4), ("a_val", 4), ("v", 4),
                        ("u", 4), ("g_a", 4), ("g_b", 4), ("mod2", 2), ("mod2T", 2), ("convT", 4), ("mix", 4),
                        ("w_b", 4), ("yaT", 4), ("w_a", 4), ("w_out", 4), ("y_tok", 4), ("h2T", 4),
                        ("router", 1), ("h2_tok", 4), ("g2_bc", 2), ("pos", 1), ("gateT", 1)):
            group(name, n)
        group("moe", 4, align=0)
        group("pooled", 4)
        group("pool_tok", 4)
        for i in range(2):
            if i == 1:
                group("x4T", 4)
                for s in range(6):
                    group(f"qkv{s}", 2)
                    if s:
                        group(f"qkvT{s - 1}", 2)
                group("z", 4)
                group("ba", 1)
                group("qkvT5", 2)
                def ahead(n):
                    for name, k in (("g_col", 1), ("g_row", 2), ("kT", 2), ("qT", 2)):
                        group(f"{name}.{n}", k)

                ahead(0)
                for n in range(NT):
                    for name, k in (("kbT", 2), ("AT", 2), ("qkT", 2), ("X1", 2)):
                        group(f"{name}.{n}", k)
                    for s in range(1, 6):
                        group(f"T{s}.{n}", 2)
                        group(f"XX{s}.{n}", 4 if s < 5 else 2)
                    group(f"u.{n}", 2)
                    group(f"wT.{n}", 2)
                    for c in range(2):
                        if 2 * n + c > 0:
                            group(f"wS.{n}.{c}", 2)
                        if 2 * n + c < 3:
                            group(f"S.{n}.{c}", 2)
                        group(f"o.{n}.{c}", 2)
                    if n == 0:
                        ahead(1)
                    group(f"oT.{n}", 2)
                group("gdn_out", 4)
            group(f"xT_{i}", 4)
            group(f"pT_{i}", 1)
            group(f"gate_{i}", 4)
            group(f"proj_{i}", 4)
            group(f"w1_{i}", 2 * DFF // BANK)
            group(f"w2_{i}", 4)

        def G(name, i=0):
            return first_group[name] + i

        def bank(g):
            return banks[g % BANKS]

        used, at = {}, [0] * BANKS
        order = []
        for name, g0 in first_group.items():
            order.append((name, g0))
        names = [n for n, _ in order]
        sizes = {}
        for j, (name, g0) in enumerate(order):
            nxt = order[j + 1][1] if j + 1 < len(order) else total[0]
            sizes[name] = nxt - g0
        sizes["gateT"] = 1
        for name in names:
            for g in range(first_group[name], first_group[name] + sizes[name]):
                at[g % BANKS] += 1
                used[g] = at[g % BANKS]

        bank_full = [sem(f"bank_full{i}") for i in range(BANKS)]
        bank_free = [sem(f"bank_free{i}") for i in range(BANKS)]

        def claim(pe, g):
            if used[g] > 1:
                pe.wait_ge(bank_free[g % BANKS], used[g] - 1)

        def full(eng, g):
            eng.wait_ge(bank_full[g % BANKS], used[g])

        def emptied(eng, g):
            eng.wait_ge(bank_free[g % BANKS], used[g])

        def fills(ins, g):
            ins.then_inc(bank_full[g % BANKS], 1)

        def empties(ins, g):
            ins.then_inc(bank_free[g % BANKS], 1)

        w_full = [sem(f"w_full{u}") for u in range(NU)]
        w_used = sem("w_used")
        w_high, w_split = sem("w_high"), sem("w_split")
        x_high = sem("x_high")
        alpha_done = sem("alpha_done")
        hid_high = sem("hid_high")
        root_asked, root_given = sem("root_asked"), sem("root_given")
        x_in = sem("x_in")
        packs_in = sem("packs_in")
        ws_in = sem("ws_in")
        rows_in = sem("rows_in")
        bc_in = sem("bc_in")
        bc_used = sem("bc_used")
        late_in = sem("late_in")
        consts = sem("consts")
        pool_step = sem("pool_step")
        dve_step = sem("dve_step")
        act_step = sem("act_step")
        conv_step = sem("conv_step")
        cond_ready = sem("cond_ready")
        wsT_ready = sem("wsT_ready")
        mod1_ready = sem("mod1_ready")
        hid_ready = sem("hid_ready")
        mod2_ready = sem("mod2_ready")
        xn_ready = sem("xn_ready")
        conv_ready = sem("conv_ready")
        v_ready = sem("v_ready")
        m_ready = sem("m_ready")
        route_ready = sem("route_ready")
        bgu_ready = sem("bgu_ready")
        areas_free = sem("areas_free")
        moe_pe, moe_dve, moe_act = sem("moe_pe"), sem("moe_dve"), sem("moe_act")
        diag_ready = sem("diag_ready")
        scaled = sem("scaled")
        windows_ready = sem("windows_ready")
        x_ready = sem("x_ready")
        cpad_ready = sem("cpad_ready")
        silu_ready = sem("silu_ready")
        conv4_ready = sem("conv4_ready")
        gdn_dve = sem("gdn_dve")
        gdn_act = sem("gdn_act")
        pe_mark = sem("pe_mark")
        out_done = sem("out_done")

        COL, c0 = {}, 0
        for name, n in (("c", ND), ("b_mod", 48), ("b_in", 48), ("conv_b", ND), ("ln_a_g", ND), ("ln_a_b", ND),
                        ("b_a", ND), ("b_b", ND), ("b_out", ND),
                        ("gdn_conv", 3 * ND * GTAPS), ("conv_w", TAPS * ND)):
            COL[name] = c0
            c0 += n
        assert c0 <= BANK
        packs = area[:, 10 * 2048:10 * 2048 + 5 * P].rearrange("p (k n) -> p k n", n=P)
        PACK_ROWS = (128, 3 * ND, 96, 128, TAPS * ND - 128)
        b_s_row = area[0:1, 10 * 2048 + 1024:11 * 2048]
        ws_raw, wsT = half(9, 0), half(9, 1)
        mod_row = area[:, 8 * 2048 + 1024:9 * 2048].rearrange("p (r n) -> p r n", n=BANK)
        row8 = area[0:1, 8 * 2048:8 * 2048 + D]

        def col(name, i):
            return cols[:, COL[name] + i:COL[name] + i + 1]

        def rows(v):
            return v.rearrange("(r n) -> r n", n=P)

        window = apad[:, :, :].rearrange("p m t -> p (m t)")[:, 0:len(WINDOWS) * 3 * P]\
            .rearrange("p (g b t) -> p g b t", g=len(WINDOWS), b=3)
        pool_scale_bc, pool_b_row = a(7)[:, 0:D], a(7)[0:1, D:2 * D]

        H = {}
        for name, (i, j) in dict(qkT=(1, 0), kbg=(1, 1), kT=(6, 0), kbT=(6, 1), qT=(7, 0), DT=(7, 1), AT=(8, 0),
                                 X=(8, 1), XT=(9, 0), T=(9, 1), state=(10, 0), g_row=(10, 1)).items():
            H[name] = half(i, j)
        per_head = g2_bc[:, :].rearrange("p (h d) -> p h d", d=P)
        H["kb"], H["qdT"], H["wT"], H["M"], H["u"], H["o"] = H["qkT"], H["kT"], H["kbT"], H["kbT"], H["T"], H["DT"]

        w3, w6, w7 = a(3), a(6), a(7)
        h2_tok = tok(2)
        g2_diag = half(8, 0)
        xg = w3[:, 0:512].rearrange("p (d s) -> p d s", s=BLK)
        g_min, g_sig, g_act = w3[:, 512:1024], w3[:, 1024:1536], w3[:, 1536:2048]
        u_clip, e_act = w6[:, 0:512], w6[:, 512:1024]
        actT = w6[:, 1024:1536].rearrange("p (j s) -> p j s", s=P)
        y_blk = w6[:, 1536:2048]
        spread = w7[:, 0:256].rearrange("p (t s) -> p t s", s=P)
        spread_T = w7[:, 256:512]
        slots = w7[:, 512:640].rearrange("p (t s) -> p t s", s=BLK)
        xg_o = w7[:, 640:1152].rearrange("p (d s) -> p d s", s=BLK)
        y_blk_o = w7[:, 1152:1664]
        spread_T_o = w7[:, 1664:1920]
        slots_o = w7[:, 1920:2048].rearrange("p (t s) -> p t s", s=BLK)
        spread_o = area[:, 5 * 2048:5 * 2048 + 256].rearrange("p (t s) -> p t s", s=P)
        bgu_raw = a(5)[0:96, :]
        bgu_res = a(6)[0:96, :]
        bgu_parts = a(4)[0:96, 1024:2048].bitcast(BF16)
        bgu_tmp = a(7)[0:96, 0:1024].bitcast(BF16)
        b_dn_sb = area[0:NE, 4 * 2048:4 * 2048 + D]

        R = {n: rt[:, i, :, :] for i, n in enumerate(
            ("logits", "above", "equal", "prefix", "tmp", "sel", "ex", "gates", "pos", "tmp2"))}
        s_ = {n: sm[:, i, :, :] for i, n in enumerate(
            ("b", "al", "abs", "sp", "gl", "beta", "g", "last", "eg", "kd", "ssq", "ssk", "sso", "ea", "t0"))}

        class Steps:

            def __init__(self, sem_, main, over, base):
                self.sem, self.base, self.over_len = sem_, base, len(over)
                self.per = len(main) + (NBLK - 1) * len(over)
                self.main = {n: (NBLK - 1) * len(over) + i + 1 for i, n in enumerate(main)}
                self.over = {n: i + 1 for i, n in enumerate(over)}

            def did(self, eng, where, step):
                e, b = where
                if isinstance(b, int):
                    eng.wait_ge(self.sem, e * self.per + (self.base + self.main[step]))
                else:
                    eng.wait_ge(self.sem, e * self.per + b * self.over_len +
                                (self.base - self.over_len + self.over[step]))

            def started(self, eng, where):
                e, b = where
                if isinstance(b, int):
                    eng.wait_ge(self.sem, e * self.per + (self.base + (NBLK - 1) * self.over_len))
                else:
                    eng.wait_ge(self.sem, e * self.per + b * self.over_len + (self.base - self.over_len))

        PE = Steps(moe_pe, PE_MAIN, PE_OVER, 2)
        DV = Steps(moe_dve, DVE_MAIN, DVE_OVER, 2)
        AC = Steps(moe_act, ACT_MAIN, ACT_OVER, 1)

        def experts(eng, steps, overflow, last_block):
            with eng.Fori(0, NE) as e:
                n_tok = eng.value_load(counts[0:1, bass.ds(e, 1)], min_val=0, max_val=S)
                with eng.Fori(1, NBLK) as b:
                    with eng.If(n_tok - b * BLK > 0):
                        overflow((e, b))
                    with eng.Else():
                        steps.started(eng, (e, b))
                        eng.sem_inc(steps.sem, steps.over_len)
                last_block((e, 0))

        block = ctx.enter_context(nc.Block())

        @block.sync
        def _(sp):
            def load(n):
                s = slot_of(n)
                if n >= PRE + RING2:
                    sp.wait_ge(w_split, n - PRE - RING2 + 1)
                elif n >= PRE:
                    sp.wait_ge(w_used, PRE + NU * (NE - 1) + (n - PRE) + 1)
                elif n >= RING:
                    sp.wait_ge(w_used, n - RING + 1)
                sp.dma_start(ring[:, s, :, :], stream[n][1]).then_inc(w_full[s], 16)

            def expert_source(u, e):
                kind, kq, c = EXPERT[u]
                w = A["w_gu"] if kind == "gu" else A["w_dn"]
                w = w[0, bass.ds(e, 1), :, :] if not isinstance(e, int) else w[0, e:e + 1, :, :]
                return w[:, UK * P * kq:UK * P * (kq + 1), BANK * c:BANK * (c + 1)]\
                    .rearrange("o (k p) n -> p (o k) n", p=P)

            for n in range(PRE):
                load(n)
            for u in range(NU):
                if u < RING:
                    sp.wait_ge(w_used, PRE - RING + u + 1)
                elif u == RING:
                    sp.wait_ge(areas_free, 1)
                sp.dma_start(eslot[u], expert_source(u, 0)).then_inc(w_full[u], 16)
            with sp.Fori(1, NE) as e:
                for u in range(NU):
                    sp.wait_ge(w_used, e * NU + (PRE - NU + u + 1))
                    sp.dma_start(eslot[u], expert_source(u, e)).then_inc(w_full[u], 16)
            for n in range(PRE, len(stream)):
                load(n)
            sp.wait_ge(x_ready, 5 * NT)
            sp.dma_start(out[0].rearrange("(t p) d -> p t d", p=P), x_tok).then_inc(out_done, 16)
            sp.wait_ge(out_done, 16)

        @block.gpsimd
        def _(pool):
            n = [0]

            def link(ins):
                n[0] += 1
                ins.then_inc(pool_step, 1)
                pool.wait_ge(pool_step, n[0])

            def masked(t, pattern, base, cm, op, fill):
                link(nc.gpsimd.affine_select(out=t, in_=t, compare_op=op, fill=fill, base=base,
                                             pattern=pattern, channel_multiplier=cm))

            link(nc.gpsimd.memset(ident[:, :], 0.0))
            masked(ident[:, :], [[-1, P]], 0, 1, ALU.not_equal, 1.0)
            link(nc.gpsimd.memset(ones[:, :], 1.0))
            link(nc.gpsimd.memset(minus_half[:, :], -0.5))
            nc.gpsimd.memset(apad[:, :, 0:PADC], 0.0).then_inc(consts, 1)
            roots = [0]

            def inverse_root(t):
                roots[0] += 1
                pool.wait_ge(root_asked, roots[0])
                nc.gpsimd.tensor_tensor(t, t, minus_half[:, 0:t.shape[1]], ALU.pow).then_inc(root_given, 1)

            def norm_root():
                inverse_root(rstd[:, :])

            norm_root()
            link(nc.gpsimd.memset(before[:, :], 1.0))
            masked(before[:, :], [[1, P]], 0, -1, ALU.is_gt, 0.0)
            link(nc.gpsimd.memset(upto[:, :], 1.0))
            masked(upto[:, :], [[1, P]], 0, -1, ALU.is_ge, 0.0)
            link(nc.gpsimd.memset(upto[0:KCH, KCH:P], 0.0))
            link(nc.gpsimd.memset(chunk_ones[:, :], 0.0))
            link(nc.gpsimd.memset(chunk_ones[0:KCH, 0:KCH], 1.0))
            link(nc.gpsimd.memset(chunk_ones[KCH:P, KCH:P], 1.0))
            link(nc.gpsimd.tensor_scalar(decay_mask[:, :], upto[:, :], -1.0, 1e30, ALU.add, ALU.mult))
            link(nc.gpsimd.memset(level[:, :, :], 0.0))
            for i in range(6):
                s = 1 << i
                k = P // (2 * s)
                v = level[:, i, :].rearrange("p (k r) -> p k r", r=2 * s)[:, :, s:2 * s]
                link(nc.gpsimd.memset(v, 1.0))
                masked(v, [[-2 * s, k], [0, s]], 0, 1, ALU.is_ge, 0.0)
                masked(v, [[2 * s, k], [0, s]], s - 1, -1, ALU.is_ge, 0.0)
            link(nc.gpsimd.iota(slot_int, pattern=[[BLK, NBLK], [0, 2], [1, BLK]], base=0,
                                channel_multiplier=0))
            link(nc.gpsimd.tensor_copy(slot_row[:, :, :, :].rearrange("p b r s -> p (b r s)"), slot_int))
            link(nc.gpsimd.iota(slot_int[:, 0:16], pattern=[[1, 16]], base=1, channel_multiplier=0))
            link(nc.gpsimd.tensor_copy(inv_pos[:, :], slot_int[:, 0:16]))
            link(nc.gpsimd.memset(expert_hot[:, :], 0.0))
            for r in range(3):
                masked(expert_hot[:, 0:NE], [[-1, NE]], -NE * r, 1, ALU.not_equal, 1.0)
            nc.gpsimd.memset(top8[:, :, :], 0.0).then_inc(consts, 1)

            def bc(dst, v):
                pool.dma_start(dst, v.rearrange("(o n) -> o n", o=1).to_broadcast([P, v.shape[0]]))\
                    .then_inc(bc_in, 16)

            norms = [(A["ln_v_g"][0], A["ln_v_b"][0]), (A["post1_g"][0], A["post1_b"][0]),
                     (A["post2_g"][0], A["post2_b"][0])] + \
                    [(A["ln_gain_2"][i, j], A["ln_bias_2"][i, j]) for i in range(2) for j in range(2)]

            def load_norm(i):
                if i:
                    pool.wait_ge(bc_used, i)
                bc(gain_bc[:, :], norms[i][0])
                bc(bias_bc[:, :], norms[i][1])

            late = [0]

            def load(*pairs):
                for dst, src in pairs:
                    late[0] += 16
                    pool.dma_start(dst, src).then_inc(late_in, 16)
                pool.wait_ge(late_in, late[0])

            load_norm(0)
            norm_root()
            load_norm(1)
            norm_root()
            for e in range(4):
                emptied(pool, G("w_b", e))
            load(*[(bgu_raw[NE * r:NE * (r + 1), :], A["b_gu"][0]) for r in range(3)],
                 (b_dn_sb, A["b_dn"][0]))
            norm_root()
            load_norm(2)
            norm_root()
            pool.wait_ge(conv_ready, 1)
            pool.wait_ge(bgu_ready, 1)
            for gi, w in enumerate(WINDOWS):
                near, far = window[:, gi, 0:2, :], window[:, gi, 2, :]
                link(nc.gpsimd.memset(window[:, gi, :, :], 1.0 / w))
                masked(near, [[0, 2], [1, P]], 0, -1, ALU.is_ge, 0.0)
                masked(near, [[0, 2], [-1, P]], w - 1, 1, ALU.is_ge, 0.0)
                masked(far, [[-1, P]], w - 1 - P, 1, ALU.is_ge, 0.0)
                link(nc.gpsimd.tensor_scalar(window[:, gi, 0, 0:w], window[:, gi, 0, 0:w], float(w), None, ALU.mult))
                link(nc.gpsimd.tensor_tensor(window[:, gi, 0, 0:w], window[:, gi, 0, 0:w], inv_pos[:, 0:w], ALU.mult))
                for b in range(2):
                    link(nc.gpsimd.tensor_tensor(window[:, gi, b, :], window[:, gi, b, :], ident[:, :],
                                                 ALU.subtract))
            nc.gpsimd.sem_inc(windows_ready, 1)
            norm_root()
            for e in range(4):
                emptied(pool, G("moe", e))
            load((a(6).rearrange("p (g k d) -> p g k d", g=4, k=2),
                  A["pool_w_2"][0].rearrange("g (k p) d -> p g k d", p=P)),
                 (pool_scale_bc, A["pool_scale_2"][0:1, :].to_broadcast([P, D])),
                 (pool_b_row, A["pool_b_2"][0].rearrange("(o g) d -> o (g d)", o=1)),
                 (alog_bc[:, :], A["gdn_a_log_2"][0:1, :].to_broadcast([P, HEADS])),
                 (dt_bc[:, :], A["gdn_dt_bias_2"][0:1, :].to_broadcast([P, HEADS])),
                 (normw_bc[:, :], A["gdn_norm_w_2"][0:1, :].to_broadcast([P, P])),
                 (w_ba[:, :, :], gdn_in[:, 4 * D:4 * D + 2 * HEADS].rearrange("(k p) n -> p k n", p=P)))
            load_norm(3)
            norm_root()

            def load_ffn(i):
                pool.wait_ge(x_ready, NT * (2 + 2 * i))
                load((tok(7), A["ple_proj_2"][i].rearrange("(k p) n -> p k n", p=P)),
                     (area[:, 8 * 2048:8 * 2048 + 512].rearrange("p (t c) -> p t c", t=NT),
                      A["p_2"][i, 0].rearrange("(t p) c -> p t c", p=P)),
                     (area[0:1, 8 * 2048 + 1024:9 * 2048], A["ple_gate_b_2"][i:i + 1, :]))

            load_ffn(0)
            load_norm(4)
            cp = apad[:, :, :].rearrange("p m t -> p (m t)")[:, 0:8 * (S + 3)]\
                .rearrange("p (c m t) -> p c m t", c=2, m=4)
            nc.gpsimd.memset(cp[:, :, :, 0:3], 0.0).then_inc(cpad_ready, 1)
            norm_root()
            load_norm(5)
            for n_ in range(NT):
                inverse_root(s_["ssq"][:, n_, :])
                inverse_root(s_["ssk"][:, n_, :])
            for n_ in range(NT):
                inverse_root(s_["sso"][:, n_, :])
            norm_root()
            load_ffn(1)
            load_norm(6)
            norm_root()

        @block.tensor
        def _(pe):
            mm = nc.tensor.matmul
            owed = [False]

            def settle(ins):
                if owed[0]:
                    ins.then_inc(w_used, 1)
                    owed[0] = False

            def transposed(g, pieces):
                claim(pe, g)
                for i, (src, c) in enumerate(pieces):
                    k = src.shape[0]
                    ins = mm(bank(g)[0:src.shape[1], c:c + k], src, ident[0:k, 0:k], is_transpose=True,
                             start=True, stop=True)
                    if i == 0:
                        settle(ins)
                fills(ins, g)

            def unit_ready(n):
                pe.wait_ge(w_full[slot_of(n)], landed_count(n))
                return ring[:, slot_of(n), :, :]

            def feature_major(name, gname, xT, n_slab):
                n0 = first_unit[name]
                for s in range(n_slab):
                    u = [unit_ready(n0 + 2 * s), unit_ready(n0 + 2 * s + 1)]
                    for q in range(2):
                        g = G(gname, 2 * s + q)
                        claim(pe, g)
                        for m in range(2):
                            for k in range(ND):
                                c = (2 * q + m) * P
                                ins = mm(bank(g)[:, m * S:(m + 1) * S], u[k // UK][:, k % UK, c:c + P],
                                         xT[:, k, :], start=k == 0, stop=k == ND - 1)
                                settle(ins)
                                if q == 1 and m == 1 and k == UK - 1:
                                    ins.then_inc(w_used, 1)
                        fills(ins, g)
                    owed[0] = True

            def token_major(name, gname, lhs, n_slab, bias=None):
                n0 = first_unit[name]
                for s in range(n_slab):
                    u = [unit_ready(n0 + 2 * s), unit_ready(n0 + 2 * s + 1)]
                    for t in range(NT):
                        g = G(gname, NT * s + t)
                        claim(pe, g)
                        if bias is not None:
                            mm(bank(g)[:, :], ones[0:1, :], bias[0:1, BANK * s:BANK * (s + 1)],
                               start=True, stop=False)
                        for k in range(ND):
                            ins = mm(bank(g)[:, :], lhs(k, t), u[k // UK][:, k % UK, :],
                                     start=k == 0 and bias is None, stop=k == ND - 1)
                            settle(ins)
                            if t == NT - 1 and k == UK - 1:
                                ins.then_inc(w_used, 1)
                        fills(ins, g)
                    owed[0] = True

            def late_unit(i):
                pe.wait_ge(w_split, i + 1)
                return unit_high(i), unit_low(i)

            def three(out_, a_, b_, start, stop):
                ins = mm(out_, a_[0], b_[0], start=start, stop=False)
                settle(ins)
                mm(out_, a_[0], b_[1], start=False, stop=False)
                return mm(out_, a_[1], b_[0], start=False, stop=stop)

            def parts_of(xs, *at):
                return tuple(x[(slice(None),) + at] for x in xs)

            def feature_major_late(name, gname, xs, slab, gi):
                gs = [G(gname, gi), G(gname, gi + 1)]
                for h in range(2):
                    i = LATE[name] + 2 * slab + h
                    u = late_unit(i)
                    for q in range(2):
                        if h == 0:
                            claim(pe, gs[q])
                        for m in range(2):
                            c = (2 * q + m) * P
                            for k in range(UK):
                                ins = three(bank(gs[q])[:, m * S:(m + 1) * S],
                                            parts_of(u, k, slice(c, c + P)),
                                            parts_of(xs, UK * h + k, slice(None)),
                                            h == 0 and m == 0 and k == 0, h == 1 and m == 1 and k == UK - 1)
                        if h == 1:
                            fills(ins, gs[q])
                    if h == 0:
                        ins.then_inc(w_used, 1)
                    else:
                        owed[0] = True

            def token_major_late(name, gname, lhs, n_slab, bias=None):
                for s in range(n_slab):
                    for h in range(2):
                        u = late_unit(LATE[name] + 2 * s + h)
                        for t in range(NT):
                            g = G(gname, NT * s + t)
                            if h == 0:
                                claim(pe, g)
                                if bias is not None:
                                    mm(bank(g)[:, :], ones[0:1, :], bias[0:1, BANK * s:BANK * (s + 1)],
                                       start=True, stop=False)
                            for k in range(UK):
                                ins = three(bank(g)[:, :], lhs(UK * h + k, t),
                                            parts_of(u, k, slice(None)),
                                            h == 0 and k == 0 and bias is None, h == 1 and k == UK - 1)
                            if h == 1:
                                fills(ins, g)
                        if h == 0:
                            ins.then_inc(w_used, 1)
                    owed[0] = True

            xs = (feat_r(X_HIGH), feat_r(X_LOW))

            def x_parts(k, t):
                return parts_of(xs, k, slice(t * P, (t + 1) * P))

            def tokens_of(xT):
                return lambda k, t: xT[:, k, t * P:(t + 1) * P]

            def to_features(gname, src, ready, done):
                for t in range(NT):
                    pe.wait_ge(ready, done + t + 1)
                    for q in range(4):
                        g = G(gname, q)
                        if t == 0:
                            claim(pe, g)
                        for m in range(2):
                            ins = mm(bank(g)[:, m * S + t * P:m * S + (t + 1) * P],
                                     src[:, t, (2 * q + m) * P:(2 * q + m + 1) * P], ident[:, :],
                                     is_transpose=True, start=True, stop=True)
                            settle(ins)
                        if t == NT - 1:
                            fills(ins, g)

            def to_tokens(gname, src, wait=None):
                for hf in range(NH):
                    for t in range(NT):
                        if wait:
                            wait(hf)
                        transposed(G(gname, NT * hf + t),
                                   [(src[:, 4 * hf + m, t * P:(t + 1) * P], m * P) for m in range(4)])

            pe.wait_ge(consts, 1)
            pe.wait_ge(packs_in, 16 * 12)
            g = G("cols")
            claim(pe, g)
            c = 0
            for i, r in enumerate(PACK_ROWS):
                ins = mm(bank(g)[:, c:c + r], packs[0:r, i, :], ident[0:r, 0:r], is_transpose=True,
                         start=True, stop=True)
                c += r
            fills(ins, g)
            pe.wait_ge(ws_in, 16)
            for q in range(2):
                transposed(G("wsT", q), [(ws_raw[:, 4 * q + i, :], i * P) for i in range(4)])

            def modulation(name, rounds):
                for r in range(rounds):
                    g = G(name, r)
                    claim(pe, g)
                    for kq in range(2):
                        n0 = first_unit[name] + 8 * r + 4 * kq
                        u = [unit_ready(n0 + j) for j in range(4)]
                        for k in range(UK):
                            for j in range(4):
                                ins = mm(bank(g)[32 * j:32 * j + 32, :], cond[:, UK * kq + k, :], u[j][:, k, :],
                                         start=kq == 0 and k == 0, stop=kq == 1 and k == UK - 1)
                                settle(ins)
                                if k == UK - 1 and not (kq == 1 and j == 3):
                                    ins.then_inc(w_used, 1)
                    fills(ins, g)
                    owed[0] = True
                for r in range(rounds):
                    emptied(pe, G(name, r))
                    transposed(G(name + "T", r), [(mod_row[:, r, i * P:(i + 1) * P], i * P) for i in range(4)])

            pe.wait_ge(cond_ready, 1)
            modulation("mod1", 1)
            to_features("hT", tok(2), xn_ready, 0)
            hT = feat(1)
            for q in range(4):
                emptied(pe, G("hT", q))
            feature_major("a_gate", "a_gate", hT, C)
            feature_major("a_val", "a_val", hT, C)
            pe.wait_ge(rows_in, 64)
            token_major("v", "v", tokens_of(hT), C, bias=row8)
            feature_major("u", "u", hT, C)
            feature_major("g_a", "g_a", hT, C)
            feature_major("g_b", "g_b", hT, C)
            modulation("mod2", 2)
            pe.wait_ge(conv_ready, 1)
            to_tokens("convT", feat(3))
            pe.wait_ge(v_ready, NT)
            pe.wait_ge(wsT_ready, 1)
            vt = tok(4)
            for q in range(4):
                g = G("mix", q)
                claim(pe, g)
                for m in range(2):
                    gr = 2 * q + m
                    for t in range(NT):
                        o = bank(g)[:, m * S + t * P:m * S + (t + 1) * P]
                        mm(o, ones[0:1, :], b_s_row[0:1, gr * P:(gr + 1) * P], start=True, stop=False)
                        ins = mm(o, vt[:, t, gr * P:(gr + 1) * P], wsT[:, gr, :], start=False, stop=True)
                fills(ins, g)
            for q in range(4):
                emptied(pe, G("mix", q))
            feature_major("w_b", "w_b", feat(5), C)
            to_features("yaT", tok(8), xn_ready, NT)
            for q in range(4):
                emptied(pe, G("yaT", q))
            feature_major("w_a", "w_a", feat(2), C)
            pe.wait_ge(m_ready, 4)
            feature_major("w_out", "w_out", feat(6), C)
            to_tokens("y_tok", feat(7), wait=lambda hf: (emptied(pe, G("w_out", 2 * hf)),
                                                         emptied(pe, G("w_out", 2 * hf + 1))))
            to_features("h2T", tok(3), xn_ready, 2 * NT)
            for q in range(4):
                emptied(pe, G("h2T", q))
            h2T = feat(1)
            pe.wait_ge(rows_in, 64)
            g = G("router")
            claim(pe, g)
            for t in range(NT):
                for k in range(ND):
                    ins = mm(bank(g)[:, t * NE:(t + 1) * NE], h2T[:, k, t * P:(t + 1) * P], w_router[:, k, :],
                             start=k == 0, stop=k == ND - 1)
            fills(ins, g)
            to_tokens("h2_tok", h2T)
            pe.wait_ge(diag_ready, 1)
            for q in range(2):
                g = G("g2_bc", q)
                claim(pe, g)
                for i in range(4):
                    ins = mm(bank(g)[:, i * P:(i + 1) * P], ones[:, :], g2_diag[:, 4 * q + i, :],
                             start=True, stop=True)
                fills(ins, g)
            pe.wait_ge(route_ready, 1)
            g = G("pos")
            claim(pe, g)
            sel = R["sel"]
            mm(bank(g)[:, 0:NE], before[:, :], sel[:, 0, :], start=True, stop=True)
            mm(bank(g)[:, NE:2 * NE], before[:, :], sel[:, 1, :], start=True, stop=False)
            mm(bank(g)[:, NE:2 * NE], ones[:, :], sel[:, 0, :], start=False, stop=True)
            mm(bank(g)[0:1, 2 * NE:3 * NE], ones[:, 0:1], sel[:, 0, :], start=True, stop=False)
            ins = mm(bank(g)[0:1, 2 * NE:3 * NE], ones[:, 0:1], sel[:, 1, :], start=False, stop=True)
            fills(ins, g)
            pe.wait_ge(route_ready, 2)
            transposed(G("gateT"), [(R["gates"][:, t, :], t * P) for t in range(NT)])

            emptied(pe, G("gateT"))
            pe.wait_ge(route_ready, 3)
            pe.wait_ge(bgu_ready, 1)
            for q in range(4):
                emptied(pe, G("h2_tok", q))
            emptied(pe, G("pos"))
            for i in range(4):
                t, hf = i // NH, i % NH
                ins = mm(banks[i][:, :], gateT[:, t * P:(t + 1) * P], b_dn_sb[:, hf * BANK:(hf + 1) * BANK],
                         start=True, stop=False)
            ins.then_inc(moe_pe, 1)
            bX, bG, bU, bT = banks[4], banks[5], banks[6], banks[7]

            def step(ins):
                ins.then_inc(moe_pe, 1)

            def gather(s_):
                for d in range(ND):
                    for t in range(NT):
                        ins = mm(bX[:, d * BLK:(d + 1) * BLK], h2_tok[:, t, d * P:(d + 1) * P], s_[:, t, :],
                                 start=t == 0, stop=t == NT - 1)
                        if d == 0 and t == 0:
                            first = ins
                step(ins)
                return first

            def gate_or_up(e, bk, u0, part, x, last):
                for hf in range(2):
                    ins = mm(bk[hf * BLK:(hf + 1) * BLK, :], expert_sel[:, :],
                             bgu_parts[:, (2 * part + hf) * BANK:(2 * part + hf + 1) * BANK],
                             start=True, stop=False)
                for kt in range(ND):
                    for hf in range(2):
                        u = u0 + 2 * (kt // UK) + hf
                        if kt % UK == 0:
                            weights(e, u)
                        ins = mm(bk[hf * BLK:(hf + 1) * BLK, :], x[:, kt, :], eslot[u][:, kt % UK, :],
                                 start=False, stop=kt == ND - 1)
                        if kt == ND - 1 and hf == 1:
                            step(ins)
                        elif kt % UK == UK - 1 and last:
                            ins.then_inc(w_used, 1)

            def weights(e, u):
                pe.wait_ge(w_full[u], e * 16 + (16 * (PRE // RING if u < RING else 0) + 16))

            def activation_T(w, i, bk):
                DV.did(pe, w, f"act{i}")
                for j in range(2):
                    ins = mm(bk[:, j * P:(j + 1) * P], e_act[:, (2 * i + j) * P:(2 * i + j + 1) * P],
                             ident[:, :], is_transpose=True, start=True, stop=True)
                step(ins)

            def spread_transposed(w, src):
                DV.did(pe, w, "spread1")
                for t in range(NT):
                    ins = mm(bX[:, t * P:(t + 1) * P], src[:, t, :], ident[:, :], is_transpose=True,
                             start=True, stop=True)
                step(ins)

            def down(w, last):
                for n, kt in enumerate((0, 1, 4, 5, 2, 3, 6, 7)):
                    if n % 4 == 0:
                        DV.did(pe, w, f"act_T{n // 4}")
                    for hf in range(2):
                        u = 8 + 2 * (kt // UK) + hf
                        if kt % UK == 0:
                            weights(w[0], u)
                        j, fh = kt % UK, kt // UK
                        ins = mm(bT[hf * BLK:(hf + 1) * BLK, :], actT[:, j, fh * BLK:(fh + 1) * BLK],
                                 eslot[u][:, kt % UK, :], start=n == 0, stop=n == ND - 1)
                        if kt in (3, 7) and last:
                            ins.then_inc(w_used, 1)
                        elif n == ND - 1 and hf == 1:
                            step(ins)

            def scatter(st, y, last=False):
                for t in range(NT):
                    for hf in range(2):
                        ins = mm(banks[2 * t + hf][:, :], st[hf * BLK:(hf + 1) * BLK, t * P:(t + 1) * P],
                                 y[hf * BLK:(hf + 1) * BLK, :], start=False, stop=last)
                        if last:
                            fills(ins, G("moe", 2 * t + hf))
                        if t == 0 and hf == 0:
                            first = ins
                if not last:
                    step(ins)
                return first

            pe.wait_ge(moe_dve, 1)
            gather(slots)

            def overflow(w):
                DV.did(pe, w, "slots1")
                AC.started(pe, w)
                gather(slots_o)
                DV.did(pe, w, "tokens")
                gate_or_up(w[0], bG, 0, 0, xg_o, False)
                gate_or_up(w[0], bU, 4, 1, xg_o, False)
                spread_transposed(w, spread_o)
                activation_T(w, 0, bG)
                activation_T(w, 1, bU)
                down(w, False)
                AC.did(pe, w, "down")
                scatter(spread_T_o, y_blk_o)

            def last_block(w):
                e = w[0]
                DV.started(pe, w)
                gate_or_up(e, bG, 0, 0, xg, True)
                AC.started(pe, w)
                scatter(spread_T, y_blk).then_inc(w_used, 1)
                gate_or_up(e, bU, 4, 1, xg, True)
                DV.did(pe, w, "next_slots1")
                gather(slots).then_inc(w_used, 1)
                activation_T(w, 0, bG)
                activation_T(w, 1, bU)
                DV.did(pe, w, "next_tokens")
                spread_transposed(w, spread)
                down(w, True)

            experts(pe, PE, overflow, last_block)
            pe.wait_ge(moe_act, AC.base + NE * AC.per)
            scatter(spread_T, y_blk, last=True)

            pe.wait_ge(windows_ready, 1)
            for t in range(NT):
                pe.wait_ge(x_ready, t + 1)
                for gi in range(4):
                    g = G("pooled", gi)
                    if t == 0:
                        claim(pe, g)
                    for m in range(2):
                        o = bank(g)[:, m * S + t * P:m * S + (t + 1) * P]
                        fs = slice((2 * gi + m) * P, (2 * gi + m + 1) * P)
                        ins = mm(o, x_tok[:, t, fs], window[:, gi, t, :], start=True, stop=t == 0)
                        if t == 1:
                            ins = mm(o, x_tok[:, 0, fs], window[:, gi, 2, :], start=False, stop=True)
                    if t == NT - 1:
                        fills(ins, g)
            pe.wait_ge(scaled, 3)
            pw = a(6).rearrange("p (g k d) -> p g k d", g=4, k=2)
            pooled = feat(8)
            for hf in range(NH):
                for t in range(NT):
                    g = G("pool_tok", NT * hf + t)
                    claim(pe, g)
                    for gi in (2 * hf, 2 * hf + 1):
                        emptied(pe, G("pooled", gi))
                        o = bank(g)[:, (gi - 2 * hf) * S:(gi - 2 * hf + 1) * S]
                        mm(o, ones[0:1, :], pool_b_row[:, gi * S:(gi + 1) * S], start=True, stop=False)
                        for k in range(2):
                            ins = mm(o, pooled[:, 2 * gi + k, t * P:(t + 1) * P], pw[:, gi, k, :],
                                     start=False, stop=k == 1)
                    fills(ins, g)

            def ffn(i):
                to_features(f"xT_{i}", x_tok, x_ready, NT * (1 + 2 * i))
                pe.wait_ge(late_in, 224 + 48 * i)
                pt = area[:, 8 * 2048:8 * 2048 + 512].rearrange("p (t c) -> p t c", t=NT)
                transposed(G(f"pT_{i}"), [(pt[:, t, m * P:(m + 1) * P], m * S + t * P)
                                          for m in range(2) for t in range(NT)])
                for q in range(4):
                    emptied(pe, G(f"xT_{i}", q))
                gb = area[0:1, 8 * 2048 + 1024:9 * 2048]
                token_major_late(f"gate{i}", f"gate_{i}", x_parts, C, bias=gb)
                emptied(pe, G(f"pT_{i}"))
                pT = area[:, 8 * 2048 + 512:8 * 2048 + 1024].rearrange("p (m t) -> p m t", m=2)
                proj = tok(7)
                for s in range(NH):
                    for t in range(NT):
                        g = G(f"proj_{i}", NT * s + t)
                        claim(pe, g)
                        for k in range(2):
                            ins = mm(bank(g)[:, :], pT[:, k, t * P:(t + 1) * P],
                                     proj[:, k, s * BANK:(s + 1) * BANK], start=k == 0, stop=k == 1)
                        fills(ins, g)
                for s in range(DFF // BANK):
                    feature_major_late(f"w1_{i}", f"w1_{i}", xs, s, 2 * s)
                n0 = LATE[f"w2_{i}"]
                KQ = DFF // (UK * P)
                for j in range(4):
                    claim(pe, G(f"w2_{i}", j))
                for kq in range(KQ):
                    pe.wait_ge(hid_ready, 2 * (DFF // BANK * i + kq + 1))
                    for c in range(C):
                        u = late_unit(n0 + C * kq + c)
                        for t in range(NT):
                            g = G(f"w2_{i}", NT * c + t)
                            for k in range(UK):
                                f = UK * kq + k
                                hid = parts_of((feat_r(HID_HIGH[f // 8]), feat_r(HID + f // 8)),
                                               f % 8, slice(t * P, (t + 1) * P))
                                ins = three(bank(g)[:, :], hid, parts_of(u, k, slice(None)),
                                            kq == 0 and k == 0, kq == KQ - 1 and k == UK - 1)
                            if kq == KQ - 1:
                                fills(ins, g)
                            elif t == NT - 1:
                                ins.then_inc(w_used, 1)
                        if kq == KQ - 1:
                            owed[0] = True

            ffn(0)

            to_features("x4T", x_tok, x_ready, NT * 2)
            for q in range(4):
                emptied(pe, G("x4T", q))
            sl = [half(6, j).rearrange("p (m u) d -> p m (u d)", m=4) for j in range(2)]

            def qkv_T(s):
                pe.wait_ge(silu_ready, s + 1)
                for t in range(NT):
                    transposed(G(f"qkvT{s}", t), [(sl[s % 2][:, m, t * P:(t + 1) * P], m * P) for m in range(4)])

            for s in range(6):
                feature_major_late("qkv", f"qkv{s}", xs, s, 0)
                if s:
                    qkv_T(s - 1)
            token_major_late("z", "z", x_parts, C)
            g = G("ba")
            claim(pe, g)
            pe.wait_ge(late_in, 176)
            for t in range(NT):
                for k in range(ND):
                    for i in (X_HIGH, X_LOW):
                        ins = mm(bank(g)[:, t * 2 * HEADS:(t + 1) * 2 * HEADS],
                                 feat_r(i)[:, k, t * P:(t + 1) * P].bitcast(F32), w_ba[:, k, :],
                                 start=k == 0 and i == X_HIGH, stop=k == ND - 1 and i == X_LOW)
                        settle(ins)
            fills(ins, g)
            qkv_T(5)
            kk, qq = tok(3), tok(2)
            ev = [0]

            def dve_step_ready():
                ev[0] += 1
                pe.wait_ge(gdn_dve, ev[0])

            def heads(name, fn, qs=(0, 1), at=0, ready=None):
                for q in qs:
                    g = G(name, at + q)
                    if ready:
                        ready(q)
                    claim(pe, g)
                    for i in range(4):
                        ins = fn(bank(g), i, 4 * q + i)
                        settle(ins) if i == 0 else None
                    fills(ins, g)

            def product(l, r):
                return lambda bk, i, h: mm(bk[:, i * P:(i + 1) * P], l[:, h, :], r[:, h, :], start=True, stop=True)

            def tr(src):
                return lambda bk, i, h: mm(bk[:, i * P:(i + 1) * P], src(h), ident[:, :], is_transpose=True,
                                           start=True, stop=True)

            def both_emptied(name):
                for q in range(2):
                    emptied(pe, G(name, q))

            def rows_and_transposes(n):
                dve_step_ready()
                g = G(f"g_col.{n}")
                claim(pe, g)
                mm(bank(g)[:, 0:HEADS], upto[:, :], s_["gl"][:, n, :], start=True, stop=True)
                ins = mm(bank(g)[:, HEADS:2 * HEADS], chunk_ones[:, :], s_["gl"][:, n, :], start=True, stop=True)
                fills(ins, g)
                heads(f"g_row.{n}", lambda bk, i, h: mm(bk[:, i * P:(i + 1) * P], per_head[:, h, :], upto[:, :],
                                                        start=True, stop=True))
                heads(f"kT.{n}", tr(lambda h: kk[:, n, h * P:(h + 1) * P]))
                heads(f"qT.{n}", tr(lambda h: qq[:, n, h * P:(h + 1) * P]))

            for n in range(NT):
                if n == 0:
                    rows_and_transposes(0)
                dve_step_ready()
                heads(f"kbT.{n}", tr(lambda h: H["kb"][:, h, :]))
                both_emptied(f"kT.{n}")
                both_emptied(f"kbT.{n}")
                heads(f"AT.{n}", product(H["kT"], H["kbT"]))
                both_emptied(f"qT.{n}")
                heads(f"qkT.{n}", product(H["kT"], H["qT"]))
                dve_step_ready()
                heads(f"X1.{n}", tr(lambda h: H["XT"][:, h, :]))
                for s in range(1, 6):
                    dve_step_ready()
                    heads(f"T{s}.{n}", product(H["M"], H["X"]),
                          ready=lambda q: emptied(pe, G(f"X1.{n}", q) if s == 1 else G(f"XX{s - 1}.{n}", 2 * q)))
                    for q in range(2):
                        emptied(pe, G(f"T{s}.{n}", q))
                        if s < 5:
                            if s > 1:
                                emptied(pe, G(f"XX{s - 1}.{n}", 2 * q + 1))
                            heads(f"XX{s}.{n}", product(H["XT"], H["T"]), (q,), at=q)
                            heads(f"XX{s}.{n}", product(H["T"], H["XT"]), (q,), at=q + 1)
                        else:
                            emptied(pe, G(f"XX{s - 1}.{n}", 2 * q + 1))
                            heads(f"XX{s}.{n}", product(H["T"], H["XT"]), (q,))
                dve_step_ready()
                vb = tok(4)[:, n, :].rearrange("p (h d) -> p h d", d=P)
                kd = tok(3)[:, n, :].rearrange("p (h d) -> p h d", d=P)
                heads(f"u.{n}", product(H["XT"], vb))
                heads(f"wT.{n}", product(H["kbg"], H["XT"]))
                both_emptied(f"u.{n}")
                both_emptied(f"wT.{n}")
                for c in range(2):
                    r = slice(c * KCH, (c + 1) * KCH)
                    first = 2 * n + c == 0
                    if not first:
                        dve_step_ready()
                        heads(f"wS.{n}.{c}", lambda bk, i, h: mm(
                            bk[r, i * P:(i + 1) * P], H["wT"][:, h, r], H["state"][:, h, :], start=True, stop=True))
                        both_emptied(f"wS.{n}.{c}")

                    def o_of(bk, i, h):
                        if not first:
                            mm(bk[r, i * P:(i + 1) * P], H["qdT"][:, h, r], H["state"][:, h, :],
                               start=True, stop=False)
                        return mm(bk[r, i * P:(i + 1) * P], H["qkT"][r, h, r], H["u"][r, h, :],
                                  start=first, stop=True)

                    if 2 * n + c < 3:
                        heads(f"S.{n}.{c}", lambda bk, i, h: mm(
                            bk[:, i * P:(i + 1) * P], kd[r, h, :], H["u"][r, h, :], start=True, stop=True))
                    heads(f"o.{n}.{c}", o_of)
                if n == 0:
                    rows_and_transposes(1)
                dve_step_ready()
                heads(f"oT.{n}", tr(lambda h: H["o"][:, h, :]))
            for n in range(NT):
                both_emptied(f"oT.{n}")
            oT = (tok_r(2), tok_r(3))
            token_major_late("gdn_out", "gdn_out", lambda k, t: parts_of(oT, t, slice(k * P, (k + 1) * P)), C)
            ffn(1)

        @block.scalar
        def _(act):
            f = nc.scalar.activation
            n = [0]

            def link(ins):
                n[0] += 1
                ins.then_inc(act_step, 1)
                act.wait_ge(act_step, n[0])

            def load(dst, src, s):
                act.dma_start(dst, src).then_inc(s, 16)

            load(x_tok, A["x"][0].rearrange("(t p) d -> p t d", p=P), x_in)
            r = 0
            for v in (A["c"][0], A["b_mod"][0], A["b_in"][0], A["conv_b"][0], A["ln_a_g"][0], A["ln_a_b"][0]):
                k = v.shape[0] // P
                load(packs[r:r + k, 0, :], rows(v), packs_in)
                r += k
            r = 0
            for v in (A["b_a"][0], A["b_b"][0], A["b_out"][0]):
                load(packs[r:r + ND, 1, :], rows(v), packs_in)
                r += ND
            load(packs[0:96, 2, :], A["gdn_conv_2"][0].rearrange("j (m n) -> (j m) n", n=P), packs_in)
            cw = A["conv_w"][0].rearrange("j (m n) -> (j m) n", n=P)
            load(packs[0:P, 3, :], cw[0:P, :], packs_in)
            load(packs[0:PACK_ROWS[4], 4, :], cw[P:TAPS * ND, :], packs_in)
            load(ws_raw, A["w_s"][0].rearrange("g i j -> i g j"), ws_in)
            load(row8, A["b_in"][0:1, 3 * D:4 * D], rows_in)
            load(b_s_row, A["b_s"][0].rearrange("(o g) i -> o (g i)", o=1), rows_in)
            load(w_router[:, :, :], A["w_router"][0].rearrange("(k p) e -> p k e", p=P), rows_in)
            load(router_bc[:, :], A["b_router"][0:1, :].to_broadcast([P, NE]), rows_in)

            emptied(act, G("cols"))
            f(cond[:, :, :], cols[:, COL["c"]:COL["c"] + ND].unsqueeze(2).to_broadcast([P, ND, 32]), ACT.Silu)\
                .then_inc(cond_ready, 1)
            g = G("mod1")
            full(act, g)
            empties(f(mod_row[:, 0, :], bank(g)[:, :], ACT.Copy), g)

            def pairs(gname, fn):
                for q in range(4):
                    g = G(gname, q)
                    full(act, g)
                    for m in range(2):
                        ins = fn(2 * q + m, bank(g)[:, m * S:(m + 1) * S])
                    empties(ins, g)

            act.wait_ge(mod1_ready, 1)
            pairs("hT", lambda m, ps: f(feat(1)[:, m, :], ps, ACT.Identity, bias=modc[:, m:m + 1],
                                        scale=sc1p[:, m:m + 1]))
            pairs("a_gate", lambda m, ps: f(feat(3)[:, m, :], ps, ACT.Sigmoid, bias=col("b_in", ND + m)))
            for s in range(C):
                for t in range(NT):
                    g = G("v", NT * s + t)
                    full(act, g)
                    empties(f(tok(4)[:, t, s * BANK:(s + 1) * BANK], bank(g)[:, :], ACT.Gelu), g)
            pairs("u", lambda m, ps: f(feat(5)[:, m, :], ps, ACT.Gelu, bias=col("b_in", 2 * ND + m)))
            pairs("g_a", lambda m, ps: f(feat(6)[:, m, :], ps, ACT.Sigmoid, bias=col("b_in", 4 * ND + m)))
            pairs("g_b", lambda m, ps: f(feat(7)[:, m, :], ps, ACT.Sigmoid, bias=col("b_in", 5 * ND + m)))
            for r in range(2):
                g = G("mod2", r)
                full(act, g)
                empties(f(mod_row[:, r, :], bank(g)[:, :], ACT.Copy), g)
            for hf in range(NH):
                for t in range(NT):
                    g = G("convT", NT * hf + t)
                    full(act, g)
                    empties(f(tok(8)[:, t, hf * BANK:(hf + 1) * BANK], bank(g)[:, :], ACT.Copy), g)
            pairs("yaT", lambda m, ps: f(feat(2)[:, m, :], ps, ACT.Silu, bias=col("ln_a_b", m),
                                         scale=col("ln_a_g", m)))
            act.wait_ge(mod2_ready, 1)
            pairs("h2T", lambda m, ps: f(feat(1)[:, m, :], ps, ACT.Identity, bias=modc[:, 24 + m:25 + m],
                                         scale=sc2p[:, m:m + 1]))
            for hf in range(NH):
                for t in range(NT):
                    g = G("h2_tok", NT * hf + t)
                    full(act, g)
                    empties(f(h2_tok[:, t, hf * BANK:(hf + 1) * BANK], bank(g)[:, :], ACT.Copy), g)
            act.wait_ge(route_ready, 1)
            for t in range(NT):
                ins = f(R["ex"][:, t, :], R["tmp"][:, t, :], ACT.Exp)
            ins.then_inc(moe_act, 1)

            def act_block(w, st, y):
                DV.did(act, w, "gate_min")
                f(g_sig, g_min, ACT.Sigmoid, scale=SWIGLU).then_inc(moe_act, 1)
                PE.did(act, w, "spread_T")
                f(st, banks[4][:, 0:S], ACT.Copy).then_inc(moe_act, 1)
                if isinstance(w[1], int):
                    act.wait_ge(w_used, w[0] * NU + (PRE + NU))
                else:
                    PE.did(act, w, "down")
                f(y, banks[7][:, :], ACT.Copy).then_inc(moe_act, 1)

            act.wait_ge(route_ready, 3)
            experts(act, AC, lambda w: act_block(w, spread_T_o, y_blk_o), lambda w: act_block(w, spread_T, y_blk))

            late = Splitter(act, "high")
            late.below(2)
            for q in range(4):
                g = G("pooled", q)
                full(act, g)
                empties(f(feat(8)[:, 2 * q:2 * q + 2, :], bank(g)[:, :].rearrange("p (m t) -> p m t", m=2),
                          ACT.Copy), g)

            def copy_high(gname):
                for q in range(4):
                    g = G(gname, q)
                    full(act, g)
                    f(feat_r(X_HIGH)[:, 2 * q:2 * q + 2, :], bank(g)[:, :].rearrange("p (m t) -> p m t", m=2),
                      ACT.Copy).then_inc(x_high, 1)

            def ffn(i):
                w0 = LATE[f"gate{i}"]
                late.below(w0 + 2)
                copy_high(f"xT_{i}")
                g = G(f"pT_{i}")
                full(act, g)
                empties(f(area[:, 8 * 2048 + 512:8 * 2048 + 1024], bank(g)[:, :], ACT.Copy), g)
                for s in range(NH):
                    late.below(w0 + 2 * s + 4)
                    for t in range(NT):
                        g = G(f"gate_{i}", NT * s + t)
                        full(act, g)
                        empties(f(tok(6)[:, t, s * BANK:(s + 1) * BANK], bank(g)[:, :], ACT.Sigmoid), g)
                w0 = LATE[f"w1_{i}"]

                def square_high(q):
                    c = HID_HIGH[q // 4] * 2048 + q % 4 * BANK
                    emptied(act, G(f"w1_{i}", q))
                    f(area_r[:, c:c + BANK], area[:, HID * 2048 + q * BANK:HID * 2048 + (q + 1) * BANK],
                      ACT.Square).then_inc(hid_high, 1)

                NQ = 2 * DFF // BANK
                for q in range(NQ):
                    if q % 2 == 0:
                        late.below(w0 + q + 4)
                    g = G(f"w1_{i}", q)
                    full(act, g)
                    empties(f(area[:, HID * 2048 + q * BANK:HID * 2048 + (q + 1) * BANK], bank(g)[:, :],
                              ACT.Relu), g)
                    if q < NQ - 4:
                        square_high(q)
                late.below(w0 + NQ + 2)
                for q in range(NQ - 4, NQ):
                    square_high(q)
                late.below(w0 + 2 * NQ + 2)

            ffn(0)
            copy_high("x4T")
            cp = apad[:, :, :].rearrange("p m t -> p (m t)")[:, 0:8 * (S + 3)]\
                .rearrange("p (c m t) -> p c m t", c=2, m=4)
            sl = [half(6, j).rearrange("p (m u) d -> p m (u d)", m=4) for j in range(2)]
            act.wait_ge(cpad_ready, 1)

            def silu(s):
                act.wait_ge(conv4_ready, s + 1)
                f(sl[s % 2], sl[s % 2], ACT.Silu).then_inc(silu_ready, 1)

            w0 = LATE["qkv"]
            for s in range(6):
                late.below(w0 + 2 * s + 4)
                if s >= 2:
                    act.wait_ge(conv4_ready, s - 1)
                for q in range(2):
                    g = G(f"qkv{s}", q)
                    full(act, g)
                    empties(f(cp[:, s % 2, 2 * q:2 * q + 2, 3:3 + S],
                              bank(g)[:, :].rearrange("p (m t) -> p m t", m=2), ACT.Copy), g)
                if s:
                    silu(s - 1)
                late.below(w0 + 2 * s + 5)
            silu(5)
            for s in range(NH):
                late.below(w0 + 2 * s + 16)
                for t in range(NT):
                    g = G("z", NT * s + t)
                    full(act, g)
                    empties(f(tok(5)[:, t, s * BANK:(s + 1) * BANK], bank(g)[:, :], ACT.Silu), g)
            late.below(w0 + 19)
            act.wait_ge(gdn_act, 1)
            link(f(s_["beta"], s_["b"], ACT.Sigmoid))
            link(f(s_["abs"], s_["abs"], ACT.Exp, scale=-1.0))
            link(f(s_["ea"][:, 0, :], alog_bc[:, :], ACT.Exp))
            f(s_["sp"], s_["abs"], ACT.Ln, bias=1.0).then_inc(gdn_act, 1)
            ev = [2]

            def dve_gave():
                ev[0] += 1
                act.wait_ge(gdn_act, ev[0])

            def copy_heads(name, dst):
                for q in range(2):
                    g = G(name, q)
                    full(act, g)
                    empties(f(dst[:, 4 * q:4 * q + 4, :],
                              bank(g)[:, :].rearrange("p (h d) -> p h d", d=P), ACT.Copy), g)

            def decay_columns(n_):
                dve_gave()
                link(f(s_["eg"][:, n_, :], s_["g"][:, n_, :], ACT.Exp))
                f(s_["kd"][:, n_, :], s_["kd"][:, n_, :], ACT.Exp).then_inc(gdn_act, 1)
                ev[0] += 1

            def copies(n_):
                copy_heads(f"kT.{n_}", H["kT"])
                copy_heads(f"qT.{n_}", H["qT"])

            for n_ in range(NT):
                if n_ == 0:
                    decay_columns(0)
                dve_gave()
                link(f(H["DT"], H["DT"], ACT.Exp))
                f(H["g_row"], H["g_row"], ACT.Exp).then_inc(gdn_act, 1)
                ev[0] += 1
                if n_ == 0:
                    copies(0)
                copy_heads(f"kbT.{n_}", H["kbT"])
                copy_heads(f"X1.{n_}", H["X"])
                for s in range(1, 6):
                    copy_heads(f"T{s}.{n_}", H["T"])
                copy_heads(f"u.{n_}", H["u"])
                copy_heads(f"wT.{n_}", H["wT"])
                for c in range(2):
                    r = slice(c * KCH, (c + 1) * KCH)
                    for q in range(2):
                        g = G(f"o.{n_}.{c}", q)
                        full(act, g)
                        empties(f(H["o"][r, 4 * q:4 * q + 4, :],
                                  bank(g)[r, :].rearrange("p (h d) -> p h d", d=P), ACT.Copy), g)
                if n_ == 0:
                    copies(1)
                    decay_columns(1)
                for q in range(2):
                    g = G(f"oT.{n_}", q)
                    full(act, g)
                    f(tok_r(2)[:, n_, q * BANK:(q + 1) * BANK], bank(g)[:, :], ACT.Copy).then_inc(x_high, 1)
            late.below(w0 + 20)
            ffn(1)

        @block.vector
        def _(dve):
            v = nc.vector
            n = [0]

            def link(ins):
                n[0] += 1
                ins.then_inc(dve_step, 1)
                dve.wait_ge(dve_step, n[0])

            roots = [0]

            def inverse_root():
                roots[0] += 1
                dve.sem_inc(root_asked, 1)
                dve.wait_ge(root_given, roots[0])

            def piece_stats(src, t, hf):
                link(v.bn_stats(stats[:, t, hf, :], src[:, t, hf * BANK:(hf + 1) * BANK]))

            def moments():
                for t in range(NT):
                    n[0] += 1
                    v.bn_aggr(mv[:, t, :], stats[:, t, :, :].rearrange("p a b -> p (a b)")).then_inc(dve_step, 1)
                dve.wait_ge(dve_step, n[0])
                link(v.tensor_scalar(rstd[:, :], mv[:, :, 1], EPS, None, ALU.add))
                dve.sem_inc(root_asked, 1)

            def root_there():
                roots[0] += 1
                dve.wait_ge(root_given, roots[0])

            def all_stats(src):
                for t in range(NT):
                    for hf in range(NH):
                        piece_stats(src, t, hf)

            def normalise(dst, src, ready):
                moments()
                root_there()
                for t in range(NT):
                    v.tensor_scalar(dst[:, t, :], src[:, t, :], mv[:, t, 0:1], rstd[:, t:t + 1],
                                    ALU.subtract, ALU.mult).then_inc(ready, 1)

            norm = [0]

            def layer_norm(x, ready=None, after=lambda t: None):
                norm[0] += 1
                moments()
                dve.wait_ge(bc_in, 32 * norm[0])
                for t in range(NT):
                    n[0] += 1
                    v.scalar_tensor_tensor(x[:, t, :], x[:, t, :], mv[:, t, 0:1], gain_bc[:, :],
                                           ALU.subtract, ALU.mult).then_inc(dve_step, 1)
                dve.wait_ge(dve_step, n[0])
                root_there()
                for t in range(NT):
                    link(v.scalar_tensor_tensor(x[:, t, :], x[:, t, :], rstd[:, t:t + 1], bias_bc[:, :],
                                                ALU.mult, ALU.add))
                    if ready:
                        tick(ready)
                    after(t)
                tick(bc_used)

            def tick(s, k=1):
                dve.sem_inc(s, k)

            g = G("cols")
            full(dve, g)
            empties(v.tensor_copy(cols[:, 0:c0], bank(g)[:, 0:c0]), g)
            for q in range(2):
                g = G("wsT", q)
                full(dve, g)
                empties(v.tensor_copy(wsT[:, 4 * q:4 * q + 4, :],
                                      bank(g)[:, :].rearrange("p (h d) -> p h d", d=P)), g)
                emptied(dve, g)
            v.memset(wsT[KCH:P, :, 0:KCH], 0.0).then_inc(wsT_ready, 1)
            dve.wait_ge(x_in, 16)
            all_stats(x_tok)
            normalise(tok(2), x_tok, xn_ready)
            emptied(dve, G("cols"))
            def mod_columns(g, r):
                full(dve, g)
                c = slice(16 * r, 16 * r + 16)
                empties(v.tensor_tensor(modc[:, c].rearrange("p (j i) -> p j i", i=4),
                                        bank(g)[:, :].rearrange("p (i j r) -> p j i r", i=4, r=32)[:, :, :, 0],
                                        cols[:, COL["b_mod"]:COL["b_mod"] + 48][:, c]
                                        .rearrange("p (j i) -> p j i", i=4), ALU.add), g)
                emptied(dve, g)

            mod_columns(G("mod1T"), 0)
            v.tensor_scalar(sc1p[:, :], modc[:, 8:16], 1.0, None, ALU.add).then_inc(mod1_ready, 1)
            dve.wait_ge(consts, 1)
            for q in range(4):
                emptied(dve, G("a_gate", q))
            for q in range(4):
                g = G("a_val", q)
                full(dve, g)
                for m in range(2):
                    ins = v.scalar_tensor_tensor(apad[:, 2 * q + m, PADC:PADC + S], bank(g)[:, m * S:(m + 1) * S],
                                                 col("b_in", 2 * q + m), feat(3)[:, 2 * q + m, :], ALU.add, ALU.mult)
                    if m == 0:
                        link(ins)
                empties(ins, g)
                emptied(dve, g)
            acc = feat(3)
            for m in range(ND):
                v.tensor_scalar(acc[:, m, :], apad[:, m, 0:S], col("conv_w", m), col("conv_b", m),
                                ALU.mult, ALU.add).then_inc(conv_step, 1)
            with dve.Fori(1, TAPS) as j:
                for m in range(ND):
                    dve.wait_ge(conv_step, j * ND + (m + 1 - ND))
                    v.scalar_tensor_tensor(acc[:, m, :], apad[:, m, bass.ds(j, S)],
                                           cols[:, bass.ds(j * ND + (COL["conv_w"] + m), 1)], acc[:, m, :],
                                           ALU.mult, ALU.add).then_inc(conv_step, 1)
            dve.wait_ge(conv_step, TAPS * ND)
            tick(conv_ready)
            for q in range(4):
                emptied(dve, G("v", q))
            all_stats(tok(4))
            layer_norm(tok(4), v_ready)
            for r in range(2):
                mod_columns(G("mod2T", r), 1 + r)
            v.tensor_scalar(sc2p[:, :], modc[:, 32:40], 1.0, None, ALU.add).then_inc(mod2_ready, 1)
            dve.wait_ge(mod2_ready, 1)
            for q in range(4):
                emptied(dve, G("convT", q))
            all_stats(tok(8))
            normalise(tok(8), tok(8), xn_ready)
            for q in range(4):
                emptied(dve, G("u", q))
            for q in range(4):
                g = G("mix", q)
                full(dve, g)
                empties(v.tensor_tensor(feat(5)[:, 2 * q:2 * q + 2, :],
                                        bank(g)[:, :].rearrange("p (m t) -> p m t", m=2),
                                        feat(5)[:, 2 * q:2 * q + 2, :], ALU.mult), g)
            tick(areas_free)
            for nm, i in (("w_b", 7), ("w_a", 6)):
                for q in range(4):
                    emptied(dve, G("g_b" if nm == "w_b" else "g_a", q))
                    g = G(nm, q)
                    full(dve, g)
                    for m in range(2):
                        mi = 2 * q + m
                        ins = v.scalar_tensor_tensor(feat(i)[:, mi, :], bank(g)[:, m * S:(m + 1) * S],
                                                     col("b_b" if nm == "w_b" else "b_a", mi), feat(i)[:, mi, :],
                                                     ALU.add, ALU.mult)
                        if m == 0:
                            link(ins)
                    empties(ins, g)
                    if nm == "w_a":
                        emptied(dve, g)
                        emptied(dve, G("w_b", q))
                        v.tensor_tensor(feat(6)[:, 2 * q:2 * q + 2, :], feat(6)[:, 2 * q:2 * q + 2, :],
                                        feat(7)[:, 2 * q:2 * q + 2, :], ALU.add).then_inc(m_ready, 1)
            dve.wait_ge(m_ready, 4)
            for q in range(4):
                g = G("w_out", q)
                full(dve, g)
                for m in range(2):
                    mi = 2 * q + m
                    ins = v.tensor_scalar(feat(7)[:, mi, :], bank(g)[:, m * S:(m + 1) * S], col("b_out", mi),
                                          modc[:, 16 + mi:17 + mi], ALU.add, ALU.mult)
                    if m == 0:
                        link(ins)
                empties(ins, g)

            late = Splitter(dve, "low")
            highs = [0]

            def low_part(g, dst, high):
                highs[0] += 1
                dve.wait_ge(x_high, highs[0])
                full(dve, g)
                empties(v.tensor_tensor(dst, bank(g)[:, :].rearrange("p (m t) -> p m t", m=dst.shape[1])
                                        if len(dst.shape) == 3 else bank(g)[:, :], high, ALU.subtract), g)

            def x_low(gname):
                for q in range(4):
                    low_part(G(gname, q), feat_r(X_LOW)[:, 2 * q:2 * q + 2, :], feat_r(X_HIGH)[:, 2 * q:2 * q + 2, :])

            def residual(gname, alpha, between=lambda hf: None):
                last = None
                for hf in range(NH):
                    between(hf)
                    for t in range(NT):
                        g = G(gname, NT * hf + t)
                        full(dve, g)
                        xs = x_tok[:, t, hf * BANK:(hf + 1) * BANK]
                        empties(v.scalar_tensor_tensor(xs, xs, alpha, bank(g)[:, :], ALU.mult, ALU.add), g)
                        if last:
                            emptied(dve, last[0])
                            piece_stats(x_tok, *last[1:])
                        last = g, t, hf
                emptied(dve, last[0])
                piece_stats(x_tok, *last[1:])

            residual("y_tok", ALPHA1)
            layer_norm(x_tok, after=lambda t: [piece_stats(x_tok, t, hf) for hf in range(NH)])
            normalise(tok(3), x_tok, xn_ready)
            for m in range(ND):
                n[0] += 1
                v.tensor_scalar(g2_diag[:, m, :], ident[:, :], modc[:, 40 + m:41 + m], None, ALU.mult)\
                    .then_inc(dve_step, 1)
            dve.wait_ge(dve_step, n[0])
            tick(diag_ready)
            dve.wait_ge(late_in, 64)
            dve.wait_ge(consts, 2)
            for r in range(3):
                ps = slice(NE * r, NE * (r + 1))
                for hf in range(2):
                    cs = slice(hf * 1024, (hf + 1) * 1024)
                    src = bgu_raw[ps, cs]
                    for i in range(r):
                        link(v.tensor_copy(bgu_tmp[ps, 0:1024], src))
                        link(v.tensor_tensor(bgu_res[ps, cs], src, bgu_tmp[ps, 0:1024], ALU.subtract))
                        src = bgu_res[ps, cs]
                    link(v.tensor_copy(bgu_parts[ps, cs], src))
            link(v.reciprocal(inv_pos[:, :], inv_pos[:, :]))
            tick(bgu_ready)
            g = G("router")
            full(dve, g)
            dve.wait_ge(rows_in, 64)
            L = R["logits"]
            for t in range(NT):
                ins = v.tensor_tensor(L[:, t, :], bank(g)[:, t * NE:(t + 1) * NE], router_bc[:, :], ALU.add)
                if t == 0:
                    link(ins)
            empties(ins, g)
            emptied(dve, g)
            for t in range(NT):
                link(v.max(top8[:, t, :], L[:, t, :]))
            for t in range(NT):
                fourth = top8[:, t, TOPK - 1:TOPK]
                link(v.tensor_scalar(R["above"][:, t, :], L[:, t, :], fourth, None, ALU.is_gt))
                link(v.tensor_scalar(R["equal"][:, t, :], L[:, t, :], fourth, None, ALU.is_equal))
                link(v.tensor_reduce(rsum[:, t:t + 1], R["above"][:, t, :], AX.X, ALU.add))
                link(v.tensor_tensor_scan(R["prefix"][:, t, :], R["equal"][:, t, :], R["equal"][:, t, :], 0.0,
                                          ALU.add, ALU.bypass))
                link(v.tensor_scalar(R["tmp2"][:, t, :], R["prefix"][:, t, :], rsum[:, t:t + 1], float(TOPK),
                                     ALU.add, ALU.is_le))
                link(v.tensor_tensor(R["tmp2"][:, t, :], R["tmp2"][:, t, :], R["equal"][:, t, :], ALU.mult))
                link(v.tensor_tensor(R["sel"][:, t, :], R["tmp2"][:, t, :], R["above"][:, t, :], ALU.add))
                link(v.tensor_scalar(R["tmp"][:, t, :], L[:, t, :], top8[:, t, 0:1], None, ALU.subtract))
            tick(route_ready)
            for q in range(2):
                g = G("g2_bc", q)
                full(dve, g)
                empties(v.tensor_copy(g2_bc[:, q * BANK:(q + 1) * BANK], bank(g)[:, :]), g)
                emptied(dve, g)
            dve.wait_ge(moe_act, 1)
            for t in range(NT):
                link(v.tensor_tensor(R["gates"][:, t, :], R["ex"][:, t, :], R["sel"][:, t, :], ALU.mult))
                link(v.tensor_reduce(rsum[:, t:t + 1], R["gates"][:, t, :], AX.X, ALU.add))
                link(v.reciprocal(rsum[:, t:t + 1], rsum[:, t:t + 1]))
                link(v.tensor_scalar(R["gates"][:, t, :], R["gates"][:, t, :], rsum[:, t:t + 1], None, ALU.mult))
            tick(route_ready)
            g = G("pos")
            full(dve, g)
            link(v.tensor_copy(counts[:, :], bank(g)[0:1, 2 * NE:3 * NE]))
            empties(v.scalar_tensor_tensor(R["pos"], bank(g)[:, 0:2 * NE].rearrange("p (t e) -> p t e", t=NT), 1.0,
                                           R["sel"], ALU.add, ALU.mult), g)
            emptied(dve, g)
            link(v.tensor_scalar(R["pos"], R["pos"], -1.0, None, ALU.add))
            g = G("gateT")
            full(dve, g)
            empties(v.tensor_copy(gateT[:, :], bank(g)[0:NE, 0:S]), g)
            emptied(dve, g)
            tick(route_ready)
            link(v.memset(place[:, :, :], -1.0))
            link(v.memset(gate_of[:, :, :], 0.0))
            link(v.tensor_copy(place[:, :, 0:NE], R["pos"]))
            link(v.tensor_copy(gate_of[:, :, 0:NE], R["gates"]))
            link(v.memset(w6[:, :], 0.0))
            link(v.memset(w7[:, :], 0.0))

            def step(ins):
                ins.then_inc(moe_dve, 1)

            def find_slots(dst, e, b):
                row = slot_row[:, 0, 0, :] if isinstance(b, int) else \
                    slot_row[:, bass.ds(b, 1), 0, :].rearrange("p o s -> p (o s)")
                for t in range(NT):
                    step(v.tensor_scalar(dst[:, t, :], row, place[:, t, bass.ds(e, 1)], None, ALU.is_equal))

            def find_spread(dst, e, b):
                row = slot_row[:, 0, :, :] if isinstance(b, int) else \
                    slot_row[:, bass.ds(b, 1), :, :].rearrange("p o r s -> p (o r) s")
                for t in range(NT):
                    step(v.tensor_scalar(dst[:, t, :].rearrange("p (r s) -> p r s", r=2), row,
                                         place[:, t, bass.ds(e, 1)], gate_of[:, t, bass.ds(e, 1)],
                                         ALU.is_equal, ALU.mult))

            def copy_tokens(dst):
                step(v.tensor_copy(dst, banks[4][:, :].rearrange("p (d s) -> p d s", s=BLK)))

            def expert_row(e):
                step(v.tensor_copy(expert_sel[:, :], expert_hot[:, bass.ds(e, 1)].to_broadcast([96, BLK])))

            def gate_min(w):
                PE.did(dve, w, "gate")
                step(v.tensor_scalar(g_min, banks[5][:, :], LIMIT, None, ALU.min))

            def gated_and_up(w):
                AC.did(dve, w, "sigmoid")
                step(v.tensor_tensor(g_act, g_min, g_sig, ALU.mult))
                PE.did(dve, w, "up")
                step(v.tensor_scalar(u_clip, banks[6][:, :], LIMIT, -LIMIT, ALU.min, ALU.max))
                DV.did(dve, w, "up_clip")
                for i in range(2):
                    cs = slice(i * 256, (i + 1) * 256)
                    step(v.scalar_tensor_tensor(e_act[:, cs], u_clip[:, cs], 1.0, g_act[:, cs], ALU.add, ALU.mult))

            def copy_act_T(w):
                for i, bk in enumerate((banks[5], banks[6])):
                    PE.did(dve, w, f"act_T{i}")
                    step(v.tensor_copy(actT[:, 2 * i:2 * i + 2, :],
                                       bk[:, 0:256].rearrange("p (j s) -> p j s", s=P)))

            for t in range(NT):
                link(v.tensor_scalar(slots[:, t, :], slot_row[:, 0, 0, :], place[:, t, 0:1], None, ALU.is_equal))
            tick(moe_dve)
            dve.wait_ge(moe_pe, 2)
            link(v.tensor_copy(xg[:, :, :], banks[4][:, :].rearrange("p (d s) -> p d s", s=BLK)))
            link(v.tensor_copy(expert_sel[:, :], expert_hot[:, 0:1].to_broadcast([96, BLK])))
            tick(moe_dve)

            def overflow(w):
                e, b = w
                PE.started(dve, w)
                find_slots(slots_o, e, b)
                find_spread(spread_o, e, b)
                PE.did(dve, w, "gathered")
                copy_tokens(xg_o)
                gate_min(w)
                gated_and_up(w)
                copy_act_T(w)

            def last_block(w):
                e = w[0]
                gate_min(w)
                find_slots(slots, e + 1, 0)
                find_spread(spread, e, 0)
                gated_and_up(w)
                PE.did(dve, w, "next_gathered")
                copy_tokens(xg)
                expert_row(e + 1)
                copy_act_T(w)

            experts(dve, DV, overflow, last_block)

            ytmp = tok(4)
            for t in range(NT):
                for hf in range(NH):
                    g = G("moe", 2 * t + hf)
                    full(dve, g)
                    cs = slice(hf * BANK, (hf + 1) * BANK)
                    empties(v.tensor_tensor(ytmp[:, t, cs], bank(g)[:, :], g2_bc[:, cs], ALU.mult), g)
                    emptied(dve, g)
                    link(v.scalar_tensor_tensor(x_tok[:, t, cs], x_tok[:, t, cs], ALPHA1, ytmp[:, t, cs],
                                                ALU.mult, ALU.add))
                    piece_stats(x_tok, t, hf)
            layer_norm(x_tok, x_ready)
            dve.wait_ge(late_in, 176)
            pw = a(6).rearrange("p (g k d) -> p g k d", g=4, k=2)
            for k in range(2):
                v.tensor_tensor(pw[:, :, k, :], pw[:, :, k, :], pool_scale_bc.rearrange("p (g d) -> p g d", g=4),
                                ALU.mult).then_inc(scaled, 1)
            v.tensor_tensor(pool_b_row, pool_b_row, pool_scale_bc[0:1, :], ALU.mult).then_inc(scaled, 1)
            residual("pool_tok", ALPHA2)
            layer_norm(x_tok, x_ready)

            def ffn(i):
                w0 = LATE[f"gate{i}"]
                late.below(w0 + 1)
                x_low(f"xT_{i}")
                late.below(w0 + 6)
                pe_part = tok(6)
                for s in range(NH):
                    for t in range(NT):
                        emptied(dve, G(f"gate_{i}", NT * s + t))
                        g = G(f"proj_{i}", NT * s + t)
                        full(dve, g)
                        cs = slice(s * BANK, (s + 1) * BANK)
                        empties(v.tensor_tensor(pe_part[:, t, cs], bank(g)[:, :], pe_part[:, t, cs], ALU.mult), g)
                        emptied(dve, g)
                        v.scalar_tensor_tensor(x_tok[:, t, cs], x_tok[:, t, cs], ALPHA2, pe_part[:, t, cs],
                                               ALU.mult, ALU.add).then_inc(alpha_done, 1)
                w0 = LATE[f"w1_{i}"]
                NQ = 2 * DFF // BANK
                for q in range(NQ):
                    if q < NQ - 4 and q % 2 == 0:
                        late.below(w0 + q + 4)
                    elif q >= NQ - 4 and q % 2 == 0:
                        late.below(w0 + q + 6)
                    emptied(dve, G(f"w1_{i}", q))
                    dve.wait_ge(hid_high, NQ * i + q + 1)
                    c = slice(HID * 2048 + q * BANK, HID * 2048 + (q + 1) * BANK)
                    ch = HID_HIGH[q // 4] * 2048 + q % 4 * BANK
                    link(v.tensor_tensor(area[:, c], area[:, c], area[:, c], ALU.mult))
                    v.tensor_tensor(area_r[:, c], area[:, c], area_r[:, ch:ch + BANK], ALU.subtract)\
                        .then_inc(hid_ready, 1)
                late.below(w0 + 2 * NQ + 2)
                dve.wait_ge(alpha_done, NT * NH * (i + 1))
                residual(f"w2_{i}", 1.0)
                layer_norm(x_tok, x_ready)

            ffn(0)

            w0 = LATE["qkv"]
            x_low("x4T")
            cp = apad[:, :, :].rearrange("p m t -> p (m t)")[:, 0:8 * (S + 3)]\
                .rearrange("p (c m t) -> p c m t", c=2, m=4)
            sl = [half(6, j).rearrange("p (m u) d -> p m (u d)", m=4) for j in range(2)]

            def qkv_tokens(s):
                for t in range(NT):
                    g = G(f"qkvT{s}", t)
                    full(dve, g)
                    dst = tok(2 + s // 2)[:, t, (s % 2) * BANK:(s % 2 + 1) * BANK]
                    empties(v.tensor_copy(dst, bank(g)[:, :]), g)

            for s in range(6):
                late.below(w0 + 2 * s + 4)
                if s >= 2:
                    qkv_tokens(s - 2)
                for q in range(2):
                    emptied(dve, G(f"qkv{s}", q))
                for j in range(GTAPS):
                    for m in range(4):
                        w = col("gdn_conv", j * 3 * ND + 4 * s + m)
                        src, dst = cp[:, s % 2, m, j:j + S], sl[s % 2][:, m, :]
                        if j == 0:
                            ins = v.tensor_scalar(dst, src, w, None, ALU.mult)
                        else:
                            ins = v.scalar_tensor_tensor(dst, src, w, dst, ALU.mult, ALU.add)
                        n[0] += 1
                        ins.then_inc(dve_step, 1)
                    dve.wait_ge(dve_step, n[0])
                    if j == 1:
                        late.below(w0 + 2 * s + 5)
                tick(conv4_ready)
            qkv_tokens(4)
            late.below(w0 + 16)
            qq, kk, vv, zz = tok(2), tok(3), tok(4), tok(5)

            def by_head(x, n_):
                return x[:, n_, :].rearrange("p (h d) -> p h d", d=P)

            def spread_head(c):
                return c.unsqueeze(2).to_broadcast([P, HEADS, P])

            def squares(x, ss, n_):
                x, ss = by_head(x, n_), s_[ss][:, n_, :]
                link(v.tensor_tensor(per_head, x, x, ALU.mult))
                link(v.tensor_reduce(ss, per_head, AX.X, ALU.add))
                link(v.tensor_scalar(ss, ss, 1e-6, None, ALU.add))
                dve.sem_inc(root_asked, 1)

            def unit_length(x, ss, n_, scale):
                x, ss = by_head(x, n_), s_[ss][:, n_, :]
                root_there()
                if scale != 1.0:
                    link(v.tensor_scalar(ss, ss, scale, None, ALU.mult))
                link(v.tensor_tensor(x, x, spread_head(ss), ALU.mult))

            squares(qq, "ssq", 0)
            squares(kk, "ssk", 0)
            unit_length(qq, "ssq", 0, P ** -0.5)
            unit_length(kk, "ssk", 0, 1.0)
            g = G("ba")
            full(dve, g)
            ba = bank(g)[:, 0:4 * HEADS].rearrange("p (t c) -> p t c", t=NT)
            link(v.tensor_copy(s_["b"], ba[:, :, 0:HEADS]))
            empties(v.tensor_tensor(s_["al"], ba[:, :, HEADS:2 * HEADS],
                                    dt_bc[:, :].unsqueeze(1).to_broadcast([P, NT, HEADS]), ALU.add), g)
            emptied(dve, g)
            link(v.tensor_scalar(s_["abs"], s_["al"], -1.0, None, ALU.mult))
            link(v.tensor_tensor(s_["abs"], s_["abs"], s_["al"], ALU.max))
            tick(gdn_act)
            qkv_tokens(5)
            for i in range(2):
                emptied(dve, G("qkvT5", i))
            dve.wait_ge(gdn_act, 2)
            link(v.scalar_tensor_tensor(s_["sp"], s_["al"], 0.0, s_["sp"], ALU.max, ALU.add))
            link(v.scalar_tensor_tensor(s_["gl"], s_["sp"], -1.0,
                                        s_["ea"][:, 0, :].unsqueeze(1).to_broadcast([P, NT, HEADS]),
                                        ALU.mult, ALU.mult))
            ev = [2]

            def z_weighed(n_):
                z = by_head(zz, n_)
                link(v.tensor_tensor(z, z, normw_bc[:, :].unsqueeze(1).to_broadcast([P, HEADS, P]), ALU.mult))

            def decay_columns(n_):
                g = G(f"g_col.{n_}")
                full(dve, g)
                link(v.tensor_copy(s_["g"][:, n_, :], bank(g)[:, 0:HEADS]))
                empties(v.tensor_tensor(s_["kd"][:, n_, :], bank(g)[:, HEADS:2 * HEADS], s_["g"][:, n_, :],
                                        ALU.subtract), g)
                emptied(dve, g)
                tick(gdn_act)
                ev[0] += 1

            def masked_by(i):
                return level[:, i, :].unsqueeze(1).to_broadcast([P, HEADS, P])

            for n_ in range(NT):
                if n_ == 0:
                    link(v.tensor_copy(per_head, spread_head(s_["gl"][:, 0, :])))
                    tick(gdn_dve)
                link(v.tensor_tensor(H["kb"], by_head(kk, n_), spread_head(s_["beta"][:, n_, :]), ALU.mult))
                tick(gdn_dve)
                if n_ == 0:
                    decay_columns(0)
                dve.wait_ge(gdn_act, ev[0] + 1)
                ev[0] += 1
                for q in range(2):
                    g = G(f"g_row.{n_}", q)
                    full(dve, g)
                    link(v.tensor_copy(H["g_row"][:, 4 * q:4 * q + 4, :],
                                       bank(g)[:, :].rearrange("p (h d) -> p h d", d=P)))
                    for i in range(4):
                        h = 4 * q + i
                        ins = v.scalar_tensor_tensor(H["DT"][:, h, :], bank(g)[:, i * P:(i + 1) * P],
                                                     s_["g"][:, n_, h:h + 1], decay_mask[:, :],
                                                     ALU.subtract, ALU.add)
                        if i < 3:
                            n[0] += 1
                            ins.then_inc(dve_step, 1)
                    dve.wait_ge(dve_step, n[0])
                    empties(ins, g)
                    emptied(dve, g)
                tick(gdn_act)
                ev[0] += 1
                dve.wait_ge(gdn_act, ev[0] + 1)
                ev[0] += 1
                link(v.tensor_tensor(by_head(vv, n_), by_head(vv, n_), spread_head(s_["beta"][:, n_, :]), ALU.mult))
                link(v.tensor_tensor(H["kbg"], H["kb"], spread_head(s_["eg"][:, n_, :]), ALU.mult))
                for nm, dst in (("AT", H["AT"]), ("qkT", H["qkT"])):
                    for q in range(2):
                        g = G(f"{nm}.{n_}", q)
                        full(dve, g)
                        empties(v.tensor_tensor(dst[:, 4 * q:4 * q + 4, :],
                                                bank(g)[:, :].rearrange("p (h d) -> p h d", d=P),
                                                H["DT"][:, 4 * q:4 * q + 4, :], ALU.mult), g)
                        emptied(dve, g)
                link(v.tensor_tensor(by_head(kk, n_), by_head(kk, n_), spread_head(s_["kd"][:, n_, :]), ALU.mult))
                for q in range(2):
                    full(dve, G(f"qkT.{n_}", q))
                link(v.tensor_tensor(H["qdT"], H["qT"], H["g_row"], ALU.mult))
                link(v.tensor_tensor(H["M"], H["AT"], masked_by(0), ALU.mult))
                link(v.tensor_tensor(H["XT"], ident[:, :].unsqueeze(1).to_broadcast([P, HEADS, P]), H["M"],
                                     ALU.subtract))
                tick(gdn_dve)
                link(v.tensor_tensor(H["M"], H["AT"], masked_by(1), ALU.mult))
                tick(gdn_dve)
                for s in range(1, 6):
                    if s < 5:
                        for q in range(2):
                            full(dve, G(f"T{s}.{n_}", q))
                        link(v.tensor_tensor(H["M"], H["AT"], masked_by(s + 1), ALU.mult))
                        tick(gdn_dve)
                        if n_ == 0:
                            if s == 1:
                                squares(qq, "ssq", 1)
                            if s == 2:
                                unit_length(qq, "ssq", 1, P ** -0.5)
                            if s == 3:
                                squares(kk, "ssk", 1)
                            if s == 4:
                                unit_length(kk, "ssk", 1, 1.0)
                        if n_ == 1 and s < 4:
                            late.below(w0 + 16 + s)
                    for q in range(2):
                        todo = [(2 * q, H["X"]), (2 * q + 1, H["XT"])] if s < 5 else [(q, H["XT"])]
                        full(dve, G(f"XX{s}.{n_}", todo[-1][0]))
                        for i, dst in todo:
                            g = G(f"XX{s}.{n_}", i)
                            full(dve, g)
                            d4 = dst[:, 4 * q:4 * q + 4, :]
                            empties(v.tensor_tensor(d4, d4, bank(g)[:, :].rearrange("p (h d) -> p h d", d=P),
                                                    ALU.subtract), g)
                            emptied(dve, g)
                tick(gdn_dve)
                for i in range(NT * NH):
                    emptied(dve, G("z", i))
                z_weighed(n_)
                for c in range(2):
                    r = slice(c * KCH, (c + 1) * KCH)
                    if 2 * n_ + c > 0:
                        tick(gdn_dve)
                        for q in range(2):
                            emptied(dve, G(f"u.{n_}", q))
                            g = G(f"wS.{n_}.{c}", q)
                            full(dve, g)
                            d4 = H["u"][r, 4 * q:4 * q + 4, :]
                            empties(v.tensor_tensor(d4, d4, bank(g)[r, :].rearrange("p (h d) -> p h d", d=P),
                                                    ALU.subtract), g)
                    if 2 * n_ + c < 3:
                        for q in range(2):
                            full(dve, G(f"o.{n_}.{c}", 1))
                            g = G(f"S.{n_}.{c}", q)
                            full(dve, g)
                            if 2 * n_ + c == 0:
                                empties(v.tensor_copy(H["state"][:, 4 * q:4 * q + 4, :],
                                                      bank(g)[:, :].rearrange("p (h d) -> p h d", d=P)), g)
                            else:
                                for i in range(4):
                                    h = 4 * q + i
                                    ins = v.scalar_tensor_tensor(
                                        H["state"][:, h, :], H["state"][:, h, :],
                                        H["g_row"][:, h, (c + 1) * KCH - 1:(c + 1) * KCH],
                                        bank(g)[:, i * P:(i + 1) * P], ALU.mult, ALU.add)
                                    if i < 3:
                                        n[0] += 1
                                        ins.then_inc(dve_step, 1)
                                dve.wait_ge(dve_step, n[0])
                                empties(ins, g)
                            emptied(dve, g)
                for c in range(2):
                    for q in range(2):
                        emptied(dve, G(f"o.{n_}.{c}", q))
                if n_ == 0:
                    link(v.tensor_copy(per_head, spread_head(s_["gl"][:, 1, :])))
                    tick(gdn_dve)
                so = s_["sso"][:, n_, :]
                link(v.tensor_tensor(H["X"], H["o"], H["o"], ALU.mult))
                link(v.tensor_reduce(so, H["X"], AX.X, ALU.add))
                link(v.tensor_scalar(so, so, 1.0 / P, 1e-6, ALU.mult, ALU.add))
                inverse_root()
                link(v.tensor_tensor(H["o"], H["o"], spread_head(so), ALU.mult))
                link(v.tensor_tensor(H["o"], H["o"], by_head(zz, n_), ALU.mult))
                tick(gdn_dve)
                if n_ == 0:
                    decay_columns(1)
                for q in range(2):
                    cs = slice(q * BANK, (q + 1) * BANK)
                    low_part(G(f"oT.{n_}", q), tok_r(3)[:, n_, cs], tok_r(2)[:, n_, cs])
            residual("gdn_out", ALPHA2, between=lambda hf: late.below(w0 + 20 + 2 * hf))
            layer_norm(x_tok, x_ready)
            ffn(1)


def kernel(**inputs):
    import numpy as np
    import concourse.bacc as bacc
    from concourse.bass_utils import run_bass_kernel_spmd

    nc = bacc.Bacc("TRN2", target_bir_lowering=False, num_devices=1)
    arrays, A = {}, {}
    for name, value in inputs.items():
        array = np.ascontiguousarray(value)
        arrays[f"in_{name}"] = array
        A[name] = nc.dram_tensor(f"in_{name}", array.shape, mybir.dt.from_np(array.dtype), kind="ExternalInput").ap()
    out = nc.dram_tensor("out", inputs["x"].shape, F32, kind="ExternalOutput").ap()
    build(nc, A, out)
    got = run_bass_kernel_spmd(nc, [arrays], core_ids=[0])
    return got.results[0]["out"]
```
